# Optimizing a Trainium2 kernel written in Bass

```python
import jax, jax.numpy as jnp
from jax import lax
import numpy as np
import jax
import jax.numpy as jnp

D_MODEL = 1024
BATCH = 1
SEQ = 256
DEPTH = 2

GRID_W = 64
CTX_LEN = 256
HEAD_DIM = 64
N_Q_HEADS = 8
N_KV_HEADS = 2
GQA_GROUP = N_Q_HEADS // N_KV_HEADS
ATTN_WIDTH = N_Q_HEADS * HEAD_DIM
KV_WIDTH = N_KV_HEADS * HEAD_DIM
CONV_GROUPS = 4
CONV_WIDTH = CONV_GROUPS * 64
CONV_K = 3
FOURIER_GROUPS = 4
FOURIER_GROUP_DIM = 64
FOURIER_WIDTH = FOURIER_GROUPS * FOURIER_GROUP_DIM
N_BRANCHES = 3
D_FF = 4 * D_MODEL
Q_BLOCK = 128
ROPE_THETA = 10000.0
ROPE_HALF = HEAD_DIM // 2
EPS = 1e-6
N_MOD = 6

OFF_B = 0
OFF_C = OFF_B + CONV_WIDTH
OFF_X = OFF_C + CONV_WIDTH
OFF_F = OFF_X + CONV_WIDTH
OFF_Q = OFF_F + FOURIER_WIDTH
OFF_K = OFF_Q + ATTN_WIDTH
OFF_V = OFF_K + KV_WIDTH
OFF_G = OFF_V + KV_WIDTH
IN_WIDTH = OFF_G + N_BRANCHES * D_MODEL


def rms_norm(x, g):
    xf = x.astype(jnp.float32)
    y = xf * lax.rsqrt(jnp.mean(xf * xf, axis=-1, keepdims=True) + EPS)
    return (y * g.astype(jnp.float32)).astype(x.dtype)

def modulate(x, g, shift, scale):
    return rms_norm(x, g) * (1 + scale) + shift

def axial_rope_tables(rows):
    n_freq = ROPE_HALF // 2
    inv = ROPE_THETA ** (-jnp.arange(n_freq, dtype=jnp.float32) / n_freq)
    row_ang = jnp.repeat(jnp.arange(rows, dtype=jnp.float32)[:, None] * inv, GRID_W, axis=0)
    col_ang = jnp.tile(jnp.arange(GRID_W, dtype=jnp.float32)[:, None] * inv, (rows, 1))
    ang = jnp.concatenate([row_ang, col_ang], axis=-1)
    return jnp.cos(ang), jnp.sin(ang)

def apply_rope(x, cos, sin):
    xf = x.astype(jnp.float32)
    x1, x2 = xf[..., :ROPE_HALF], xf[..., ROPE_HALF:]
    c = cos[None, :, None, :]
    s = sin[None, :, None, :]
    return jnp.concatenate([x1 * c - x2 * s, x1 * s + x2 * c], axis=-1).astype(x.dtype)

def short_conv(u, w):
    L = u.shape[1]
    pad = CONV_K // 2
    up = jnp.pad(u, ((0, 0), (pad, pad), (0, 0)))
    return sum(up[:, j:j + L] * w[j] for j in range(CONV_K))

def fourier_mix(u):
    b, L, _ = u.shape
    ug = u.astype(jnp.float32).reshape(b, L, FOURIER_GROUPS, FOURIER_GROUP_DIM)
    y = jnp.fft.fft2(ug, axes=(1, 3), norm="ortho").real
    return y.reshape(b, L, FOURIER_WIDTH).astype(u.dtype)

def local_branches(z, w_conv):
    y_conv = z[..., OFF_B:OFF_C] * short_conv(z[..., OFF_C:OFF_X] * z[..., OFF_X:OFF_F], w_conv)
    y_four = fourier_mix(z[..., OFF_F:OFF_Q])
    return y_conv, y_four

def qkv_heads(z, g_q, g_k):
    b, L, _ = z.shape
    q = rms_norm(z[..., OFF_Q:OFF_K].reshape(b, L, N_Q_HEADS, HEAD_DIM), g_q)
    k = rms_norm(z[..., OFF_K:OFF_V].reshape(b, L, N_KV_HEADS, HEAD_DIM), g_k)
    v = z[..., OFF_V:OFF_G].reshape(b, L, N_KV_HEADS, HEAD_DIM)
    return q, k, v

def gqa(q, k, v):
    b, lq = q.shape[:2]
    qg = q.reshape(b, lq, N_KV_HEADS, GQA_GROUP, HEAD_DIM)
    s = jnp.einsum('bqgrd,bkgd->bgrqk', qg, k).astype(jnp.float32) * (HEAD_DIM ** -0.5)
    p = jax.nn.softmax(s, axis=-1).astype(v.dtype)
    o = jnp.einsum('bgrqk,bkgd->bqgrd', p, v)
    return o.reshape(b, lq, ATTN_WIDTH)

def blocked_gqa(q, k, v):
    b, lq = q.shape[:2]
    nb = lq // Q_BLOCK
    qb = q.reshape(b, nb, Q_BLOCK, N_Q_HEADS, HEAD_DIM).transpose(1, 0, 2, 3, 4)
    ob = lax.map(lambda qi: gqa(qi, k, v), qb)
    return ob.transpose(1, 0, 2, 3).reshape(b, lq, ATTN_WIDTH)

def merge_branches(z, y_conv, y_four, y_attn, w_conv_out, w_four_out, w_attn_out, w_o):
    gates = jax.nn.sigmoid(z[..., OFF_G:].astype(jnp.float32)).astype(z.dtype)
    g_conv, g_four, g_attn = jnp.split(gates, N_BRANCHES, axis=-1)
    m = g_conv * (y_conv @ w_conv_out) + g_four * (y_four @ w_four_out) + g_attn * (y_attn @ w_attn_out)
    return m @ w_o

def sq_relu_mlp(h, w1, w2):
    return jnp.square(jax.nn.relu(h @ w1)) @ w2

def first_inputs(seed: int = 0) -> dict:
    key = jax.random.key(seed)
    ks = jax.random.split(key, 20)
    f32 = jnp.float32
    nrm = lambda k, shape, s: jax.random.normal(k, shape, f32) * s
    return {
        "x": nrm(ks[0], (BATCH, SEQ, D_MODEL), 1.0),
        "c": nrm(ks[1], (BATCH, D_MODEL), 1.0),
        "ctx": nrm(ks[2], (BATCH, CTX_LEN, D_MODEL), 1.0),
        "c_ctx": nrm(ks[3], (D_MODEL,), 1.0),
        "w_mod": nrm(ks[4], (DEPTH, D_MODEL, N_MOD * D_MODEL), 0.5 * D_MODEL ** -0.5),
        "b_mod": nrm(ks[5], (DEPTH, N_MOD * D_MODEL), 0.01),
        "g_norm1": 1.0 + nrm(ks[6], (DEPTH, D_MODEL), 0.05),
        "g_norm2": 1.0 + nrm(ks[7], (DEPTH, D_MODEL), 0.05),
        "w_in": nrm(ks[8], (DEPTH, D_MODEL, IN_WIDTH), D_MODEL ** -0.5),
        "w_conv": nrm(ks[9], (DEPTH, CONV_K, CONV_WIDTH), CONV_K ** -0.5),
        "g_q": 1.0 + nrm(ks[10], (DEPTH, HEAD_DIM), 0.05),
        "g_k": 1.0 + nrm(ks[11], (DEPTH, HEAD_DIM), 0.05),
        "w_conv_out": nrm(ks[12], (DEPTH, CONV_WIDTH, D_MODEL), CONV_WIDTH ** -0.5),
        "w_four_out": nrm(ks[13], (DEPTH, FOURIER_WIDTH, D_MODEL), FOURIER_WIDTH ** -0.5),
        "w_attn_out": nrm(ks[14], (DEPTH, ATTN_WIDTH, D_MODEL), ATTN_WIDTH ** -0.5),
        "w_o": nrm(ks[15], (DEPTH, D_MODEL, D_MODEL), D_MODEL ** -0.5),
        "w_ff1": nrm(ks[16], (DEPTH, D_MODEL, D_FF), D_MODEL ** -0.5),
        "w_ff2": nrm(ks[17], (DEPTH, D_FF, D_MODEL), D_FF ** -0.5),
    }

def first_block(x, c, ctx, c_ctx, w_mod, b_mod, g_norm1, g_norm2, w_in, w_conv, g_q, g_k,
              w_conv_out, w_four_out, w_attn_out, w_o, w_ff1, w_ff2):
    S = x.shape[1]
    ROWS = S // GRID_W
    cos, sin = axial_rope_tables(ROWS)
    ctx_s = ctx
    for l in range(DEPTH):
        mod = (jax.nn.silu(c) @ w_mod[l] + b_mod[l])[:, None, :]
        mod_c = (jax.nn.silu(c_ctx)[None] @ w_mod[l] + b_mod[l])[:, None, :]
        sh1, sc1, gt1, sh2, sc2, gt2 = jnp.split(mod, N_MOD, axis=-1)
        csh1, csc1, cgt1, csh2, csc2, cgt2 = jnp.split(mod_c, N_MOD, axis=-1)

        hc = modulate(ctx_s, g_norm1[l], csh1, csc1)
        zc = hc @ w_in[l]
        qc, kc, vc = qkv_heads(zc, g_q[l], g_k[l])

        h = modulate(x, g_norm1[l], sh1, sc1)
        z = h @ w_in[l]
        q, k, v = qkv_heads(z, g_q[l], g_k[l])
        q = apply_rope(q, cos, sin)
        k = apply_rope(k, cos, sin)
        k_all = jnp.concatenate([k, kc], axis=1)
        v_all = jnp.concatenate([v, vc], axis=1)
        y_attn = blocked_gqa(q, k_all, v_all)
        y_conv, y_four = local_branches(z, w_conv[l])
        x = x + gt1 * merge_branches(z, y_conv, y_four, y_attn,
                                     w_conv_out[l], w_four_out[l], w_attn_out[l], w_o[l])
        x = x + gt2 * sq_relu_mlp(modulate(x, g_norm2[l], sh2, sc2), w_ff1[l], w_ff2[l])

        if l < DEPTH - 1:
            yc_attn = gqa(qc, kc, vc)
            yc_conv, yc_four = local_branches(zc, w_conv[l])
            ctx_s = ctx_s + cgt1 * merge_branches(zc, yc_conv, yc_four, yc_attn,
                                                  w_conv_out[l], w_four_out[l], w_attn_out[l], w_o[l])
            ctx_s = ctx_s + cgt2 * sq_relu_mlp(modulate(ctx_s, g_norm2[l], csh2, csc2),
                                               w_ff1[l], w_ff2[l])
    return x


DEPTH_2 = 4

N_MIXERS = 3
CHUNK = 64
NORM_EPS = 1e-6
RET_HEADS = 4
RET_QK_DIM = D_MODEL // RET_HEADS
RET_V_DIM = 2 * D_MODEL // RET_HEADS
RET_IN = 2 * RET_HEADS * RET_QK_DIM + 2 * RET_HEADS * RET_V_DIM
ROPE_BASE = 10000.0
CONV_WIDTH_2 = 31
GLA_HEADS = 4
GLA_K_DIM = D_MODEL // 2 // GLA_HEADS
GLA_V_DIM = D_MODEL // GLA_HEADS
GLA_IN = 2 * GLA_HEADS * GLA_K_DIM + 2 * GLA_HEADS * GLA_V_DIM
GLA_GATE_RANK = 16
GLA_GATE_NORMALIZER = 16.0
D_FF_2 = 4 * D_MODEL
N_RET = (DEPTH_2 + 2) // 3
N_CONV = (DEPTH_2 + 1) // 3
N_GLA = DEPTH_2 // 3

F32 = jnp.float32


def rmsnorm(x, gain=None):
    xf = x.astype(F32)
    y = xf * lax.rsqrt(jnp.mean(xf * xf, axis=-1, keepdims=True) + NORM_EPS)
    if gain is not None:
        y = y * gain.astype(F32)
    return y.astype(x.dtype)

def layernorm(x, gain, bias):
    xf = x.astype(F32)
    mu = jnp.mean(xf, axis=-1, keepdims=True)
    var = jnp.mean(jnp.square(xf - mu), axis=-1, keepdims=True)
    y = (xf - mu) * lax.rsqrt(var + NORM_EPS) * gain.astype(F32) + bias.astype(F32)
    return y.astype(x.dtype)

def split_heads(t, n):
    b, l, _ = t.shape
    return t.reshape(b, l, n, -1).transpose(0, 2, 1, 3)

def merge_heads(t):
    b, n, l, d = t.shape
    return t.transpose(0, 2, 1, 3).reshape(b, l, n * d)

def rotary(t, positions):
    d = t.shape[-1]
    half = d // 2
    inv_freq = ROPE_BASE ** (-jnp.arange(half, dtype=F32) / half)
    ang = positions.astype(F32)[:, None, :, None] * inv_freq
    cos, sin = jnp.cos(ang), jnp.sin(ang)
    tf = t.astype(F32)
    t1, t2 = tf[..., :half], tf[..., half:]
    return jnp.concatenate([t1 * cos - t2 * sin, t2 * cos + t1 * sin], axis=-1).astype(t.dtype)

def gated_linear_scan(q, k, v, log_g, strict):
    dtype = v.dtype
    bsz, nh, seq, dk = q.shape
    dv = v.shape[-1]
    n = seq // CHUNK
    q = q.astype(F32).reshape(bsz, nh, n, CHUNK, dk)
    k = k.astype(F32).reshape(bsz, nh, n, CHUNK, dk)
    v = v.astype(F32).reshape(bsz, nh, n, CHUNK, dv)
    lg = log_g.astype(F32)
    lg = lg.reshape(lg.shape[0], nh, n, CHUNK, lg.shape[-1])
    c = jnp.cumsum(lg, axis=3)
    c_last = c[:, :, :, -1:, :]
    q_dec = q * jnp.exp(c)
    k_dec = k * jnp.exp(-c)
    k_end = k * jnp.exp(c_last - c)
    mask = jnp.tril(jnp.ones((CHUNK, CHUNK), dtype=bool), k=-1 if strict else 0)
    scores = jnp.einsum("bhncd,bhnsd->bhncs", q_dec, k_dec)
    o_intra = jnp.einsum("bhncs,bhnsv->bhncv", jnp.where(mask, scores, 0.0), v)
    chunk_decay = jnp.exp(c_last[:, :, :, 0, :])

    def step(state, inp):
        qd, ke, vv, dec = inp
        o = jnp.einsum("bhcd,bhdv->bhcv", qd, state)
        state = dec[..., None] * state + jnp.einsum("bhcd,bhcv->bhdv", ke, vv)
        return state, o

    state0 = jnp.zeros((bsz, nh, dk, dv), F32)
    xs = (jnp.moveaxis(q_dec, 2, 0), jnp.moveaxis(k_end, 2, 0),
          jnp.moveaxis(v, 2, 0), jnp.moveaxis(chunk_decay, 2, 0))
    _, o_inter = lax.scan(step, state0, xs)
    o = o_intra + jnp.moveaxis(o_inter, 0, 2)
    return o.reshape(bsz, nh, seq, dv).astype(dtype)

def bidirectional_scan(q, k, v, log_g_fwd, log_g_bwd):
    fwd = gated_linear_scan(q, k, v, log_g_fwd, strict=False)
    rev = lambda t: jnp.flip(t, axis=2)
    bwd = rev(gated_linear_scan(rev(q), rev(k), rev(v), rev(log_g_bwd), strict=True))
    return fwd + bwd

def retention(u, positions, w_in, decay_logit, w_out):
    seq = u.shape[1]
    qk = RET_HEADS * RET_QK_DIM
    vd = RET_HEADS * RET_V_DIM
    q, k, v, g = jnp.split(u @ w_in, [qk, 2 * qk, 2 * qk + vd], axis=-1)
    q = rotary(split_heads(q, RET_HEADS), positions) * (RET_QK_DIM ** -0.5)
    k = rotary(split_heads(k, RET_HEADS), positions)
    v = split_heads(v, RET_HEADS)
    log_gamma = jax.nn.log_sigmoid(decay_logit.astype(F32))
    lg = lambda d: jnp.broadcast_to(log_gamma[d][None, :, None, None], (1, RET_HEADS, seq, 1))
    o = bidirectional_scan(q, k, v, lg(0), lg(1))
    o = merge_heads(rmsnorm(o)) * jax.nn.silu(g)
    return o @ w_out

def conformer_conv(u, w_in, b_in, w_dw, b_dw, ln_gain, ln_bias, w_out, b_out):
    a, gate = jnp.split(u @ w_in + b_in, 2, axis=-1)
    h = a * jax.nn.sigmoid(gate)
    pad = CONV_WIDTH_2 // 2
    h = lax.conv_general_dilated(
        h, w_dw[:, None, :].astype(h.dtype), window_strides=(1,), padding=[(pad, pad)],
        dimension_numbers=("NWC", "WIO", "NWC"), feature_group_count=D_MODEL) + b_dw
    h = jax.nn.silu(layernorm(h, ln_gain, ln_bias))
    return h @ w_out + b_out

def gla(u, w_in, gate_w1, gate_w2, gate_b, norm_gain, w_out):
    kd = GLA_HEADS * GLA_K_DIM
    vd = GLA_HEADS * GLA_V_DIM
    q, k, v, r = jnp.split(u @ w_in, [kd, 2 * kd, 2 * kd + vd], axis=-1)
    q = split_heads(q, GLA_HEADS) * (GLA_K_DIM ** -0.5)
    k = split_heads(k, GLA_HEADS)
    v = split_heads(v, GLA_HEADS)

    def log_gate(d):
        logits = (u @ gate_w1[d]) @ gate_w2[d] + gate_b[d]
        return split_heads(jax.nn.log_sigmoid(logits.astype(F32)) / GLA_GATE_NORMALIZER, GLA_HEADS)

    o = bidirectional_scan(q, k, v, log_gate(0), log_gate(1))
    o = merge_heads(rmsnorm(o, norm_gain)) * jax.nn.silu(r)
    return o @ w_out

def sq_relu_mlp_2(u, w_up, w_down):
    return jnp.square(jax.nn.relu(u @ w_up)) @ w_down

def second_inputs(seed: int = 0) -> dict:
    key = jax.random.key(seed)
    ks = jax.random.split(key, 24)
    nrm = lambda k, shape, scale: jax.random.normal(k, shape, F32) * scale
    x = jax.random.normal(ks[0], (BATCH, SEQ, D_MODEL), F32)
    positions = (jnp.arange(SEQ, dtype=jnp.int32)[None, :]
                 + jax.random.randint(ks[1], (BATCH, 1), 0, SEQ, dtype=jnp.int32))
    norm_gains = 1.0 + nrm(ks[2], (DEPTH_2, 4, D_MODEL), 0.1)
    ret_w_in = nrm(ks[3], (N_RET, D_MODEL, RET_IN), D_MODEL ** -0.5)
    a = 5.0 + jnp.arange(RET_HEADS, dtype=F32)
    base_logit = jnp.log(2.0 ** a - 1.0)
    ret_decay_logit = base_logit + nrm(ks[4], (N_RET, 2, RET_HEADS), 0.05)
    ret_w_out = nrm(ks[5], (N_RET, RET_HEADS * RET_V_DIM, D_MODEL), (RET_HEADS * RET_V_DIM) ** -0.5)
    conv_w_in = nrm(ks[6], (N_CONV, D_MODEL, 2 * D_MODEL), D_MODEL ** -0.5)
    conv_b_in = nrm(ks[7], (N_CONV, 2 * D_MODEL), 0.02)
    conv_w_dw = nrm(ks[8], (N_CONV, CONV_WIDTH_2, D_MODEL), CONV_WIDTH_2 ** -0.5)
    conv_b_dw = nrm(ks[9], (N_CONV, D_MODEL), 0.02)
    conv_ln_gain = 1.0 + nrm(ks[10], (N_CONV, D_MODEL), 0.1)
    conv_ln_bias = nrm(ks[11], (N_CONV, D_MODEL), 0.02)
    conv_w_out = nrm(ks[12], (N_CONV, D_MODEL, D_MODEL), D_MODEL ** -0.5)
    conv_b_out = nrm(ks[13], (N_CONV, D_MODEL), 0.02)
    gla_w_in = nrm(ks[14], (N_GLA, D_MODEL, GLA_IN), D_MODEL ** -0.5)
    gla_gate_w1 = nrm(ks[15], (N_GLA, 2, D_MODEL, GLA_GATE_RANK), D_MODEL ** -0.5)
    gla_gate_w2 = nrm(ks[16], (N_GLA, 2, GLA_GATE_RANK, GLA_HEADS * GLA_K_DIM), GLA_GATE_RANK ** -0.5)
    gla_gate_b = nrm(ks[17], (N_GLA, 2, GLA_HEADS * GLA_K_DIM), 0.1)
    gla_norm_gain = 1.0 + nrm(ks[18], (N_GLA, GLA_V_DIM), 0.1)
    gla_w_out = nrm(ks[19], (N_GLA, GLA_HEADS * GLA_V_DIM, D_MODEL), (GLA_HEADS * GLA_V_DIM) ** -0.5)
    mlp_w_up = nrm(ks[20], (DEPTH_2, D_MODEL, D_FF_2), D_MODEL ** -0.5)
    mlp_w_down = nrm(ks[21], (DEPTH_2, D_FF_2, D_MODEL), D_FF_2 ** -0.5)
    return {
        "x": x, "positions": positions, "norm_gains": norm_gains,
        "ret_w_in": ret_w_in, "ret_decay_logit": ret_decay_logit, "ret_w_out": ret_w_out,
        "conv_w_in": conv_w_in, "conv_b_in": conv_b_in, "conv_w_dw": conv_w_dw,
        "conv_b_dw": conv_b_dw, "conv_ln_gain": conv_ln_gain, "conv_ln_bias": conv_ln_bias,
        "conv_w_out": conv_w_out, "conv_b_out": conv_b_out,
        "gla_w_in": gla_w_in, "gla_gate_w1": gla_gate_w1, "gla_gate_w2": gla_gate_w2,
        "gla_gate_b": gla_gate_b, "gla_norm_gain": gla_norm_gain, "gla_w_out": gla_w_out,
        "mlp_w_up": mlp_w_up, "mlp_w_down": mlp_w_down,
    }

def second_block(x, positions, norm_gains, ret_w_in, ret_decay_logit, ret_w_out,
              conv_w_in, conv_b_in, conv_w_dw, conv_b_dw, conv_ln_gain, conv_ln_bias,
              conv_w_out, conv_b_out, gla_w_in, gla_gate_w1, gla_gate_w2, gla_gate_b,
              gla_norm_gain, gla_w_out, mlp_w_up, mlp_w_down):
    h = x
    for i in range(DEPTH_2):
        kind = i % N_MIXERS
        j = i // N_MIXERS
        u = rmsnorm(h, norm_gains[i, 0])
        if kind == 0:
            y = retention(u, positions, ret_w_in[j], ret_decay_logit[j], ret_w_out[j])
        elif kind == 1:
            y = conformer_conv(u, conv_w_in[j], conv_b_in[j], conv_w_dw[j], conv_b_dw[j],
                               conv_ln_gain[j], conv_ln_bias[j], conv_w_out[j], conv_b_out[j])
        else:
            y = gla(u, gla_w_in[j], gla_gate_w1[j], gla_gate_w2[j], gla_gate_b[j],
                    gla_norm_gain[j], gla_w_out[j])
        h = h + rmsnorm(y, norm_gains[i, 1])
        u = rmsnorm(h, norm_gains[i, 2])
        h = h + rmsnorm(sq_relu_mlp_2(u, mlp_w_up[i], mlp_w_down[i]), norm_gains[i, 3])
    return h


def setup_inputs(seed=0):
    out = dict(first_inputs(seed))
    for name, value in second_inputs(seed + 1).items():
        if name != "x":
            out[name + "_2"] = value
    return out


def reference(
    x, c, ctx, c_ctx, w_mod, b_mod, g_norm1, g_norm2, w_in, w_conv, g_q, g_k, w_conv_out,
    w_four_out, w_attn_out, w_o, w_ff1, w_ff2, positions_2, norm_gains_2, ret_w_in_2,
    ret_decay_logit_2, ret_w_out_2, conv_w_in_2, conv_b_in_2, conv_w_dw_2, conv_b_dw_2,
    conv_ln_gain_2, conv_ln_bias_2, conv_w_out_2, conv_b_out_2, gla_w_in_2, gla_gate_w1_2,
    gla_gate_w2_2, gla_gate_b_2, gla_norm_gain_2, gla_w_out_2, mlp_w_up_2, mlp_w_down_2,
):
    x = first_block(
        x, c, ctx, c_ctx, w_mod, b_mod, g_norm1, g_norm2, w_in, w_conv, g_q, g_k, w_conv_out,
        w_four_out, w_attn_out, w_o, w_ff1, w_ff2,
    )
    return second_block(
        x, positions_2, norm_gains_2, ret_w_in_2, ret_decay_logit_2, ret_w_out_2, conv_w_in_2,
        conv_b_in_2, conv_w_dw_2, conv_b_dw_2, conv_ln_gain_2, conv_ln_bias_2, conv_w_out_2,
        conv_b_out_2, gla_w_in_2, gla_gate_w1_2, gla_gate_w2_2, gla_gate_b_2, gla_norm_gain_2,
        gla_w_out_2, mlp_w_up_2, mlp_w_down_2,
    )


_drawn_inputs = setup_inputs


def setup_inputs(seed=0):
    import zlib

    import numpy as np

    out = dict(_drawn_inputs(seed))
    spreads = {}
    factors = {'g_q': 8.0, 'g_k': 8.0, 'conv_b_in_2': 2.667, 'conv_ln_bias_2': 2.946}
    for name, (base, spread) in spreads.items():
        noise = np.random.default_rng([zlib.crc32(name.encode()), seed]).standard_normal(out[name].shape)
        drawn = base * np.exp(spread * noise) if base else spread * noise
        out[name] = jnp.asarray(drawn.astype(out[name].dtype))
    for name, factor in factors.items():
        out[name] = (out[name] * factor).astype(out[name].dtype)
    return out
```

```python
from contextlib import ExitStack

import numpy as np
import concourse.bass as bass
from concourse import mybir

F32 = mybir.dt.float32
F32R = mybir.dt.float32r
I32 = mybir.dt.int32
ALU = mybir.AluOpType
ACT = mybir.ActivationFunctionType
AX_X = mybir.AxisListType.X

P = 128
D = 1024
KT = D // P
TOK = 256
TT = TOK // P
FF = 4 * D
NM = 6 * KT
EPS = 1e-6
RAW = 8
SPLIT = 4
LEAD = SPLIT - 1
DEPTH = 2
HEADS, HD = 8, 64
CHUNK = 64


def block1_stages():
    s = []
    for l in range(DEPTH):
        s.append((f"mod{l}", NM, f"mod{l}"))
        for who in ("ctx", "x"):
            if who == "ctx" and l == DEPTH - 1:
                s.append((f"ctx{l}.kv", 2, f"small{l}"))
                continue
            for part, n in (("small", 14), ("gates", 24), ("outs", 8), ("wo", 8), ("up", 32), ("down", 32)):
                s.append((f"{who}{l}.{part}", n, f"{part}{l}"))
    return s


def block2_stages():
    s = []
    for i in range(4):
        if i % 3 == 0:
            parts = (("qk", 16), ("v", 16), ("g", 16), ("out", 16))
        elif i % 3 == 1:
            parts = (("glu", 16), ("out", 8))
        else:
            parts = (("gate", 2), ("qk", 8), ("v", 8), ("r", 8), ("out", 8))
        for part, n in parts + (("up", 32), ("down", 32)):
            s.append((f"b{i}.{part}", n, f"b{i}.{part}"))
    return s


STAGES = block1_stages() + block2_stages()
FIRST, TOTAL = {}, 0
for _name, _n, _src in STAGES:
    FIRST[_name] = TOTAL
    TOTAL += _n
COUNT = {name: n for name, n, _ in STAGES}
SOURCE, N_STREAM = {}, 0
for _name, _n, _src in STAGES:
    if _src not in SOURCE:
        SOURCE[_src] = N_STREAM
        N_STREAM += 14 if _src.startswith("small") else _n

def columns(*parts):
    at, out = 0, {}
    for name, n in parts:
        out[name] = at
        at += n
    return out, at


VEC, N_VEC = columns(
    ("b_mod0", NM), ("b_mod1", NM), ("g1_0", KT), ("g1_1", KT), ("g2_0", KT), ("g2_1", KT),
    ("w_conv0", 6), ("w_conv1", 6), ("g_q0", 1), ("g_q1", 1), ("g_k0", 1), ("g_k1", 1), ("c", 2 * KT),
    ("gains", 16 * KT), ("b_in", 16), ("w_dw", 31 * KT), ("b_dw", KT), ("ln_gain", KT), ("ln_bias", KT),
    ("b_out", KT), ("gate_b", 8), ("gla_gain", 2), ("decay", 16), ("inv_freq", 1),
)
CON, N_CON = columns(
    ("ones", P), ("ident", P), ("rot", P), ("head_sel", 2), ("part_sel", 2), ("dim_dft", 2 * P), ("tok_cos", TT * TOK),
    ("tok_sin", TT * TOK), ("rope_cos", TOK), ("rope_sin", TOK),
)
CON2, N_CON2 = columns(("after", TT * TOK), ("before", TT * TOK), ("mask_fwd", CHUNK), ("mask_bwd", CHUNK))
CON |= {name: CON["dim_dft"] + at for name, at in CON2.items()}
CON["pos_cos"] = CON["dim_dft"] + N_CON2
CON["pos_sin"] = CON["pos_cos"] + TOK


class Unit:

    def __init__(self, stage, j, e=0, turn=0):
        self.j, self.e, self.turn, self.s = j, e, turn, FIRST[stage] + j

    def raw(self, lead=0):
        return (self.s + lead) % RAW

    def split(self, lead=0):
        return (self.s + lead) % SPLIT

    bank = property(lambda self: self.s % 4)
    index = property(lambda self: self.j + self.e)


def at_least(eng, sem, known, e=0):
    if isinstance(e, int):
        if known + e > 0:
            eng.wait_ge(sem, known + e)
        return
    assert known >= 0
    eng.wait_ge(sem, e + known)


def over_units(eng, stage, body, peel=False):
    n = COUNT[stage]
    head = RAW if (FIRST[stage] == 0 or peel) and n > RAW else 0
    tail = RAW if FIRST[stage] + n == TOTAL and n > RAW else 0
    for j in range(head):
        body(Unit(stage, j))
    loops = (n - head - tail) // RAW
    if loops > 1:
        with eng.Fori(0, loops) as i:
            e = i * RAW
            for j in range(head, head + RAW):
                body(Unit(stage, j, e, i))
    else:
        tail += loops * RAW
    done = head + (loops * RAW if loops > 1 else 0)
    for j in range(done, n):
        body(Unit(stage, j))


def build(nc, stream, xT, ctxT, vec_d, con_d, con2_d, pos_d, w2_d, out_d):
    ctx = ExitStack()
    with ctx:
        def sb(name, cols, dt=F32):
            return ctx.enter_context(nc.sbuf_tensor(name, [P, cols], dt))

        def tiles(ap, n):
            return ap.rearrange("p (k n) -> p k n", k=n)

        def sem(name):
            return ctx.enter_context(nc.semaphore(name))

        bank = [ctx.enter_context(nc.psum_tensor(f"bank{i}", [P, 512], F32)) for i in range(8)]
        w_raw = tiles(sb("w_raw", RAW * D)[:, :], RAW)
        w_hi = tiles(sb("w_hi", SPLIT * D, F32R)[:, :], SPLIT)
        w_lo = tiles(sb("w_lo", SPLIT * D, F32R)[:, :], SPLIT)
        resid = {w: tiles(sb(f"resid_{w}", KT * TOK)[:, :], KT) for w in ("x", "ctx")}
        h_hi = tiles(sb("h_hi", KT * TOK, F32R)[:, :], KT)
        h_lo = tiles(sb("h_lo", KT * TOK, F32R)[:, :], KT)
        vec = sb("vec", N_VEC)
        con = sb("con", N_CON)
        scratch = tiles(sb("scratch", 24 * TOK)[:, :], 24)
        squares, scaled, full, gates = scratch[:, 0:8, :], scratch[:, 8:16, :], scratch[:, 16:24, :], scratch
        ring = sb("ring", 6 * TOK)
        relu, relu_sq = tiles(ring[:, 0:4 * TOK], 4), tiles(ring[:, 4 * TOK:6 * TOK], 2)
        spread = tiles(ring[:, 0:10 * P], 10)
        mod_rows = ring[0:4, 4 * TOK:5 * TOK]
        variance = sb("variance", 20)
        inv_rms = sb("inv_rms", 20)
        neg_half = sb("neg_half", 1)
        cond_sig = sb("cond_sig", 2 * KT)
        cond_full = sb("cond_full", 2 * KT)
        cond_parts = tiles(sb("cond_parts", 4 * KT, F32R)[:, :], KT)
        mod_raw = sb("mod_raw", 2 * NM)
        mod = tiles(sb("mod", 2 * NM)[:, :], NM)
        mod_gain = tiles(sb("mod_gain", 4 * KT)[:, :], 4)
        ctx_k = sb("ctx_k", TOK)
        ctx_v = tiles(sb("ctx_v", TT * P)[:, :], TT)

        spare = resid["ctx"].rearrange("p k n -> p (k n)")
        decay_m, scores = tiles(spare[:, 0:1024], 2), tiles(spare[:, 1024:2048], 2)
        gla_low, gla_state, gla_s = spare[:, 0:TOK], tiles(spare[:, 256:1792], 6), tiles(spare[:, 1792:2048], TT)

        def added(j):
            b, half = ((4, 0), (6, 0), (4, 1), (6, 1), (5, 0), (7, 1))[j]
            return bank[b][:, half * TOK:(half + 1) * TOK]
        decay_end = sb("decay_end", 32)
        sum_ring = tiles(ring[:, 4 * TOK:5 * TOK], 2)
        gate_w2 = ring[:, 4 * TOK:6 * TOK]
        log_decay = sb("log_decay", 16)
        log_tmp = sb("log_tmp", 48)
        row_max = sb("row_max", TT)
        neg_max = sb("neg_max", TT)
        row_sum = sb("row_sum", TT)
        inv_sum = sb("inv_sum", TT)

        def overlay(*parts):
            with ExitStack() as inner:
                return [inner.enter_context(nc.sbuf_tensor(name, [P, cols], dt)) for name, cols, dt in parts]

        y_hi_t, y_lo_t, work = overlay(("y_hi", KT * TOK, F32R), ("y_lo", KT * TOK, F32R), ("work", 48 * TOK, F32))
        y_hi, y_lo = tiles(y_hi_t[:, :], KT), tiles(y_lo_t[:, :], KT)

        def zone(at, n, width=TOK):
            return tiles(work[:, at:at + n * width], n)

        z_k = work[:, 0:TOK]
        z_v = zone(256, TT, P)
        z_q, z_four, z_conv = zone(512, 4), zone(1536, 2), zone(2048, 6)
        qk_n, qk = zone(3584, 5), zone(4864, 5)
        four_mid = zone(6144, 4)
        conv_in = zone(7168, 2, TOK + 2)
        prob, prob_t = zone(7684, TT, 512), zone(8708, 4)
        terms = work[:, 9732:9732 + 6 * TOK].rearrange("p (a b n) -> p a b n", a=2, b=3)
        sums = zone(512, 4)
        ret_qk, ret_v_t, ret_o = overlay(("ret_qk", 32 * TOK, F32), ("ret_v", 16 * TOK, F32), ("ret_o", 16 * TOK, F32))
        ret_hi, ret_lo = overlay(("ret_hi", 16 * TOK, F32R), ("ret_lo", 16 * TOK, F32R))
        ret_raw, ret_rot = ret_qk[:, 0:16 * TOK], ret_qk[:, 16 * TOK:32 * TOK]
        ret_v = tiles(ret_v_t[:, :], TT)
        (conv_t,) = overlay(("conv_t", KT * (TOK + 30) + 2 * KT * TOK, F32))
        glu = tiles(conv_t[:, 0:KT * (TOK + 30)], KT)
        dw_out = conv_t[:, KT * (TOK + 30):KT * (TOK + 30) + KT * TOK]
        dw = tiles(dw_out, KT)
        (gla_t,) = overlay(("gla_t", 64 * TOK, F32))
        gla_q, gla_k = gla_t[:, 0:4 * TOK], gla_t[:, 4 * TOK:8 * TOK]
        gla_v = tiles(gla_t[:, 8 * TOK:16 * TOK], TT)
        log_g, cum_g = gla_t[:, 16 * TOK:24 * TOK], gla_t[:, 24 * TOK:32 * TOK]
        decayed = tiles(gla_t[:, 32 * TOK:56 * TOK], 6)
        ke_tok = tiles(gla_t[:, 56 * TOK:64 * TOK], 16)
        hidden_hi = sb("hidden_hi", 32 * TOK, F32R)
        hidden_lo = sb("hidden_lo", 32 * TOK, F32R)


        def V(name, i=0, n=1):
            return vec[:, VEC[name] + i:VEC[name] + i + n]

        def C(name, i=0, n=None):
            n = n or P
            return con[:, CON[name] + i:CON[name] + i + n]

        consts_in = sem("consts_in")
        raw_in = [sem(f"raw_in{i}") for i in range(RAW)]
        hi_ready = sem("hi_ready")
        lo_ready = sem("lo_ready")
        unit_done = sem("unit_done")
        evicted = sem("evicted")
        cond_sig_ready = sem("cond_sig_ready")
        cond_full_ready = sem("cond_full_ready")
        cond_hi_ready = sem("cond_hi_ready")
        cond_ready = sem("cond_ready")
        mod_cols_ready = sem("mod_cols_ready")
        mod_cols_out = sem("mod_cols_out")
        mod_ready = sem("mod_ready")
        sq_ready = sem("sq_ready")
        sums_ready = sem("sums_ready")
        var_ready = sem("var_ready")
        rms_ready = sem("rms_ready")
        spread_ready = sem("spread_ready")
        bcast_ready = sem("bcast_ready")
        norm_ready = sem("norm_ready")
        full_ready = sem("full_ready")
        h_hi_ready = sem("h_hi_ready")
        h_lo_ready = sem("h_lo_ready")
        relu_ready = sem("relu_ready")
        hid_hi_ready = sem("hid_hi_ready")
        hid_sq_ready = sem("hid_sq_ready")
        hid_ready = sem("hid_ready")
        pool_const = sem("pool_const")
        dve_chain = sem("dve_chain")
        qk_norm_ready = sem("qk_norm_ready")
        rot_ready = sem("rot_ready")
        rope_part = sem("rope_part")
        qk_ready = sem("qk_ready")
        four_ready = sem("four_ready")
        four_mid_ready = sem("four_mid_ready")
        four_out = sem("four_out")
        four_hi = sem("four_hi")
        y_full_ready = sem("y_full_ready")
        conv_hi = sem("conv_hi")
        y_ready = sem("y_ready")
        s_ready = sem("s_ready")
        max_ready = sem("max_ready")
        exp_ready = sem("exp_ready")
        p_ready = sem("p_ready")
        pt_ready = sem("pt_ready")
        pt_act = sem("pt_act")
        pt_dve = sem("pt_dve")
        o_ready = sem("o_ready")
        o_hi = sem("o_hi")
        o_lo = sem("o_lo")
        terms_ready = sem("terms_ready")
        merged = sem("merged")
        merge_step = sem("merge_step")
        stored = sem("stored")
        con2_in = sem("con2_in")
        pos_ready = sem("pos_ready")
        angle_ready = sem("angle_ready")
        sin_ready = sem("sin_ready")
        updated = sem("updated")
        copied = sem("copied")
        tanh_ready = sem("tanh_ready")
        gate_ready = sem("gate_ready")
        rot_a = sem("rot_a")
        rot_done = sem("rot_done")
        decay_arg = sem("decay_arg")
        decay_ready = sem("decay_ready")
        scores_ready = sem("scores_ready")
        weighted = sem("weighted")
        head_out = sem("head_out")
        head_copied = sem("head_copied")
        head_summed = sem("head_summed")
        heads_wide = sem("heads_wide")
        gated = sem("gated")
        gated_full = sem("gated_full")
        ret_hi_ready = sem("ret_hi_ready")
        ret_ready = sem("ret_ready")
        glu_a = sem("glu_a")
        glu_ready = sem("glu_ready")
        pad_ready = sem("pad_ready")
        tap = sem("tap")
        dw_ready = sem("dw_ready")
        centred = sem("centred")
        ln_scaled = sem("ln_scaled")
        silu_in = sem("silu_in")
        w2_in = sem("w2_in")
        low_ready = sem("low_ready")
        logits_ready = sem("logits_ready")
        gla_dve = sem("gla_dve")
        gla_act = sem("gla_act")
        gla_pool = sem("gla_pool")
        ke_ready = sem("ke_ready")
        ke_out = sem("ke_out")
        state_in = sem("state_in")
        state_ready = sem("state_ready")
        gla_o = sem("gla_o")

        CHAINS, FILLS, NORMS, squared = {}, {}, {}, [0]

        def chain(name, width):
            CHAINS[name] = (len(CHAINS), squared[0])
            squared[0] += width

        def fill(name):
            FILLS[name] = len(FILLS)
            if "norm" in name:
                NORMS[name] = len(NORMS)

        for l in range(DEPTH):
            for who in ("ctx", "x"):
                kv = who == "ctx" and l == DEPTH - 1
                chain(f"{who}{l}.norm1", KT); fill(f"{who}{l}.norm1")
                chain(f"{who}{l}.qk", 1 if kv else 5)
                if not kv:
                    fill(f"{who}{l}.m")
                    chain(f"{who}{l}.norm2", KT); fill(f"{who}{l}.norm2")
        for i in range(4):
            b = f"b{i}"
            chain(f"{b}.n0", KT); fill(f"{b}.n0"); NORMS[f"{b}.n0"] = len(NORMS)
            if i % 3 == 0:
                chain(f"{b}.heads", 16)
            elif i % 3 == 1:
                chain(f"{b}.mean", 0); chain(f"{b}.var", KT); fill(f"{b}.y"); NORMS[f"{b}.y"] = len(NORMS)
            else:
                chain(f"{b}.heads", KT); fill(f"{b}.y"); NORMS[f"{b}.y"] = len(NORMS)
            chain(f"{b}.n1", 0)
            chain(f"{b}.n2", KT); fill(f"{b}.n2"); NORMS[f"{b}.n2"] = len(NORMS)
            chain(f"{b}.n3", 0)
        RETS = {"b0": 0, "b3": 1}
        GATES = {"b0": 0, "b2": 16, "b3": 24}
        FIRST_PART = ("qk", "glu", "gate")
        CHAIN_READS = {f"b{i}.{part}": CHAINS[f"b{i}.{c}"][0] for i in range(4) for part, c in (("out", "n1"), ("down", "n3"))}
        COPIES = {f"b{i}.{part}": 8 * (2 * i + j) for i in range(4) for j, part in enumerate(("out", "down"))}
        half = 4 * TOK
        sq_flat = squares.rearrange("p k n -> p (k n)")
        GLA_ARG = [(cum_g[:, 0:half], sq_flat[:, 0:half]), (sq_flat[:, half:2 * half], log_g[:, half:2 * half])]

        def full_ring(k):
            return squares[:, k % 8, :]
        TWO_PI = [6.28125, 0.001934051513671875, float(2 * np.pi - 6.28125 - 0.001934051513671875)]

        PASSES = {w: n for n, w in enumerate(("ctx0", "x0", "x1"))}
        FFNS = {w: n for n, w in enumerate(("ctx0", "x0", "x1", "b0", "b1", "b2", "b3"))}

        block = ctx.enter_context(nc.Block())

        @block.sync
        def _(sp):
            for dst, src in ((vec[:, :], vec_d), (con[:, :], con_d),
                             (resid["ctx"], ctxT.rearrange("(k p) t -> p k t", p=P)),
                             (resid["x"], xT.rearrange("(k p) t -> p k t", p=P))):
                sp.dma_start(dst, src).then_inc(consts_in, 16)
            rows = stream.rearrange("u p n -> (u p) n")

            def block2_inputs():
                sp.wait_ge(o_lo, 3 * HEADS)
                sp.wait_ge(y_ready, 3 * 4)
                at = CON["dim_dft"]
                sp.dma_start(con[:, at:at + N_CON2], con2_d).then_inc(con2_in, 16)
                sp.wait_ge(evicted, FIRST["x1.up"])
                sp.dma_start(scaled[:, 0, :].bitcast(I32), pos_d).then_inc(con2_in, 16)
            for stage, _, src in STAGES:

                def load(u, src=src):
                    at_least(sp, lo_ready, u.s - RAW + 1, u.e)
                    sp.dma_start(w_raw[:, u.raw(), :], rows[bass.ds((SOURCE[src] + u.j + u.e) * P, P), :]
                                 ).then_inc(raw_in[u.raw()], 16)

                over_units(sp, stage, load)
                if stage == "x1.down":
                    block2_inputs()
                if stage == "b1.down":
                    sp.wait_ge(hid_ready, 32 * FFNS["b1"] + 32)
                    sp.dma_start(gate_w2[0:48, :], w2_d).then_inc(w2_in, 16)
            sp.wait_ge(updated, KT * 8)
            sp.dma_start(out_d.rearrange("(k p) t -> p k t", p=P), resid["x"]).then_inc(stored, 16)
            sp.wait_ge(stored, 16)

        @block.tensor
        def _(pe):
            def mm(out, lhsT, rhs, start=True, stop=True):
                return pe.matmul(out, lhsT, rhs, start=start, stop=stop, skip_group_check=True)

            def product(u, out, hi, lo, ks=range(KT), first=True, last=True):
                w = u.split()
                for k in ks:
                    cols = slice(k * P, (k + 1) * P)
                    a, b = first and k == ks[0], last and k == ks[-1]
                    mm(out, w_hi[:, w, cols], hi(k), start=a, stop=False)
                    mm(out, w_hi[:, w, cols], lo(k), start=False, stop=False)
                    done = mm(out, w_lo[:, w, cols], hi(k), start=False, stop=b)
                return done

            def pair_by_token(u):
                if u.j % 2 == 0:
                    return
                at_least(pe, lo_ready, u.s + 1, u.e)
                at_least(pe, evicted, u.s - 3, u.e)
                for t in range(TT):
                    tok = slice(t * P, (t + 1) * P)
                    o = bank[(u.s - 1 + t) % 4][:, 0:2 * P]
                    for k in range(KT):
                        w = slice(u.split(-1), u.split(-1) + 2)
                        both = lambda part: part[:, w, k * P:(k + 1) * P]
                        mm(o, H(k)[:, tok], both(w_hi), start=k == 0, stop=False)
                        mm(o, L(k)[:, tok], both(w_hi), start=False, stop=False)
                        m = mm(o, H(k)[:, tok], both(w_lo), start=False, stop=k == KT - 1)
                    m.then_inc(unit_done, 1)

            def product_by_token(u, out, hi, lo):
                w = u.split()
                for t in range(TT):
                    tok = slice(t * P, (t + 1) * P)
                    for k in range(KT):
                        cols = slice(k * P, (k + 1) * P)
                        o = out[:, tok]
                        mm(o, hi(k)[:, tok], w_hi[:, w, cols], start=k == 0, stop=False)
                        mm(o, lo(k)[:, tok], w_hi[:, w, cols], start=False, stop=False)
                        done = mm(o, hi(k)[:, tok], w_lo[:, w, cols], start=False, stop=k == KT - 1)
                return done

            def begin(u):
                at_least(pe, lo_ready, u.s + 1, u.e)
                at_least(pe, evicted, u.s - 3, u.e)

            H = lambda k: h_hi[:, k, :]
            L = lambda k: h_lo[:, k, :]
            Y = lambda k: y_hi[:, k, :]
            YL = lambda k: y_lo[:, k, :]

            def plain(u):
                begin(u)
                product(u, bank[u.bank][:, 0:TOK], H, L).then_inc(unit_done, 1)

            def statistics(name, width):
                r, sq0 = CHAINS[name]
                at_least(pe, var_ready, r)
                for k in range(width):
                    pe.wait_ge(sq_ready, sq0 + k + 1)
                    for t in range(TT):
                        s = mm(bank[7][:, t:t + 1], squares[:, k, t * P:(t + 1) * P], C("ones", n=1),
                               start=k == 0 and t == 0, stop=k == width - 1)
                s.then_inc(sums_ready, 1)

            def broadcast(name, n, banks):
                r, _ = CHAINS[name]
                pe.wait_ge(spread_ready, r + 1)
                for j in range(n):
                    for t in range(TT):
                        o = bank[banks[j // 2]][:, (j % 2) * TOK + t * P:(j % 2) * TOK + (t + 1) * P]
                        b = mm(o, spread[:, j * TT + t, :], C("ident"))
                b.then_inc(bcast_ready, 1)

            def operand(name):
                pe.wait_ge(h_lo_ready, KT * FILLS[name] + KT)

            def modulation(l):
                pe.wait_ge(cond_ready, 1)

                def body(u):
                    if u.j % 2 == 0:
                        return
                    at_least(pe, lo_ready, u.s + 1, u.e)
                    at_least(pe, evicted, u.s - 3, u.e)
                    pair = l * NM // 2 + u.j // 2
                    w = slice(u.split(-1), u.split(-1) + 2)
                    for k in range(KT):
                        for part in (w_hi, w_lo):
                            m = mm(bank[u.bank][0:4, 0:2 * P], cond_parts[:, k, :], part[:, w, k * P:(k + 1) * P],
                                   start=k == 0 and part is w_hi, stop=k == KT - 1 and part is w_lo)
                    m.then_inc(unit_done, 2)
                    at_least(pe, evicted, u.s + 1, u.e)
                    at_least(pe, mod_cols_out, pair - 1, u.turn * 4)
                    for i in range(2):
                        m = mm(bank[4 + pair % 2][:, 2 * i:2 * i + 2], mod_rows[:, i * P:(i + 1) * P],
                               con[0:4, CON["part_sel"]:CON["part_sel"] + 2])
                    m.then_inc(mod_cols_ready, 1)
                over_units(pe, f"mod{l}", body)

            def head_statistics(name, n):
                r, sq0 = CHAINS[name]
                at_least(pe, var_ready, r)
                for j in range(n):
                    pe.wait_ge(sq_ready, sq0 + j + 1)
                    for t in range(TT):
                        c = 4 * j + 2 * t
                        s = mm(bank[7][:, c:c + 2], squares[:, j, t * P:(t + 1) * P], C("head_sel", n=2))
                s.then_inc(sums_ready, 1)

            def small(w):
                operand(f"{w}.norm1")
                n = PASSES[w]
                for j in range(14):
                    u = Unit(f"{w}.small", j)
                    begin(u)
                    if j == 1:
                        product_by_token(u, bank[u.bank][:, 0:TOK], H, L).then_inc(unit_done, 1)
                    else:
                        product(u, bank[u.bank][:, 0:TOK], H, L).then_inc(unit_done, 1)
                    if j == 7:
                        head_statistics(f"{w}.qk", 5)
                    if j == 8:
                        pe.wait_ge(evicted, FIRST[f"{w}.small"] + 8)
                        for f in range(2):
                            for t in range(TT):
                                m = mm(bank[4 + f][:, t * 2 * P:(t + 1) * 2 * P],
                                       z_four[:, f, t * P:(t + 1) * P], C("dim_dft", n=2 * P))
                        m.then_inc(four_ready, 1)
                    if j == 9:
                        pe.wait_ge(four_mid_ready, n + 1)
                        broadcast(f"{w}.qk", 5, (4, 5, 6))
                    if j == 11:
                        pe.wait_ge(qk_norm_ready, 5 * n + 5)
                        if w != "ctx0":
                            for i in range(5):
                                m = mm(bank[4 + i // 2][:, (i % 2) * TOK:(i % 2 + 1) * TOK], C("rot"),
                                       qk_n[:, i, :])
                            m.then_inc(rot_ready, 1)
                        for f in range(2):
                            for t in range(TT):
                                for part, table in enumerate(("tok_cos", "tok_sin")):
                                    m = mm(bank[7][:, f * TOK:(f + 1) * TOK],
                                           four_mid[:, f * 2 + t, part * P:(part + 1) * P],
                                           C(table, t * TOK, TOK), start=t == 0 and part == 0,
                                           stop=t == TT - 1 and part == 1)
                        m.then_inc(four_out, 1)

            def attention(w):
                n = PASSES[w]
                keys = 2 if w == "ctx0" else 4
                K = [ctx_k[:, :]] if w == "ctx0" else [qk[:, 0, :], ctx_k[:, :]]
                VT = [ctx_v[:, t, :] for t in range(TT)]
                if w != "ctx0":
                    VT = [z_v[:, t, :] for t in range(TT)] + VT
                pe.wait_ge(qk_ready, n + 1)
                pe.wait_ge(y_ready, 4 * n + 2)
                for a in range(HEADS):
                    g = HEADS * n + a
                    rows = slice((a % 2) * HD, (a % 2) * HD + HD)
                    at_least(pe, o_lo, g)
                    at_least(pe, exp_ready, 2 * g)
                    for t in range(TT):
                        for i, keys_t in enumerate(K):
                            m = mm(bank[4 + t][:, i * TOK:(i + 1) * TOK],
                                   qk[rows, 1 + a // 2, t * P:(t + 1) * P], keys_t[rows, :])
                        m.then_inc(s_ready, 1)
                    plain(Unit(f"{w}.gates", 3 * a))
                    plain(Unit(f"{w}.gates", 3 * a + 1))
                    at_least(pe, pt_act, g)
                    at_least(pe, pt_dve, g)
                    for t in range(TT):
                        pe.wait_ge(p_ready, 2 * g + t + 1)
                        for k in range(keys):
                            o = bank[6 + k // 2][:, (k % 2) * TOK + t * P:(k % 2) * TOK + (t + 1) * P]
                            m = pe.transpose(o, prob[:, t, k * P:(k + 1) * P], C("ident"))
                    m.then_inc(pt_ready, 1)
                    plain(Unit(f"{w}.gates", 3 * a + 2))
                    pe.wait_ge(pt_act, g + 1)
                    pe.wait_ge(pt_dve, g + 1)
                    for k in range(keys):
                        m = mm(bank[4][rows, 0:TOK], VT[k][:, rows], prob_t[:, k, :], start=k == 0,
                               stop=k == keys - 1)
                    m.then_inc(o_ready, 1)

            def merge(w):
                n = PASSES[w]
                pe.wait_ge(o_lo, HEADS * n + HEADS)
                pe.wait_ge(y_ready, 4 * n + 4)

                def body(u):
                    begin(u)
                    at_least(pe, evicted, u.s - 1, u.e)
                    b = bank[u.bank]
                    product(u, b[:, 0:TOK], Y, YL, ks=range(0, 2))
                    product(u, b[:, TOK:2 * TOK], Y, YL, ks=range(2, 4))
                    product(u, bank[4 + u.s % 2][:, 0:TOK], Y, YL, ks=range(4, 8)).then_inc(unit_done, 1)
                over_units(pe, f"{w}.outs", body)

            def up(w):
                over_units(pe, f"{w}.up", plain)

            def down(w):
                f = FFNS[w]

                def body(u):
                    kg = u.j % 4
                    at_least(pe, lo_ready, u.s + 1, u.e)
                    if kg == 0:
                        at_least(pe, evicted, u.s - 4, u.e)
                    pe.wait_ge(hid_ready, 32 * f + KT * (kg + 1))
                    hid = lambda big: lambda k: big[:, (kg * KT + k) * TOK:(kg * KT + k + 1) * TOK]
                    product(u, bank[4 + (u.j // 4) % 2][:, 0:TOK], hid(hidden_hi), hid(hidden_lo),
                            first=kg == 0, last=kg == 3).then_inc(unit_done, 1)
                over_units(pe, f"{w}.down", body)

            def norm(name):
                statistics(name, KT)
                broadcast(name, 1, (6,))

            pe.wait_ge(consts_in, 16 * 4)
            for l in range(DEPTH):
                modulation(l)
                for who in ("ctx", "x"):
                    w = f"{who}{l}"
                    norm(f"{w}.norm1")
                    if w == "ctx1":
                        operand(f"{w}.norm1")
                        plain(Unit("ctx1.kv", 0))
                        u = Unit("ctx1.kv", 1)
                        begin(u)
                        product_by_token(u, bank[u.bank][:, 0:TOK], H, L).then_inc(unit_done, 1)
                        head_statistics("ctx1.qk", 1)
                        broadcast("ctx1.qk", 1, (4,))
                        continue
                    small(w)
                    attention(w)
                    merge(w)
                    operand(f"{w}.m")
                    over_units(pe, f"{w}.wo", plain)
                    norm(f"{w}.norm2")
                    operand(f"{w}.norm2")
                    up(w)
                    down(w)

            def post(name):
                r, _ = CHAINS[name]
                at_least(pe, var_ready, r)
                for k in range(KT):
                    for t in range(TT):
                        s = mm(bank[7][:, t:t + 1], squares[:, k, t * P:(t + 1) * P], C("ones", n=1),
                               start=k == 0 and t == 0, stop=k == KT - 1)
                s.then_inc(sums_ready, 1)
                broadcast(name, 1, (6,))

            def head_broadcast(name):
                broadcast(name, 4, (4, 5))

            def retention(b):
                n = RETS[b]
                qt = lambda i: ret_rot[:, i * TOK:(i + 1) * TOK]

                over_units(pe, f"{b}.qk", plain)
                over_units(pe, f"{b}.v", pair_by_token)
                pe.wait_ge(evicted, FIRST[f"{b}.g"])
                r, sq0 = CHAINS[f"{b}.heads"]
                at_least(pe, var_ready, r)
                for h in range(4):
                    pe.wait_ge(rot_done, 8 * n + 5 + h)
                    at_least(pe, weighted, 4 * n + h)
                    for t in range(TT):
                        for d in range(2):
                            m = mm(bank[4][:, t * TOK:(t + 1) * TOK], qt(8 + 2 * h + d)[:, t * P:(t + 1) * P],
                                   qt(2 * h + d), start=d == 0, stop=d == 1)
                    m.then_inc(scores_ready, 1)
                    plain(Unit(f"{b}.g", 4 * h))
                    plain(Unit(f"{b}.g", 4 * h + 1))
                    pe.wait_ge(weighted, 4 * n + h + 1)
                    at_least(pe, sq_ready, sq0 + 4 * h)
                    for v in range(4):
                        for t in range(TT):
                            m = mm(bank[5 + v // 2][:, (v % 2) * TOK:(v % 2 + 1) * TOK],
                                   ret_v[:, t, h * 512 + v * P:h * 512 + (v + 1) * P],
                                   scores[:, h % 2, t * TOK:(t + 1) * TOK], start=t == 0, stop=t == 1)
                    m.then_inc(head_out, 1)
                    plain(Unit(f"{b}.g", 4 * h + 2))
                    plain(Unit(f"{b}.g", 4 * h + 3))
                    pe.wait_ge(sq_ready, sq0 + 4 * h + 4)
                    for v in range(4):
                        for t in range(TT):
                            m = mm(bank[7][:, 2 * h + t:2 * h + t + 1],
                                   squares[:, 4 * (h % 2) + v, t * P:(t + 1) * P], C("ones", n=1),
                                   start=v == 0 and t == 0, stop=v == 3)
                    m.then_inc(head_summed, 1)
                mm(bank[7][0:1, 8:9], C("ones", n=1), C("ones", n=1)).then_inc(sums_ready, 1)
                head_broadcast(f"{b}.heads")

                def out(u):
                    kg = u.j % 2
                    at_least(pe, lo_ready, u.s + 1, u.e)
                    if kg == 0:
                        at_least(pe, evicted, u.s - 2, u.e)
                    pe.wait_ge(ret_ready, 16 * n + KT * (kg + 1))
                    part = lambda big: lambda k: big[:, (kg * KT + k) * TOK:(kg * KT + k + 1) * TOK]
                    product(u, bank[4 + (u.j // 2) % 2][:, 0:TOK], part(ret_hi), part(ret_lo),
                            first=kg == 0, last=kg == 1).then_inc(unit_done, 1)
                pe.wait_ge(heads_wide, n + 1)
                over_units(pe, f"{b}.out", out)

            def conformer(b):
                over_units(pe, f"{b}.glu", plain)
                r, _ = CHAINS[f"{b}.mean"]
                at_least(pe, var_ready, r)
                for k in range(KT):
                    pe.wait_ge(dw_ready, k + 1)
                    for t in range(TT):
                        s = mm(bank[7][:, t:t + 1], dw[:, k, t * P:(t + 1) * P], C("ones", n=1),
                               start=k == 0 and t == 0, stop=k == KT - 1)
                s.then_inc(sums_ready, 1)
                broadcast(f"{b}.mean", 1, (6,))
                statistics(f"{b}.var", KT)
                pe.wait_ge(centred, 1)
                broadcast(f"{b}.var", 1, (6,))
                operand(f"{b}.y")
                over_units(pe, f"{b}.out", plain)

            def gla(b):
                over_units(pe, f"{b}.gate", plain)
                pe.wait_ge(w2_in, 16)
                pe.wait_ge(low_ready, 1)
                for d in range(2):
                    rows = slice(32 * d, 32 * d + 16)
                    for h in range(4):
                        i = 4 * d + h
                        m = mm(bank[4 + i // 2][:, (i % 2) * TOK:(i % 2 + 1) * TOK],
                               gate_w2[rows, h * P:(h + 1) * P], gla_low[rows, :])
                m.then_inc(logits_ready, 1)
                over_units(pe, f"{b}.qk", plain)

                over_units(pe, f"{b}.v", pair_by_token)
                for d in range(2):
                    pe.wait_ge(ke_ready, d + 1)
                    for h in range(4):
                        for t in range(TT):
                            i = (d * 4 + h) * 2 + t
                            m = pe.transpose(bank[4 + i // 4][:, (i % 4) * P:(i % 4 + 1) * P],
                                             decayed[:, 3 * d + 2, h * TOK + t * P:h * TOK + (t + 1) * P],
                                             C("ident"))
                m.then_inc(ke_out, 1)
                pe.wait_ge(evicted, FIRST[f"{b}.r"])
                chunk = lambda c: slice((c % 2) * CHUNK, (c % 2 + 1) * CHUNK)
                for h in range(4):
                    col = lambda c: slice(h * TOK + c * CHUNK, h * TOK + (c + 1) * CHUNK)
                    if h == 0:
                        pe.wait_ge(state_in, 1)
                    else:
                        pe.wait_ge(gla_o, 2 * h)
                    for d in range(2):
                        for c in range(4):
                            m = mm(bank[7][chunk(c), d * P + (c // 2) * CHUNK:d * P + (c // 2 + 1) * CHUNK],
                                   decayed[:, 3 * d + 1, col(c)], decayed[:, 3 * d, col(c)])
                    m.then_inc(scores_ready, 1)
                    for d in range(2):
                        for i in range(3):
                            c = i if d == 0 else 3 - i
                            j = 3 * d + i
                            m = mm(added(j),
                                   ke_tok[chunk(c), (d * 4 + h) * 2 + c // 2, :],
                                   gla_v[chunk(c), c // 2, h * TOK:(h + 1) * TOK])
                    m.then_inc(logits_ready, 1)
                    plain(Unit(f"{b}.r", 2 * h))
                    pe.wait_ge(state_ready, h + 1)
                    for t in range(TT):
                        for v in range(2):
                            o = bank[4][:, v * TOK + t * P:v * TOK + (t + 1) * P]
                            cols = slice(v * P, (v + 1) * P)
                            mm(o, gla_v[:, t, h * TOK + v * P:h * TOK + (v + 1) * P], gla_s[:, t, :], stop=False)
                            for c in (2 * t, 2 * t + 1):
                                o = bank[4][:, v * TOK + c * CHUNK:v * TOK + (c + 1) * CHUNK]
                                if c > 0:
                                    m = mm(o, gla_state[:, c - 1, cols], decayed[:, 0, col(c)], start=False)
                                if c < 3:
                                    m = mm(o, gla_state[:, 3 + 2 - c, cols], decayed[:, 3, col(c)], start=False)
                    m.then_inc(head_out, 1)
                    plain(Unit(f"{b}.r", 2 * h + 1))
                r, sq0 = CHAINS[f"{b}.heads"]
                at_least(pe, var_ready, r)
                pe.wait_ge(sq_ready, sq0 + KT)
                for h in range(4):
                    for v in range(2):
                        for t in range(TT):
                            m = mm(bank[7][:, 2 * h + t:2 * h + t + 1], squares[:, 2 * h + v, t * P:(t + 1) * P],
                                   C("ones", n=1), start=v == 0 and t == 0, stop=v == 1)
                m.then_inc(sums_ready, 1)
                head_broadcast(f"{b}.heads")
                operand(f"{b}.y")
                over_units(pe, f"{b}.out", plain)

            pe.wait_ge(con2_in, 32)
            for i in range(4):
                b = f"b{i}"
                norm(f"{b}.n0")
                operand(f"{b}.n0")
                (retention, conformer, gla)[i % 3](b)
                pe.wait_ge(evicted, FIRST[f"{b}.up"])
                post(f"{b}.n1")
                norm(f"{b}.n2")
                operand(f"{b}.n2")
                up(b)
                down(b)
                pe.wait_ge(evicted, FIRST[f"{b}.down"] + 32)
                post(f"{b}.n3")

        @block.scalar
        def _(act):
            def split_hi(u, lead=LEAD, pair=False):
                if isinstance(u.e, int) and u.s + lead >= TOTAL:
                    return
                s = u.s + lead
                at_least(act, raw_in[u.raw(lead)], 16 * (s // RAW + 1), 2 * u.e)
                both = 1 if pair and u.j % 2 == 1 else 0
                at_least(act, unit_done, s - SPLIT + 1 + both, u.e)
                act.activation(w_hi[:, u.split(lead), :], w_raw[:, u.raw(lead), :], ACT.Copy
                               ).then_inc(hi_ready, 1)

            def copy_out(u, out, func=ACT.Copy, scale=1.0):
                at_least(act, unit_done, u.s + 1, u.e)
                act.activation(out, bank[u.bank][:, 0:TOK], func, scale=scale).then_inc(evicted, 1)

            def square(name, k, ap):
                r, _ = CHAINS[name]
                if k == 0:
                    at_least(act, sums_ready, r)
                act.activation(squares[:, k, :], ap, ACT.Square).then_inc(sq_ready, 1)

            def norm(name, which, who, ready, before):
                for k in range(KT):
                    ready(act, k)
                    square(name, k, resid[who][:, k, :])
                f = FILLS[name]
                c = 0 if who == "x" else 1
                act.wait_ge(unit_done, before)
                at_least(act, h_lo_ready, KT * f)
                for k in range(KT):
                    act.wait_ge(norm_ready, KT * NORMS[name] + k + 1)
                    shift = mod[:, which * 3 * KT + k, c:c + 1]
                    gain = mod_gain[:, 2 * which + c, k:k + 1]
                    act.activation(full[:, k, :], scaled[:, k, :], ACT.Identity, bias=shift, scale=gain
                                   ).then_inc(full_ready, 1)
                    act.activation(h_hi[:, k, :], scaled[:, k, :], ACT.Identity, bias=shift, scale=gain
                                   ).then_inc(h_hi_ready, 1)

            def small(w):
                n = PASSES[w]
                outs = {0: z_k, 1: z_v.rearrange("p t n -> p (t n)"), 6: z_four[:, 0, :], 7: z_four[:, 1, :]}
                if w == "ctx0":
                    outs[1] = ctx_v.rearrange("p t n -> p (t n)")
                outs |= {2 + j: z_q[:, j, :] for j in range(4)} | {8 + j: z_conv[:, j, :] for j in range(6)}
                for j in range(14):
                    u = Unit(f"{w}.small", j)
                    split_hi(u)
                    copy_out(u, outs[j])
                    if j == 5:
                        act.wait_ge(evicted, u.s + 1)
                        for i in range(5):
                            square(f"{w}.qk", i, z_k if i == 0 else z_q[:, i - 1, :])
                    if j == 9:
                        act.wait_ge(four_ready, n + 1)
                        act.activation(four_mid[:, 0:2, :].rearrange("p a n -> p (a n)"), bank[4][:, :], ACT.Copy)
                        act.activation(four_mid[:, 2:4, :].rearrange("p a n -> p (a n)"), bank[5][:, :], ACT.Copy
                                       ).then_inc(four_mid_ready, 1)
                    if j == 12:
                        act.wait_ge(four_out, n + 1)
                        act.activation(y_hi[:, 2:4, :].rearrange("p a n -> p (a n)"), bank[7][:, :], ACT.Copy
                                       ).then_inc(four_hi, 1)
                for j in range(2):
                    act.wait_ge(y_full_ready, 2 * n + j + 1)
                    act.activation(y_hi[:, j, :], full[:, j, :], ACT.Copy).then_inc(conv_hi, 1)

            def attention(w):
                n = PASSES[w]
                keys = 2 if w == "ctx0" else 4
                for a in range(HEADS):
                    g = HEADS * n + a
                    units = [Unit(f"{w}.gates", 3 * a + i) for i in range(3)]

                    def gate(u):
                        copy_out(u, gates[:, u.j, :], ACT.Tanh, 0.5)
                    split_hi(units[0])
                    for t in range(TT):
                        act.wait_ge(max_ready, 2 * g + t + 1)
                        act.activation(prob[:, t, 0:keys * P], bank[4 + t][:, 0:keys * P], ACT.Exp,
                                       bias=neg_max[:, t:t + 1], scale=HD ** -0.5,
                                       accum_out=row_sum[:, t:t + 1]).then_inc(exp_ready, 1)
                    gate(units[0])
                    split_hi(units[1])
                    gate(units[1])
                    split_hi(units[2])
                    act.wait_ge(pt_ready, g + 1)
                    act.activation(prob_t[:, 0:2, :].rearrange("p a n -> p (a n)"), bank[6][:, :], ACT.Copy
                                   ).then_inc(pt_act, 1)
                    gate(units[2])
                    rows = slice((a % 2) * HD, (a % 2) * HD + HD)
                    act.wait_ge(o_ready, g + 1)
                    act.activation(y_hi[rows, 4 + a // 2, :], bank[4][rows, 0:TOK], ACT.Copy).then_inc(o_hi, 1)

            def merge(w):
                f = FILLS[f"{w}.m"]

                def body(u):
                    split_hi(u)
                    high(u.j - 1)

                def high(m):
                    if m >= 0:
                        act.wait_ge(merged, KT * PASSES[w] + m + 1)
                        act.activation(h_hi[:, m, :], sums[:, 2 + m % 2, :], ACT.Copy, scale=0.5
                                       ).then_inc(h_hi_ready, 1)
                over_units(act, f"{w}.outs", body)
                high(KT - 1)

            def up(w):
                f = FFNS[w]

                def body(u):
                    split_hi(u)
                    at_least(act, hid_ready, 32 * f + u.j - 3, u.e)
                    copy_out(u, relu[:, u.j % 4, :], ACT.Relu)
                    at_least(act, evicted, u.s + 1, u.e)
                    act.activation(hidden_hi[:, bass.ds(u.index * TOK, TOK)], relu[:, u.j % 4, :],
                                   ACT.Square).then_inc(hid_hi_ready, 1)
                over_units(act, f"{w}.up", body, peel=f == 0)

            act.wait_ge(consts_in, 16 * 4)
            act.activation(cond_sig[:, :], V("c", n=2 * KT), ACT.Sigmoid).then_inc(cond_sig_ready, 1)
            for j in range(LEAD):
                split_hi(Unit("mod0", j), 0)
            act.wait_ge(cond_full_ready, 1)
            act.activation(cond_parts[:, :, 0:2], cond_full.rearrange("p (k c) -> p k c", c=2), ACT.Copy
                           ).then_inc(cond_hi_ready, 1)
            for l in range(DEPTH):
                def mod_rows_out(u):
                    if u.j % 2 == 1:
                        at_least(act, unit_done, u.s + 1, u.e)
                        act.activation(mod_rows, bank[u.bank][0:4, 0:2 * P], ACT.Copy).then_inc(evicted, 2)
                    split_hi(u, pair=True)
                over_units(act, f"mod{l}", mod_rows_out)
                act.wait_ge(mod_ready, 6 * l + 6)
                for who in ("ctx", "x"):
                    w = f"{who}{l}"
                    norm(f"{w}.norm1", 0, who, lambda e, k: None, FIRST[f"{w}.kv" if w == "ctx1" else f"{w}.small"])
                    if w == "ctx1":
                        for j, out in ((0, z_k), (1, ctx_v.rearrange("p t n -> p (t n)"))):
                            u = Unit("ctx1.kv", j)
                            split_hi(u)
                            copy_out(u, out)
                        act.wait_ge(evicted, u.s + 1)
                        square("ctx1.qk", 0, z_k)
                        continue
                    small(w)
                    attention(w)
                    merge(w)
                    over_units(act, f"{w}.wo", split_hi)
                    first = FIRST[f"{w}.wo"]
                    norm(f"{w}.norm2", 1, who, lambda e, k: e.wait_ge(evicted, first + k + 1), FIRST[f"{w}.up"])
                    up(w)
                    over_units(act, f"{w}.down", split_hi)

            copies = [0]

            def norm2(name, ready, before, source=None):
                for k in range(KT):
                    ready(k)
                    square(name, k, resid["x"][:, k, :])
                high(name, before)

            def high(name, before):
                f, n = FILLS[name], NORMS[name]
                act.wait_ge(unit_done, before)
                for k in range(KT):
                    act.wait_ge(full_ready, KT * n + k + 1)
                    act.activation(h_hi[:, k, :], full[:, k, :], ACT.Copy).then_inc(h_hi_ready, 1)

            def product_out(stage, group, bias=None):
                flat = scratch.rearrange("p k n -> p (k n)")
                r, _ = CHAINS[stage.split(".")[0] + (".n1" if "out" in stage else ".n3")]
                before = CHAIN_READS[stage]
                act.wait_ge(sums_ready, before)
                act.wait_ge(bcast_ready, before)
                base = COPIES[stage]

                def body(u):
                    split_hi(u)
                    if u.j % group != group - 1:
                        return
                    at_least(act, unit_done, u.s + 1, u.e)
                    src = bank[u.bank if group == 1 else 4 + (u.j // group) % 2][:, 0:TOK]
                    m = (u.j // group) * TOK + u.e * (TOK // group)
                    b = bias(u.j) if bias else 0.0
                    act.activation(flat[:, bass.ds(m + KT * TOK, TOK)], src, ACT.Identity, bias=b
                                   ).then_inc(copied, 1)
                    act.activation(flat[:, bass.ds(m, TOK)], src, ACT.Square, bias=b).then_inc(evicted, group)
                over_units(act, stage, body)

            def tanh_gate(u, n):
                at_least(act, gate_ready, n - 3)
                act.wait_ge(unit_done, u.s + 1)
                act.activation(relu[:, n % 4, :], bank[u.bank][:, 0:TOK], ACT.Tanh, scale=0.5
                               ).then_inc(tanh_ready, 1)

            def retention(b):
                n = RETS[b]
                if b == "b0":
                    act.wait_ge(angle_ready, 2)
                    for i, name in enumerate(("pos_cos", "pos_sin")):
                        act.activation(C(name, n=TOK), scaled[:, 6 + i, :], ACT.Sin).then_inc(sin_ready, 1)

                def raw(u):
                    split_hi(u)
                    copy_out(u, ret_raw[:, bass.ds(u.index * TOK, TOK)])
                over_units(act, f"{b}.qk", raw)
                if b == "b0":
                    act.activation(log_tmp[:, 0:16], V("decay", n=16), ACT.Abs).then_inc(gla_act, 1)
                    act.wait_ge(gla_act, 1)
                    act.activation(log_tmp[:, 16:32], log_tmp[:, 0:16], ACT.Exp, scale=-1.0).then_inc(gla_act, 1)

                def value(u):
                    split_hi(u, pair=True)
                    at_least(act, unit_done, u.s + 1, u.e)
                    at = (u.j - u.j % 2) * P + u.e * P
                    act.activation(ret_v[:, u.j % 2, bass.ds(at, 2 * P)], bank[u.bank][:, 0:2 * P], ACT.Copy
                                   ).then_inc(evicted, 1)
                over_units(act, f"{b}.v", value)
                for h in range(4):
                    g = 4 * n + h
                    us = [Unit(f"{b}.g", 4 * h + i) for i in range(4)]
                    split_hi(us[0])
                    act.wait_ge(decay_arg, g + 1)
                    act.activation(decay_m[:, h % 2, :], decay_m[:, h % 2, :], ACT.Exp).then_inc(decay_ready, 1)
                    tanh_gate(us[0], GATES[b] + 4 * h)
                    split_hi(us[1])
                    tanh_gate(us[1], GATES[b] + 4 * h + 1)
                    split_hi(us[2])
                    act.wait_ge(head_out, g + 1 + (4 if n else 0))
                    at_least(act, head_summed, g - 1)
                    for i in range(2):
                        cols = slice((4 * h + 2 * i) * TOK, (4 * h + 2 * i + 2) * TOK)
                        act.activation(ret_o[:, cols], bank[5 + i][:, :], ACT.Copy).then_inc(head_copied, 1)
                        k = 4 * (h % 2) + 2 * i
                        act.activation(squares[:, k:k + 2, :].rearrange("p a n -> p (a n)"), bank[5 + i][:, :],
                                       ACT.Square).then_inc(sq_ready, 2)
                    tanh_gate(us[2], GATES[b] + 4 * h + 2)
                    split_hi(us[3])
                    tanh_gate(us[3], GATES[b] + 4 * h + 3)
                for k in range(16):
                    act.wait_ge(gated_full, 16 * n + k + 1)
                    act.activation(ret_hi[:, k * TOK:(k + 1) * TOK], full_ring(k), ACT.Copy
                                   ).then_inc(ret_hi_ready, 1)
                product_out(f"{b}.out", 2)

            def conformer(b):
                def body(u):
                    split_hi(u)
                    at_least(act, unit_done, u.s + 1, u.e)
                    half, pair = u.j % 2, u.j // 2
                    bias = vec[:, bass.ds(u.turn * 4 + VEC["b_in"] + half * KT + pair, 1)]
                    if half == 0:
                        at_least(act, glu_ready, pair - 1, u.turn * 4)
                        act.activation(relu[:, pair % 2, :], bank[u.bank][:, 0:TOK], ACT.Identity, bias=bias
                                       ).then_inc(evicted, 1)
                    else:
                        act.activation(relu[:, 2 + pair % 2, :], bank[u.bank][:, 0:TOK], ACT.Sigmoid, bias=bias
                                       ).then_inc(evicted, 1)
                over_units(act, f"{b}.glu", body, peel=True)
                r, _ = CHAINS[f"{b}.var"]
                for k in range(KT):
                    act.wait_ge(centred, k + 2)
                    square(f"{b}.var", k, dw[:, k, :])
                n = NORMS[f"{b}.y"]
                act.wait_ge(unit_done, FIRST[f"{b}.out"])
                for k in range(KT):
                    act.wait_ge(ln_scaled, k + 1)
                    gain, bias = V("ln_gain", k), V("ln_bias", k)
                    act.activation(squares[:, k, :], scaled[:, k, :], ACT.Identity, bias=bias, scale=gain)
                    act.activation(glu[:, k, 0:TOK], scaled[:, k, :], ACT.Sigmoid, bias=bias, scale=gain
                                   ).then_inc(silu_in, 1)
                high(f"{b}.y", FIRST[f"{b}.out"])
                product_out(f"{b}.out", 1, lambda j: V("b_out", j))

            def gla(b):
                for d in range(2):
                    u = Unit(f"{b}.gate", d)
                    split_hi(u)
                    act.wait_ge(unit_done, u.s + 1)
                    rows = slice(32 * d, 32 * d + 32)
                    act.activation(gla_low[rows, :], bank[u.bank][rows, 0:TOK], ACT.Copy).then_inc(evicted, 1)
                act.wait_ge(evicted, u.s + 1)
                act.activation(row_sum[:, 0:1], row_sum[:, 1:2], ACT.Copy).then_inc(low_ready, 1)
                for j in range(8):
                    u = Unit(f"{b}.qk", j)
                    split_hi(u)
                    if j == 2:
                        act.wait_ge(gla_dve, 1)
                        act.activation(cum_g, log_g, ACT.Abs).then_inc(gla_act, 1)
                        act.wait_ge(gla_act, 3)
                        act.activation(cum_g, cum_g, ACT.Exp, scale=-1.0).then_inc(gla_act, 1)
                        act.wait_ge(gla_act, 4)
                        act.activation(cum_g, cum_g, ACT.Ln, bias=1.0).then_inc(gla_act, 1)
                    out = (gla_q if j < 4 else gla_k)[:, (j % 4) * TOK:(j % 4 + 1) * TOK]
                    copy_out(u, out, scale=P ** -0.5 if j < 4 else 1.0)
                for j in range(8):
                    u = Unit(f"{b}.v", j)
                    split_hi(u, pair=True)
                    if j in (1, 4):
                        d = 0 if j == 1 else 1
                        act.wait_ge(gla_dve, 3 + d)
                        a, e = GLA_ARG[d]
                        for i, (arg, sign) in enumerate(((a, 1.0), (a, -1.0), (e, 1.0))):
                            act.activation(decayed[:, 3 * d + i, :], arg, ACT.Exp, scale=sign / 16.0
                                           ).then_inc(gla_act, 1)
                    if j == 4:
                        ends = cum_g.rearrange("p (c n) -> p c n", n=CHUNK)[:, :, CHUNK - 1]
                        act.activation(decay_end[:, :], ends, ACT.Exp, scale=1.0 / 16.0).then_inc(gla_act, 1)
                    act.wait_ge(unit_done, u.s + 1)
                    act.activation(gla_v[:, j % 2, (j - j % 2) * P:(j - j % 2 + 2) * P], bank[u.bank][:, 0:2 * P],
                                   ACT.Copy).then_inc(evicted, 1)
                act.wait_ge(ke_out, 1)
                for i in range(4):
                    m = act.activation(ke_tok[:, 4 * i:4 * i + 4, :].rearrange("p a n -> p (a n)"),
                                       bank[4 + i][:, :], ACT.Copy)
                m.then_inc(state_in, 1)
                for h in range(4):
                    us = [Unit(f"{b}.r", 2 * h + i) for i in range(2)]
                    split_hi(us[0])
                    tanh_gate(us[0], GATES[b] + 2 * h)
                    split_hi(us[1])
                    act.wait_ge(head_out, 4 + h + 1)
                    act.activation(full[:, 2 * h:2 * h + 2, :].rearrange("p a n -> p (a n)"), bank[4][:, :], ACT.Copy
                                   ).then_inc(gla_o, 1)
                    act.activation(squares[:, 2 * h:2 * h + 2, :].rearrange("p a n -> p (a n)"), bank[4][:, :],
                                   ACT.Square).then_inc(sq_ready, 2)
                    act.wait_ge(sq_ready, CHAINS[f"{b}.heads"][1] + 2 * h + 2)
                    act.activation(row_sum[:, 0:1], row_sum[:, 1:2], ACT.Copy).then_inc(gla_o, 1)
                    tanh_gate(us[1], GATES[b] + 2 * h + 1)
                high(f"{b}.y", FIRST[f"{b}.out"])
                product_out(f"{b}.out", 1)

            act.wait_ge(con2_in, 32)
            for i in range(4):
                b = f"b{i}"
                if i == 0:
                    norm2(f"{b}.n0", lambda k: act.wait_ge(evicted, FIRST["x1.down"] + 4 * (k + 1)), FIRST["b0.qk"])
                else:
                    norm2(f"{b}.n0", lambda k: act.wait_ge(updated, KT * (2 * i - 1) + k + 1), FIRST[f"{b}.{FIRST_PART[i % 3]}"])
                (retention, conformer, gla)[i % 3](b)
                norm2(f"{b}.n2", lambda k: act.wait_ge(updated, KT * 2 * i + k + 1), FIRST[f"{b}.up"])
                up(b)
                product_out(f"{b}.down", 4)

        @block.vector
        def _(dve):
            chained = [0]

            def link(ins):
                chained[0] += 1
                ins.then_inc(dve_chain, 1)
                dve.wait_ge(dve_chain, chained[0])

            def split_lo(u, lead=LEAD):
                if isinstance(u.e, int) and u.s + lead >= TOTAL:
                    return
                at_least(dve, hi_ready, u.s + lead + 1, u.e)
                w = u.split(lead)
                dve.tensor_tensor(w_lo[:, w, :], w_raw[:, u.raw(lead), :], w_hi[:, w, :].bitcast(F32),
                                  ALU.subtract).then_inc(lo_ready, 1)

            def mean_squares(name, cols, scale):
                r, _ = CHAINS[name]
                dve.wait_ge(sums_ready, r + 1)
                dve.tensor_scalar(variance[:, 0:cols], bank[7][:, 0:cols], scale, EPS, ALU.mult, ALU.add
                                  ).then_inc(var_ready, 1)

            def widen(name, n, heads=1):
                r, _ = CHAINS[name]
                dve.wait_ge(rms_ready, r + 1)
                at_least(dve, bcast_ready, r)
                for j in range(n):
                    src = inv_rms[:, j * heads:(j + 1) * heads].unsqueeze(2).broadcast_to([P, heads, P // heads])
                    w = dve.tensor_copy(spread[:, j, :].rearrange("p (h n) -> p h n", h=heads), src)
                w.then_inc(spread_ready, 1)

            def norm(name, who):
                mean_squares(name, TT, 1.0 / D)
                widen(name, TT)
                r, _ = CHAINS[name]
                n, f = NORMS[name], FILLS[name]
                dve.wait_ge(bcast_ready, r + 1)
                at_least(dve, h_hi_ready, KT * f)
                for k in range(KT):
                    dve.tensor_tensor(scaled[:, k, :], bank[6][:, 0:TOK], resid[who][:, k, :], ALU.mult
                                      ).then_inc(norm_ready, 1)
                for k in range(KT):
                    dve.wait_ge(full_ready, KT * n + k + 1)
                    dve.wait_ge(h_hi_ready, KT * f + k + 1)
                    dve.tensor_tensor(h_lo[:, k, :], full[:, k, :], h_hi[:, k, :].bitcast(F32), ALU.subtract
                                      ).then_inc(h_lo_ready, 1)

            def qk_normed(w, n_tiles, out):
                r, _ = CHAINS[f"{w}.qk"]
                l = w[-1]
                dve.wait_ge(bcast_ready, r + 1)
                for i in range(n_tiles):
                    b = bank[4 + i // 2][:, (i % 2) * TOK:(i % 2 + 1) * TOK]
                    src = z_k if i == 0 else z_q[:, i - 1, :]
                    q = dve.scalar_tensor_tensor(out=out(i), in0=src, scalar=V(f"g_k{l}" if i == 0 else f"g_q{l}"),
                                                 in1=b, op0=ALU.mult, op1=ALU.mult)
                    q.then_inc(qk_norm_ready, 1)

            def small(w):
                n = PASSES[w]
                l = w[-1]
                for j in range(14):
                    split_lo(Unit(f"{w}.small", j))
                    if j == 7:
                        mean_squares(f"{w}.qk", 20, 1.0 / HD)
                    if j == 8:
                        widen(f"{w}.qk", 10, heads=2)
                    if j == 9:
                        if w == "ctx0":
                            qk_normed(w, 5, lambda i: ctx_k[:, :] if i == 0 else qk[:, i, :])
                        else:
                            qk_normed(w, 5, lambda i: qk_n[:, i, :])
                    if j == 11 and w != "ctx0":
                        dve.wait_ge(rot_ready, n)
                        for i in range(5):
                            b = bank[4 + i // 2][:, (i % 2) * TOK:(i % 2 + 1) * TOK]
                            m = dve.tensor_tensor(scaled[:, i, :], b, C("rope_sin", n=TOK), ALU.mult)
                        link(m)
                        dve.wait_ge(rope_part, 5 * n)
                        for i in range(5):
                            q = dve.tensor_tensor(qk[:, i, :], scaled[:, i, :], full[:, i, :], ALU.add)
                        q.then_inc(qk_ready, 1)
                    if j == 11 and w == "ctx0":
                        dve.wait_ge(qk_norm_ready, 5)
                        dve.tensor_copy(row_max[:, 0:1], V("c")).then_inc(qk_ready, 1)
                dve.wait_ge(four_hi, n + 1)
                for f in range(2):
                    dve.tensor_tensor(y_lo[:, 2 + f, :], bank[7][:, f * TOK:(f + 1) * TOK],
                                      y_hi[:, 2 + f, :].bitcast(F32), ALU.subtract).then_inc(y_ready, 1)
                dve.wait_ge(evicted, FIRST[f"{w}.small"] + 14)
                if w != "ctx0":
                    dve.wait_ge(rope_part, 5 * n)
                    dve.wait_ge(qk_ready, n + 1)
                link(dve.memset(conv_in[:, :, 0:1], 0.0))
                link(dve.memset(conv_in[:, :, TOK + 1:TOK + 2], 0.0))
                link(dve.tensor_tensor(conv_in[:, :, 1:TOK + 1], z_conv[:, 2:4, :], z_conv[:, 4:6, :], ALU.mult))
                for j in range(3):
                    for f in range(2):
                        tap = conv_in[:, f, j:j + TOK]
                        wt = V(f"w_conv{l}", 2 * j + f)
                        if j == 0:
                            m = dve.tensor_scalar(scaled[:, f, :], tap, wt, None, ALU.mult)
                        else:
                            m = dve.scalar_tensor_tensor(out=scaled[:, f, :], in0=tap, scalar=wt,
                                                         in1=scaled[:, f, :], op0=ALU.mult, op1=ALU.add)
                    link(m)
                for f in range(2):
                    dve.tensor_tensor(full[:, f, :], scaled[:, f, :], z_conv[:, f, :], ALU.mult
                                      ).then_inc(y_full_ready, 1)
                for f in range(2):
                    dve.wait_ge(conv_hi, 2 * n + f + 1)
                    dve.tensor_tensor(y_lo[:, f, :], full[:, f, :], y_hi[:, f, :].bitcast(F32), ALU.subtract
                                      ).then_inc(y_ready, 1)

            def attention(w):
                n = PASSES[w]
                keys = 2 if w == "ctx0" else 4
                for a in range(HEADS):
                    g = HEADS * n + a
                    units = [Unit(f"{w}.gates", 3 * a + i) for i in range(3)]
                    for t in range(TT):
                        dve.wait_ge(s_ready, 2 * g + t + 1)
                        link(dve.tensor_reduce(row_max[:, t:t + 1], bank[4 + t][:, 0:keys * P], AX_X, ALU.max))
                        dve.tensor_scalar(neg_max[:, t:t + 1], row_max[:, t:t + 1], -(HD ** -0.5), None, ALU.mult
                                          ).then_inc(max_ready, 1)
                    split_lo(units[0])
                    for t in range(TT):
                        dve.wait_ge(exp_ready, 2 * g + t + 1)
                        link(dve.reciprocal(inv_sum[:, t:t + 1], row_sum[:, t:t + 1]))
                        dve.tensor_scalar(prob[:, t, 0:keys * P], prob[:, t, 0:keys * P], inv_sum[:, t:t + 1],
                                          None, ALU.mult).then_inc(p_ready, 1)
                    split_lo(units[1])
                    dve.wait_ge(pt_ready, g + 1)
                    if keys == 4:
                        dve.tensor_copy(prob_t[:, 2:4, :].rearrange("p a n -> p (a n)"), bank[7][:, :]
                                        ).then_inc(pt_dve, 1)
                    else:
                        dve.tensor_copy(row_max[:, 0:1], row_max[:, 1:2]).then_inc(pt_dve, 1)
                    split_lo(units[2])
                    rows = slice((a % 2) * HD, (a % 2) * HD + HD)
                    dve.wait_ge(o_hi, g + 1)
                    dve.tensor_tensor(y_lo[rows, 4 + a // 2, :], bank[4][rows, 0:TOK],
                                      y_hi[rows, 4 + a // 2, :].bitcast(F32), ALU.subtract).then_inc(o_lo, 1)

            def merge(w):
                n = PASSES[w]

                def body(u):
                    split_lo(u)
                    at_least(dve, unit_done, u.s + 1, u.e)
                    m = u.j
                    b = bank[u.bank]
                    at_least(dve, merged, KT * n + m - 1)
                    for i, p in enumerate((b[:, 0:TOK], b[:, TOK:2 * TOK], bank[4 + u.s % 2][:, 0:TOK])):
                        t = dve.scalar_tensor_tensor(out=terms[:, m % 2, i, :], in0=gates[:, i * KT + m, :],
                                                     scalar=1.0, in1=p, op0=ALU.add, op1=ALU.mult)
                    t.then_inc(evicted, 1)
                    low(m - 1)

                def low(m):
                    if m >= 0:
                        dve.wait_ge(h_hi_ready, KT * FILLS[f"{w}.m"] + m + 1)
                        dve.scalar_tensor_tensor(out=h_lo[:, m, :], in0=sums[:, 2 + m % 2, :], scalar=0.5,
                                                 in1=h_hi[:, m, :].bitcast(F32), op0=ALU.mult, op1=ALU.subtract
                                                 ).then_inc(h_lo_ready, 1)
                over_units(dve, f"{w}.outs", body)
                low(KT - 1)

            def add_gated(w, who, l):
                c = 0 if who == "x" else 1

                def body(u):
                    split_lo(u)
                    at_least(dve, unit_done, u.s + 1, u.e)
                    r = resid[who][:, u.j, :]
                    dve.scalar_tensor_tensor(out=r, in0=bank[u.bank][:, 0:TOK], scalar=mod[:, 2 * KT + u.j, c:c + 1],
                                             in1=r, op0=ALU.mult, op1=ALU.add).then_inc(evicted, 1)
                over_units(dve, f"{w}.wo", body)

            def up(w):
                f = FFNS[w]

                def body(u):
                    split_lo(u)
                    at_least(dve, evicted, u.s + 1, u.e)
                    dve.tensor_tensor(relu_sq[:, u.j % 2, :], relu[:, u.j % 4, :], relu[:, u.j % 4, :], ALU.mult
                                      ).then_inc(hid_sq_ready, 1)
                    at_least(dve, hid_sq_ready, 32 * f + u.j + 1, u.e)
                    at_least(dve, hid_hi_ready, 32 * f + u.j + 1, u.e)
                    cols = bass.ds(u.index * TOK, TOK)
                    dve.tensor_tensor(hidden_lo[:, cols], relu_sq[:, u.j % 2, :], hidden_hi[:, cols].bitcast(F32),
                                      ALU.subtract).then_inc(hid_ready, 1)
                over_units(dve, f"{w}.up", body)

            def down(w, who):
                c = 0 if who == "x" else 1
                flat = resid[who].rearrange("p k n -> p (k n)")
                mflat = mod.rearrange("p m c -> p (m c)")

                def body(u):
                    split_lo(u)
                    if u.j % 4 != 3:
                        return
                    at_least(dve, unit_done, u.s + 1, u.e)
                    m4 = u.e + (u.j // 4) * 4
                    r = flat[:, bass.ds(m4 * (TOK // 4), TOK)]
                    if isinstance(u.e, int):
                        m = m4 // 4
                        g = mflat[:, (5 * KT + m) * 2 + c:(5 * KT + m) * 2 + c + 1]
                    else:
                        g = mflat[:, bass.ds(u.turn * 4 + (5 * KT + u.j // 4) * 2 + c, 1)]
                    dve.scalar_tensor_tensor(out=r, in0=bank[4 + (u.j // 4) % 2][:, 0:TOK], scalar=g,
                                             in1=r, op0=ALU.mult, op1=ALU.add).then_inc(evicted, 4)
                over_units(dve, f"{w}.down", body)

            dve.wait_ge(consts_in, 16 * 4)
            dve.wait_ge(cond_sig_ready, 1)
            dve.tensor_tensor(cond_full[:, :], cond_sig[:, :], V("c", n=2 * KT), ALU.mult).then_inc(cond_full_ready, 1)
            dve.wait_ge(cond_hi_ready, 1)
            dve.tensor_tensor(cond_parts[:, :, 2:4], cond_full.rearrange("p (k c) -> p k c", c=2),
                              cond_parts[:, :, 0:2].bitcast(F32), ALU.subtract).then_inc(cond_ready, 1)
            for j in range(LEAD):
                split_lo(Unit("mod0", j), 0)
            for l in range(DEPTH):
                def mod_out(u):
                    split_lo(u)
                    if u.j % 2 == 0:
                        return
                    pair = l * NM // 2 + u.j // 2
                    at_least(dve, mod_cols_ready, pair + 1, u.turn * 4)
                    dve.tensor_copy(mod_raw[:, bass.ds((u.index - 1) * 2, 4)], bank[4 + pair % 2][:, 0:4]
                                    ).then_inc(mod_cols_out, 1)
                over_units(dve, f"mod{l}", mod_out)
                dve.wait_ge(mod_cols_out, (l + 1) * NM // 2)
                raw = tiles(mod_raw[:, :], NM)
                for c in range(2):
                    dve.tensor_tensor(mod[:, :, c], raw[:, :, c], V(f"b_mod{l}", n=NM), ALU.add
                                      ).then_inc(mod_ready, 1)
                dve.wait_ge(mod_ready, 6 * l + 2)
                for which in range(2):
                    for c in range(2):
                        dve.scalar_tensor_tensor(out=mod_gain[:, 2 * which + c, :],
                                                 in0=mod[:, (which * 3 + 1) * KT:(which * 3 + 2) * KT, c],
                                                 scalar=1.0, in1=V(f"g{which + 1}_{l}", n=KT), op0=ALU.add,
                                                 op1=ALU.mult).then_inc(mod_ready, 1)
                for who in ("ctx", "x"):
                    w = f"{who}{l}"
                    norm(f"{w}.norm1", who)
                    if w == "ctx1":
                        for j in range(2):
                            split_lo(Unit("ctx1.kv", j))
                        mean_squares("ctx1.qk", 4, 1.0 / HD)
                        widen("ctx1.qk", 2, heads=2)
                        r, _ = CHAINS["ctx1.qk"]
                        dve.wait_ge(bcast_ready, r + 1)
                        link(dve.scalar_tensor_tensor(out=ctx_k[:, :], in0=z_k, scalar=V("g_k1"),
                                                      in1=bank[4][:, 0:TOK], op0=ALU.mult, op1=ALU.mult))
                        continue
                    small(w)
                    attention(w)
                    merge(w)
                    add_gated(w, who, l)
                    norm(f"{w}.norm2", who)
                    up(w)
                    down(w, who)

            def high_low(name):
                f = FILLS[name]
                for k in range(KT):
                    dve.wait_ge(h_hi_ready, KT * f + k + 1)
                    dve.tensor_tensor(h_lo[:, k, :], full[:, k, :], h_hi[:, k, :].bitcast(F32), ALU.subtract
                                      ).then_inc(h_lo_ready, 1)

            def norm2(name, gain):
                mean_squares(name, TT, 1.0 / D)
                widen(name, TT)
                r, _ = CHAINS[name]
                dve.wait_ge(bcast_ready, r + 1)
                dve.wait_ge(h_hi_ready, KT * FILLS[name])
                for k in range(KT):
                    dve.scalar_tensor_tensor(out=full[:, k, :], in0=resid["x"][:, k, :], scalar=V("gains", gain * KT + k),
                                             in1=bank[6][:, 0:TOK], op0=ALU.mult, op1=ALU.mult
                                             ).then_inc(full_ready, 1)
                high_low(name)

            def post(name, gain):
                mean_squares(name, TT, 1.0 / D)
                widen(name, TT)
                r, _ = CHAINS[name]
                dve.wait_ge(bcast_ready, r + 1)
                for k in range(KT):
                    m = dve.scalar_tensor_tensor(out=scaled[:, k, :], in0=scaled[:, k, :],
                                                 scalar=V("gains", gain * KT + k), in1=bank[6][:, 0:TOK],
                                                 op0=ALU.mult, op1=ALU.mult)
                link(m)
                for k in range(KT):
                    x = resid["x"][:, k, :]
                    dve.tensor_tensor(x, x, scaled[:, k, :], ALU.add).then_inc(updated, 1)

            def angles():
                s = lambda i: scaled[:, i, :]
                magic = 1.5 * 2 ** 23
                link(dve.tensor_copy(s(1), s(0).bitcast(I32)))
                link(dve.tensor_scalar(s(2), s(1), V("inv_freq"), None, ALU.mult))
                for i, quarter in ((6, 0.25), (7, 0.0)):
                    link(dve.tensor_scalar(s(3), s(2), 1.0 / (2 * np.pi), quarter, ALU.mult, ALU.add))
                    link(dve.tensor_scalar(s(3), s(3), magic, None, ALU.add))
                    link(dve.tensor_scalar(s(3), s(3), magic, None, ALU.subtract))
                    src = s(2)
                    for part in TWO_PI:
                        link(dve.scalar_tensor_tensor(out=s(i), in0=s(3), scalar=-part, in1=src,
                                                      op0=ALU.mult, op1=ALU.add))
                        src = s(i)
                    link(dve.tensor_scalar(s(i), s(i), quarter * 2 * np.pi, 3.1415925, ALU.add, ALU.min))
                    dve.tensor_scalar(s(i), s(i), -3.1415925, None, ALU.max).then_inc(angle_ready, 1)

            def log_decays():
                dve.wait_ge(gla_act, 2)
                e, s, q, a = (log_tmp[:, 16:32], log_tmp[:, 0:16], log_tmp[:, 32:48], log_decay[:, :])
                link(dve.tensor_scalar(s, e, 2.0, None, ALU.add))
                link(dve.reciprocal(s, s))
                link(dve.tensor_tensor(s, s, e, ALU.mult))
                link(dve.tensor_tensor(q, s, s, ALU.mult))
                link(dve.memset(a, 1.0 / 17))
                for n in range(15, 0, -2):
                    link(dve.tensor_tensor(a, a, q, ALU.mult))
                    link(dve.tensor_scalar(a, a, 1.0 / n, None, ALU.add))
                link(dve.scalar_tensor_tensor(out=a, in0=a, scalar=-2.0, in1=s, op0=ALU.mult, op1=ALU.mult))
                link(dve.tensor_scalar(e, V("decay", n=16), 0.0, None, ALU.min))
                link(dve.tensor_tensor(a, a, e, ALU.add))

            def silu_gate(u, n, out):
                dve.wait_ge(tanh_ready, n + 1)
                dve.scalar_tensor_tensor(out=out, in0=relu[:, n % 4, :], scalar=1.0, in1=bank[u.bank][:, 0:TOK],
                                         op0=ALU.add, op1=ALU.mult).then_inc(evicted, 1)
                dve.wait_ge(evicted, u.s + 1)
                dve.tensor_copy(row_max[:, 0:1], row_max[:, 1:2]).then_inc(gate_ready, 1)

            def retention(b):
                n, j = RETS[b], int(b[1]) // 3
                if b == "b0":
                    angles()
                over_units(dve, f"{b}.qk", split_lo)
                if b == "b0":
                    log_decays()
                if b == "b0":
                    dve.wait_ge(sin_ready, 2)
                dve.wait_ge(evicted, FIRST[f"{b}.v"])

                def value(u):
                    split_lo(u)
                    if u.j % 2 == 0:
                        return
                    pair, at = u.j // 2, (u.j // 2) * 2 * TOK + u.e * TOK
                    t1, t2 = ret_raw[:, bass.ds(at, TOK)], ret_raw[:, bass.ds(at + TOK, TOK)]
                    ring_at = 4 * (pair % 2)
                    at_least(dve, rot_a, 8 * n + pair + 1, u.turn * 4)
                    dve.tensor_tensor(squares[:, ring_at + 2, :], t2, C("pos_sin", n=TOK), ALU.mult)
                    dve.tensor_tensor(squares[:, ring_at + 3, :], t1, C("pos_sin", n=TOK), ALU.mult
                                      ).then_inc(gla_pool, 1)
                    at_least(dve, gla_pool, 8 * n + pair + 1, u.turn * 4)
                    dve.tensor_tensor(ret_rot[:, bass.ds(at, TOK)], squares[:, ring_at, :], squares[:, ring_at + 2, :],
                                      ALU.subtract)
                    dve.tensor_tensor(ret_rot[:, bass.ds(at + TOK, TOK)], squares[:, ring_at + 1, :],
                                      squares[:, ring_at + 3, :], ALU.add).then_inc(rot_done, 1)
                over_units(dve, f"{b}.v", value)
                for h in range(4):
                    g = 4 * n + h
                    us = [Unit(f"{b}.g", 4 * h + i) for i in range(4)]
                    fwd, bwd = (log_decay[:, (2 * j + d) * 4 + h:(2 * j + d) * 4 + h + 1] for d in range(2))
                    link(dve.tensor_scalar(decay_m[:, h % 2, :], C("after", n=TT * TOK), fwd, None, ALU.mult))
                    dve.scalar_tensor_tensor(out=decay_m[:, h % 2, :], in0=C("before", n=TT * TOK), scalar=bwd,
                                             in1=decay_m[:, h % 2, :], op0=ALU.mult, op1=ALU.add
                                             ).then_inc(decay_arg, 1)
                    split_lo(us[0])
                    dve.wait_ge(decay_ready, g + 1)
                    dve.wait_ge(scores_ready, g + 1 + (4 if n else 0))
                    dve.scalar_tensor_tensor(out=scores[:, h % 2, :], in0=bank[4][:, :], scalar=1.0 / 16,
                                             in1=decay_m[:, h % 2, :], op0=ALU.mult, op1=ALU.mult
                                             ).then_inc(weighted, 1)
                    g0 = GATES[b] + 4 * h
                    silu_gate(us[0], g0, scratch[:, 8 + 4 * h, :])
                    for i in range(1, 4):
                        split_lo(us[i])
                        silu_gate(us[i], g0 + i, scratch[:, 8 + 4 * h + i, :])
                mean_squares(f"{b}.heads", 8, 1.0 / 512)
                widen(f"{b}.heads", 8)
                r, _ = CHAINS[f"{b}.heads"]
                dve.wait_ge(bcast_ready, r + 1)
                for i in range(2):
                    m = dve.tensor_copy(ring[:, i * 512:(i + 1) * 512], bank[4 + i][:, :])
                m.then_inc(heads_wide, 1)
                dve.wait_ge(heads_wide, n + 1)
                for k in range(16):
                    dve.wait_ge(gated, 16 * n + k + 1)
                    at_least(dve, ret_ready, 16 * n + k - 7)
                    dve.scalar_tensor_tensor(out=full_ring(k), in0=scratch[:, 8 + k, :], scalar=0.5,
                                             in1=relu[:, k // 4, :], op0=ALU.mult, op1=ALU.mult
                                             ).then_inc(gated_full, 1)
                    if k > 0:
                        ret_low(n, k - 1)
                ret_low(n, 15)
                over_units(dve, f"{b}.out", split_lo)

            def ret_low(n, k):
                dve.wait_ge(ret_hi_ready, 16 * n + k + 1)
                cols = slice(k * TOK, (k + 1) * TOK)
                dve.tensor_tensor(ret_lo[:, cols], full_ring(k), ret_hi[:, cols].bitcast(F32), ALU.subtract
                                  ).then_inc(ret_ready, 1)

            def conformer(b):
                dve.memset(glu[:, :, 0:15], 0.0).then_inc(pad_ready, 1)
                dve.memset(glu[:, :, TOK + 15:TOK + 30], 0.0).then_inc(pad_ready, 1)
                dve.wait_ge(pad_ready, 2)
                wide = TOK + 30

                def body(u):
                    split_lo(u)
                    if u.j % 2 == 0:
                        return
                    pair = u.j // 2
                    at_least(dve, evicted, u.s + 1, u.e)
                    tile = u.turn * 4 + pair
                    at = u.turn * (4 * wide) + pair * wide
                    dve.tensor_tensor(conv_t[:, bass.ds(at + 15, TOK)], relu[:, pair % 2, :], relu[:, 2 + pair % 2, :],
                                      ALU.mult).then_inc(glu_ready, 1)
                    at_least(dve, glu_ready, pair + 1, u.turn * 4)
                    acc = dw_out[:, bass.ds(u.turn * (4 * TOK) + pair * TOK, TOK)]
                    for t in range(31):
                        w = vec[:, bass.ds(u.turn * (4 * 31) + VEC["w_dw"] + pair * 31 + t, 1)]
                        src = conv_t[:, bass.ds(at + t, TOK)]
                        if t == 0:
                            m = dve.tensor_scalar(acc, src, w, vec[:, bass.ds(u.turn * 4 + VEC["b_dw"] + pair, 1)],
                                                  ALU.mult, ALU.add)
                        else:
                            at_least(dve, tap, pair * 30 + t, u.turn * (4 * 30))
                            m = dve.scalar_tensor_tensor(out=acc, in0=src, scalar=w, in1=acc, op0=ALU.mult, op1=ALU.add)
                        m.then_inc(tap if t < 30 else dw_ready, 1)
                over_units(dve, f"{b}.glu", body)
                r, _ = CHAINS[f"{b}.mean"]
                dve.wait_ge(sums_ready, r + 1)
                dve.tensor_scalar(variance[:, 0:TT], bank[7][:, 0:TT], -1.0 / D, None, ALU.mult).then_inc(var_ready, 1)
                widen(f"{b}.mean", TT)
                dve.wait_ge(bcast_ready, r + 1)
                dve.wait_ge(dw_ready, KT)
                for k in range(KT):
                    dve.tensor_tensor(dw[:, k, :], bank[6][:, 0:TOK], dw[:, k, :], ALU.add).then_inc(centred, 1)
                dve.tensor_copy(row_max[:, 0:1], row_max[:, 1:2]).then_inc(centred, 1)
                mean_squares(f"{b}.var", TT, 1.0 / D)
                widen(f"{b}.var", TT)
                dve.wait_ge(bcast_ready, r + 2)
                for k in range(KT):
                    dve.tensor_tensor(scaled[:, k, :], bank[6][:, 0:TOK], dw[:, k, :], ALU.mult).then_inc(ln_scaled, 1)
                for k in range(KT):
                    dve.wait_ge(silu_in, k + 1)
                    dve.tensor_tensor(full[:, k, :], squares[:, k, :], glu[:, k, 0:TOK], ALU.mult).then_inc(full_ready, 1)
                high_low(f"{b}.y")
                over_units(dve, f"{b}.out", split_lo)

            def gla(b):
                for d in range(2):
                    split_lo(Unit(f"{b}.gate", d))
                dve.wait_ge(logits_ready, 1)
                for i in range(8):
                    m = dve.tensor_scalar(log_g[:, i * TOK:(i + 1) * TOK], bank[4 + i // 2][:, (i % 2) * TOK:(i % 2 + 1) * TOK],
                                          V("gate_b", i), None, ALU.add)
                m.then_inc(gla_dve, 1)
                reset = squares.rearrange("p k n -> p (k n)")
                for j in range(8):
                    split_lo(Unit(f"{b}.qk", j))
                    if j == 4:
                        dve.wait_ge(gla_act, 5)
                        link(dve.scalar_tensor_tensor(out=log_g, in0=log_g, scalar=0.0, in1=cum_g, op0=ALU.min,
                                                      op1=ALU.subtract))
                        link(dve.memset(reset, 1.0))
                        link(dve.memset(reset.rearrange("p (c n) -> p c n", n=CHUNK)[:, :, 0:1], 0.0))
                        dve.tensor_tensor_scan(cum_g, reset, log_g, 0.0, ALU.mult, ALU.add).then_inc(gla_dve, 1)
                        dve.wait_ge(gla_dve, 2)
                        c3, l3 = (x.rearrange("p (c n) -> p c n", n=CHUNK) for x in (cum_g, log_g))
                        s3 = reset.rearrange("p (c n) -> p c n", n=CHUNK)
                        rest = lambda d: c3[:, 16 * d:16 * d + 16, CHUNK - 1:CHUNK].broadcast_to([P, 16, CHUNK])
                        dve.tensor_tensor(s3[:, 0:16, :], rest(0), c3[:, 0:16, :], ALU.subtract).then_inc(gla_dve, 1)
                        link(dve.tensor_tensor(s3[:, 16:32, :], rest(1), c3[:, 16:32, :], ALU.subtract))
                        link(dve.tensor_tensor(s3[:, 16:32, :], s3[:, 16:32, :], l3[:, 16:32, :], ALU.add))
                        dve.tensor_tensor(l3[:, 16:32, :], c3[:, 16:32, :], l3[:, 16:32, :], ALU.subtract
                                          ).then_inc(gla_dve, 1)
                dve.wait_ge(evicted, FIRST[f"{b}.v"])
                for j in range(8):
                    split_lo(Unit(f"{b}.v", j))
                    if j in (2, 5):
                        d = 0 if j == 2 else 1
                        dve.wait_ge(gla_act, 5 + 3 * (d + 1))
                        for i, x in ((2, gla_k), (0, gla_q), (1, gla_k)):
                            m = dve.tensor_tensor(decayed[:, 3 * d + i, :], decayed[:, 3 * d + i, :], x, ALU.mult)
                        m.then_inc(ke_ready, 1)
                dve.wait_ge(gla_act, 12)
                link(dve.memset(gla_s, 0.0))
                for h in range(4):
                    us = [Unit(f"{b}.r", 2 * h + i) for i in range(2)]
                    split_lo(us[0])
                    dve.wait_ge(scores_ready, 4 + h + 1)
                    dve.wait_ge(logits_ready, 2 + h)
                    dve.wait_ge(head_out, 4 + h)
                    for d, name in enumerate(("mask_fwd", "mask_bwd")):
                        m = C(name, n=CHUNK).unsqueeze(1).broadcast_to([P, 2, CHUNK])
                        out = sum_ring[:, d, :].rearrange("p (a n) -> p a n", a=2)
                        x = dve.tensor_tensor(out, bank[7][:, d * P:(d + 1) * P].rearrange("p (a n) -> p a n", a=2), m,
                                              ALU.mult)
                    link(x)
                    for i in range(2):
                        rows = slice(i * CHUNK, (i + 1) * CHUNK)
                        f3, b3 = (sum_ring[rows, d, :].rearrange("p (a n) -> p a n", a=2) for d in range(2))
                        x = dve.tensor_tensor(gla_s[rows, :, i * CHUNK:(i + 1) * CHUNK], f3, b3, ALU.add)
                    link(x)
                    for i in range(3):
                        for d in range(2):
                            j3 = 3 * d + i
                            u_ps = added(j3)
                            if i == 0:
                                m = dve.tensor_copy(gla_state[:, j3, :], u_ps)
                            else:
                                c = i if d == 0 else 3 - i
                                at = (4 * d + h) * 4 + c
                                m = dve.scalar_tensor_tensor(out=gla_state[:, j3, :], in0=gla_state[:, j3 - 1, :],
                                                             scalar=decay_end[:, at:at + 1], in1=u_ps, op0=ALU.mult,
                                                             op1=ALU.add)
                        if i < 2:
                            link(m)
                    m.then_inc(state_ready, 1)
                    silu_gate(us[0], GATES[b] + 2 * h, scaled[:, 2 * h, :])
                    split_lo(us[1])
                    silu_gate(us[1], GATES[b] + 2 * h + 1, scaled[:, 2 * h + 1, :])
                mean_squares(f"{b}.heads", 8, 1.0 / 256)
                widen(f"{b}.heads", 8)
                r, _ = CHAINS[f"{b}.heads"]
                dve.wait_ge(bcast_ready, r + 1)
                dve.wait_ge(gla_o, 8)
                for k in range(KT):
                    m = dve.scalar_tensor_tensor(out=full[:, k, :], in0=full[:, k, :], scalar=V("gla_gain", k % 2),
                                                 in1=bank[4 + k // 4][:, (k // 2 % 2) * TOK:(k // 2 % 2 + 1) * TOK],
                                                 op0=ALU.mult, op1=ALU.mult)
                link(m)
                for k in range(KT):
                    dve.scalar_tensor_tensor(out=full[:, k, :], in0=full[:, k, :], scalar=0.5, in1=scaled[:, k, :],
                                             op0=ALU.mult, op1=ALU.mult).then_inc(full_ready, 1)
                high_low(f"{b}.y")
                over_units(dve, f"{b}.out", split_lo)

            dve.wait_ge(con2_in, 32)
            for i in range(4):
                b = f"b{i}"
                norm2(f"{b}.n0", 4 * i)
                (retention, conformer, gla)[i % 3](b)
                post(f"{b}.n1", 4 * i + 1)
                norm2(f"{b}.n2", 4 * i + 2)
                up(b)
                over_units(dve, f"{b}.down", split_lo)
                post(f"{b}.n3", 4 * i + 3)

        @block.gpsimd
        def _(pool):
            steps = [0]

            def power(name, cols):
                r, _ = CHAINS[name]
                pool.wait_ge(var_ready, r + 1)
                pool.tensor_tensor(inv_rms[:, 0:cols], variance[:, 0:cols], neg_half[:, 0:1].broadcast_to([P, cols]),
                                   ALU.pow).then_inc(rms_ready, 1)

            pool.memset(neg_half[:, :], -0.5).then_inc(pool_const, 1)
            pool.wait_ge(pool_const, 1)
            pool.wait_ge(consts_in, 16 * 4)
            for l in range(DEPTH):
                for who in ("ctx", "x"):
                    w = f"{who}{l}"
                    power(f"{w}.norm1", TT)
                    if w == "ctx1":
                        power(f"{w}.qk", 4)
                        continue
                    power(f"{w}.qk", 20)
                    n = PASSES[w]
                    if w != "ctx0":
                        for i in range(5):
                            pool.wait_ge(qk_norm_ready, 5 * n + i + 1)
                            pool.tensor_tensor(full[:, i, :], qk_n[:, i, :], C("rope_cos", n=TOK), ALU.mult
                                               ).then_inc(rope_part, 1)
                    for m in range(KT):
                        pool.wait_ge(evicted, FIRST[f"{w}.outs"] + m + 1)
                        at_least(pool, h_lo_ready, KT * FILLS[f"{w}.m"] + m - 1)
                        pool.tensor_tensor(sums[:, m % 2, :], terms[:, m % 2, 0, :], terms[:, m % 2, 1, :], ALU.add
                                           ).then_inc(merge_step, 1)
                        pool.wait_ge(merge_step, KT * n + m + 1)
                        pool.tensor_tensor(sums[:, 2 + m % 2, :], sums[:, m % 2, :], terms[:, m % 2, 2, :], ALU.add
                                           ).then_inc(merged, 1)
                    power(f"{w}.norm2", TT)
            for i in range(4):
                b = f"b{i}"
                power(f"{b}.n0", TT)
                if i % 3 == 0:
                    n = RETS[b]
                    pool.wait_ge(sin_ready, 2)
                    pool.wait_ge(sums_ready, CHAINS[f"{b}.n0"][0] + 1)
                    pool.wait_ge(evicted, FIRST[f"{b}.v"])
                    for pair in range(8):
                        at_least(pool, rot_done, 8 * n + pair - 1)
                        for t in range(2):
                            m = pool.tensor_tensor(squares[:, 4 * (pair % 2) + t, :],
                                                   ret_raw[:, (2 * pair + t) * TOK:(2 * pair + t + 1) * TOK],
                                                   C("pos_cos", n=TOK), ALU.mult)
                        m.then_inc(rot_a, 1)
                    for k in range(16):
                        pool.wait_ge(evicted, FIRST[f"{b}.g"] + k + 1)
                        pool.wait_ge(head_copied, 8 * n + 2 * (k // 4) + 2)
                        x = scratch[:, 8 + k, :]
                        pool.tensor_tensor(x, x, ret_o[:, k * TOK:(k + 1) * TOK], ALU.mult).then_inc(gated, 1)
                    power(f"{b}.heads", 8)
                elif i % 3 == 1:
                    pool.wait_ge(var_ready, CHAINS[f"{b}.mean"][0] + 1)
                    pool.tensor_copy(inv_rms[:, 0:TT], variance[:, 0:TT]).then_inc(rms_ready, 1)
                    power(f"{b}.var", TT)
                else:
                    power(f"{b}.heads", 8)
                power(f"{b}.n1", TT)
                power(f"{b}.n2", TT)
                power(f"{b}.n3", TT)


def _by_feature(v):
    return np.ascontiguousarray(np.asarray(v).reshape(-1, P).T)


def _units(w):
    g, m = w.shape[0] // D, w.shape[1] // P
    return w.reshape(g, KT, P, m, P).transpose(3, 0, 2, 1, 4).reshape(m * g, P, D)


def _head_order(w, axis):
    shape = w.shape[:axis] + (2, 4, HD) + w.shape[axis + 1:]
    return np.swapaxes(w.reshape(shape), axis, axis + 1).reshape(w.shape)


def pack_stream(a):
    parts = []
    for l in range(DEPTH):
        w = a["w_in"][l]
        conv, four, q, kv, gates = w[:, 0:768], w[:, 768:1024], w[:, 1024:1536], w[:, 1536:1792], w[:, 1792:]
        outs = np.concatenate([a["w_conv_out"][l], a["w_four_out"][l], _head_order(a["w_attn_out"][l], 0)])
        parts += [_units(a["w_mod"][l]), _units(kv), _units(_head_order(q, 1)), _units(four), _units(conv),
                  _units(gates), _units(outs), _units(a["w_o"][l]), _units(a["w_ff1"][l]), _units(a["w_ff2"][l])]
    for i in range(4):
        j = i // 3
        if i % 3 == 0:
            parts += [_units(a["ret_w_in_2"][j]), _units(a["ret_w_out_2"][j])]
        elif i % 3 == 1:
            w = a["conv_w_in_2"][j]
            both = w.reshape(D, 2, KT, P).transpose(0, 2, 1, 3).reshape(D, 2 * D)
            parts += [_units(both), _units(a["conv_w_out_2"][j])]
        else:
            gate = np.zeros((D, 2 * P), np.float32)
            for d in range(2):
                gate[:, P * d + 32 * d:P * d + 32 * d + 16] = a["gla_gate_w1_2"][j, d]
            parts += [_units(gate), _units(a["gla_w_in_2"][j]), _units(a["gla_w_out_2"][j])]
        parts += [_units(a["mlp_w_up_2"][i]), _units(a["mlp_w_down_2"][i])]
    return np.concatenate(parts)


def pack_vectors(a):
    out = np.zeros((P, N_VEC), np.float32)

    def put(name, cols):
        out[:, VEC[name]:VEC[name] + cols.shape[1]] = cols
    for l in range(DEPTH):
        put(f"b_mod{l}", _by_feature(a["b_mod"][l]))
        put(f"g1_{l}", _by_feature(a["g_norm1"][l]))
        put(f"g2_{l}", _by_feature(a["g_norm2"][l]))
        put(f"w_conv{l}", _by_feature(a["w_conv"][l].reshape(-1)))
        put(f"g_q{l}", np.tile(a["g_q"][l], 2)[:, None])
        put(f"g_k{l}", np.tile(a["g_k"][l], 2)[:, None])
    both = np.stack([_by_feature(a["c"][0]), _by_feature(a["c_ctx"])], 2)
    put("c", both.reshape(P, 2 * KT))
    put("gains", _by_feature(a["norm_gains_2"].reshape(-1)))
    put("b_in", _by_feature(a["conv_b_in_2"].reshape(-1)))
    put("w_dw", a["conv_w_dw_2"][0].reshape(31, KT, P).transpose(2, 1, 0).reshape(P, 31 * KT))
    put("b_dw", _by_feature(a["conv_b_dw_2"]))
    put("ln_gain", _by_feature(a["conv_ln_gain_2"]))
    put("ln_bias", _by_feature(a["conv_ln_bias_2"]))
    put("b_out", _by_feature(a["conv_b_out_2"]))
    put("gate_b", _by_feature(a["gla_gate_b_2"].reshape(-1)))
    put("gla_gain", _by_feature(a["gla_norm_gain_2"]))
    put("decay", np.tile(a["ret_decay_logit_2"].reshape(1, 16), (P, 1)))
    put("inv_freq", (np.float32(10000.0) ** (-np.arange(P, dtype=np.float32) / np.float32(P)))[:, None])
    return out


def constants():
    out, out2 = np.zeros((P, N_CON), np.float32), np.zeros((P, N_CON2), np.float32)

    def put(name, cols):
        o, at = (out2, CON2[name]) if name in CON2 else (out, CON[name])
        o[:, at:at + cols.shape[1]] = cols
    p = np.arange(P)
    put("ones", np.ones((P, P)))
    put("ident", np.eye(P))
    rot = np.zeros((P, P))
    first = p[p % HD < HD // 2]
    rot[first + HD // 2, first] = -1.0
    rot[first, first + HD // 2] = 1.0
    put("rot", rot)
    put("head_sel", np.stack([p < HD, p >= HD], 1))
    put("part_sel", (p[:, None] % 2 == np.arange(2)[None]) & (p[:, None] < 4))
    dim = 2 * np.pi * np.outer(p, p) / 64
    same = p[:, None] // 64 == p[None, :] // 64
    put("dim_dft", np.concatenate([np.cos(dim) * same, np.sin(dim) * same], 1) / 8)
    t = np.arange(TOK)
    tok = 2 * np.pi * np.outer(t, t) / TOK
    by_tile = lambda m: m.reshape(TT, P, TOK).transpose(1, 0, 2).reshape(P, TT * TOK)
    put("tok_cos", by_tile(np.cos(tok) / 16))
    put("tok_sin", by_tile(-np.sin(tok) / 16))
    n_freq = HD // 4
    inv = np.float32(10000.0) ** (-np.arange(n_freq, dtype=np.float32) / np.float32(n_freq))
    row, col = (t // 64).astype(np.float32), (t % 64).astype(np.float32)
    ang = np.concatenate([row[None] * inv[:, None], col[None] * inv[:, None]]).astype(np.float32)
    ang = np.tile(ang, (4, 1)).astype(np.float64)
    put("rope_cos", np.cos(ang))
    put("rope_sin", np.sin(ang))
    s = np.arange(TOK)
    put("after", by_tile(np.maximum(t[None, :] - s[:, None], 0.0)))
    put("before", by_tile(np.maximum(s[:, None] - t[None, :], 0.0)))
    c = np.arange(CHUNK)
    put("mask_fwd", np.tile(c[None, :] >= c[:, None], (2, 1)))
    put("mask_bwd", np.tile(c[None, :] < c[:, None], (2, 1)))
    return {"constants": out, "constants2": out2}


def kernel(**inputs):
    import concourse.bacc as _bacc
    from concourse.bass_utils import run_bass_kernel_spmd as _run

    a = {k: np.asarray(v) for k, v in inputs.items()}
    w2 = np.zeros((48, 512), np.float32)
    for d in range(2):
        w2[32 * d:32 * d + 16] = a["gla_gate_w2_2"][0, d]
    arrays = {
        "stream": pack_stream(a), "xT": np.ascontiguousarray(a["x"][0].T), "ctxT": np.ascontiguousarray(a["ctx"][0].T),
        "vectors": pack_vectors(a), **constants(),
        "positions": np.ascontiguousarray(np.tile(a["positions_2"], (P, 1))), "gate_w2": w2,
    }
    nc = _bacc.Bacc("TRN2", target_bir_lowering=False, num_devices=1)
    args = [nc.dram_tensor(n, v.shape, mybir.dt.from_np(v.dtype), kind="ExternalInput").ap() for n, v in arrays.items()]
    out = nc.dram_tensor("out", (D, TOK), F32, kind="ExternalOutput").ap()
    build(nc, *args, out)
    r = _run(nc, [arrays], core_ids=[0])
    return np.ascontiguousarray(r.results[0]["out"].T)[None]
```

```python
from contextlib import ExitStack

import numpy as np
import concourse.bass as bass
from concourse import mybir

F32 = mybir.dt.float32
F32R = mybir.dt.float32r
I32 = mybir.dt.int32
ALU = mybir.AluOpType
ACT = mybir.ActivationFunctionType
AX_X = mybir.AxisListType.X

P = 128
D = 1024
KT = D // P
TOK = 256
TT = TOK // P
FF = 4 * D
NM = 6 * KT
EPS = 1e-6
RAW = 8
SPLIT = 4
LEAD = SPLIT - 1
DEPTH = 2
HEADS, HD = 8, 64
CHUNK = 64
TAPS = 31
PE_TAPS = 13
DVE_TAPS = TAPS - PE_TAPS


def block1_stages():
    s = []
    for l in range(DEPTH):
        s.append((f"mod{l}", NM, f"mod{l}"))
        for who in ("ctx", "x"):
            if who == "ctx" and l == DEPTH - 1:
                s.append((f"ctx{l}.kv", 2, f"small{l}"))
                continue
            for part, n in (("small", 14), ("gates", 24), ("outs", 8), ("wo", 8), ("up", 32), ("down", 32)):
                s.append((f"{who}{l}.{part}", n, f"{part}{l}"))
    return s


def block2_stages():
    s = []
    for i in range(4):
        if i % 3 == 0:
            parts = (("qk", 16), ("v", 16), ("g", 16), ("out", 16))
        elif i % 3 == 1:
            parts = (("glu", 16), ("out", 8))
        else:
            parts = (("gate", 2), ("qk", 8), ("v", 8), ("r", 8), ("out", 8))
        for part, n in parts + (("up", 32), ("down", 32)):
            s.append((f"b{i}.{part}", n, f"b{i}.{part}"))
    return s


STAGES = block1_stages() + block2_stages()
FIRST, TOTAL = {}, 0
for _name, _n, _src in STAGES:
    FIRST[_name] = TOTAL
    TOTAL += _n
COUNT = {name: n for name, n, _ in STAGES}
SOURCE, N_STREAM = {}, 0
for _name, _n, _src in STAGES:
    if _src not in SOURCE:
        SOURCE[_src] = N_STREAM
        N_STREAM += 14 if _src.startswith("small") else _n

def columns(*parts):
    at, out = 0, {}
    for name, n in parts:
        out[name] = at
        at += n
    return out, at


VEC, N_VEC = columns(
    ("b_mod0", NM), ("b_mod1", NM), ("g1_0", KT), ("g1_1", KT), ("g2_0", KT), ("g2_1", KT),
    ("w_conv0", 6), ("w_conv1", 6), ("g_q0", 1), ("g_q1", 1), ("g_k0", 1), ("g_k1", 1), ("c", 2 * KT),
    ("gains", 16 * KT), ("b_in", 16), ("w_dw", TAPS * KT), ("b_dw", KT), ("ln_gain", KT), ("ln_bias", KT),
    ("b_out", KT), ("gate_b", 8), ("gla_gain", 2), ("decay", 16), ("inv_freq", 1),
)
CON, N_CON = columns(
    ("mean", P), ("ident", P), ("rot", P), ("head_mean", 2), ("part_sel", 2), ("dim_dft", 2 * P), ("tok_cos", TT * TOK),
    ("tok_sin", TT * TOK), ("rope_cos", TOK), ("rope_sin", TOK),
)
CON2, N_CON2 = columns(("after", TT * TOK), ("before", TT * TOK), ("mask_fwd", CHUNK), ("mask_bwd", CHUNK))
CON |= {name: CON["dim_dft"] + at for name, at in CON2.items()}
CON["pos_cos"] = CON["dim_dft"] + N_CON2
CON["pos_sin"] = CON["pos_cos"] + TOK


class Unit:

    def __init__(self, stage, j, e=0, turn=0):
        self.j, self.e, self.turn, self.s = j, e, turn, FIRST[stage] + j

    def raw(self, lead=0):
        return (self.s + lead) % RAW

    def split(self, lead=0):
        return (self.s + lead) % SPLIT

    bank = property(lambda self: self.s % 4)
    index = property(lambda self: self.j + self.e)


def at_least(eng, sem, known, e=0):
    if isinstance(e, int):
        if known + e > 0:
            eng.wait_ge(sem, known + e)
        return
    assert known >= 0
    eng.wait_ge(sem, e + known)


def over_units(eng, stage, body, peel=False, skip=0):
    n = COUNT[stage]
    head = RAW if (FIRST[stage] == 0 or peel or skip == RAW) and n > RAW else skip % RAW
    tail = RAW if FIRST[stage] + n == TOTAL and n > RAW else 0
    for j in range(skip % RAW, head):
        body(Unit(stage, j))
    loops = (n - head - tail) // RAW
    if loops > 1:
        with eng.Fori(0, loops) as i:
            e = i * RAW
            for j in range(head, head + RAW):
                body(Unit(stage, j, e, i))
    done = head + (loops * RAW if loops > 1 else 0)
    for j in range(done, n):
        body(Unit(stage, j))


def build(nc, stream, xT, ctxT, vec_d, con_d, con2_d, pos_d, w2_d, out_d):
    ctx = ExitStack()
    with ctx:
        def sb(name, cols, dt=F32):
            return ctx.enter_context(nc.sbuf_tensor(name, [P, cols], dt))

        def tiles(ap, n):
            return ap.rearrange("p (k n) -> p k n", k=n)

        def sem(name):
            return ctx.enter_context(nc.semaphore(name))

        bank = [ctx.enter_context(nc.psum_tensor(f"bank{i}", [P, 512], F32)) for i in range(8)]
        w_raw = tiles(sb("w_raw", RAW * D)[:, :], RAW)
        w_hi = tiles(sb("w_hi", SPLIT * D, F32R)[:, :], SPLIT)
        w_lo = tiles(sb("w_lo", SPLIT * D, F32R)[:, :], SPLIT)
        resid = {w: tiles(sb(f"resid_{w}", KT * TOK)[:, :], KT) for w in ("x", "ctx")}
        h_hi = tiles(sb("h_hi", KT * TOK, F32R)[:, :], KT)
        h_lo = tiles(sb("h_lo", KT * TOK, F32R)[:, :], KT)
        vec = sb("vec", N_VEC)
        con = sb("con", N_CON)
        scratch = tiles(sb("scratch", 24 * TOK)[:, :], 24)
        squares, scaled, full, gates = scratch[:, 0:8, :], scratch[:, 8:16, :], scratch[:, 16:24, :], scratch
        ring = sb("ring", 6 * TOK)
        relu, relu_sq = tiles(ring[:, 0:4 * TOK], 4), tiles(ring[:, 4 * TOK:6 * TOK], 2)
        mod_rows = ring[0:4, 4 * TOK:5 * TOK]
        neg_half = sb("neg_half", 1)
        mean_sq = sb("mean_sq", 24)
        inv_rms = sb("inv_rms", 24)
        EARLY = {"ctx": 20, "x": 22}
        cond_sig = sb("cond_sig", 2 * KT)
        cond_full = sb("cond_full", 2 * KT)
        cond_parts = tiles(sb("cond_parts", 4 * KT, F32R)[:, :], KT)
        mod_raw = sb("mod_raw", 2 * NM)
        mod = tiles(sb("mod", 2 * NM)[:, :], NM)
        mod_gain = tiles(sb("mod_gain", 4 * KT)[:, :], 4)
        ctx_k = sb("ctx_k", TOK)
        ctx_v = tiles(sb("ctx_v", TT * P)[:, :], TT)

        spare = resid["ctx"].rearrange("p k n -> p (k n)")
        decay_m, scores = tiles(spare[:, 0:1024], 2), tiles(spare[:, 1024:2048], 2)
        gla_low, gla_state, gla_s = spare[:, 0:TOK], tiles(spare[:, 256:1792], 6), tiles(spare[:, 1792:2048], TT)

        def added(j):
            b, half = ((4, 0), (6, 0), (4, 1), (6, 1), (5, 0), (7, 1))[j]
            return bank[b][:, half * TOK:(half + 1) * TOK]
        decay_end = sb("decay_end", 32)
        sum_ring = tiles(ring[:, 4 * TOK:5 * TOK], 2)
        gate_w2 = ring[:, 4 * TOK:6 * TOK]
        log_decay = sb("log_decay", 16)
        log_tmp = sb("log_tmp", 48)
        row_max = sb("row_max", TT)
        neg_max = sb("neg_max", TT)
        row_sum = sb("row_sum", TT)
        inv_sum = sb("inv_sum", TT)

        def overlay(*parts):
            with ExitStack() as inner:
                return [inner.enter_context(nc.sbuf_tensor(name, [P, cols], dt)) for name, cols, dt in parts]

        y_hi_t, y_lo_t, work = overlay(("y_hi", KT * TOK, F32R), ("y_lo", KT * TOK, F32R), ("work", 48 * TOK, F32))
        y_hi, y_lo = tiles(y_hi_t[:, :], KT), tiles(y_lo_t[:, :], KT)

        def zone(at, n, width=TOK):
            return tiles(work[:, at:at + n * width], n)

        z_k = work[:, 0:TOK]
        z_v = zone(256, TT, P)
        z_q, z_four, z_conv = zone(512, 4), zone(1536, 2), zone(2048, 6)
        qk_n, qk = zone(3584, 5), zone(4864, 5)
        four_mid = zone(6144, 4)
        conv_in = zone(7168, 2, TOK + 2)
        prob, prob_t = zone(7684, TT, 512), zone(8708, 4)
        terms = work[:, 9732:9732 + 6 * TOK].rearrange("p (a b n) -> p a b n", a=2, b=3)
        sums = zone(512, 4)
        ret_qk, ret_v_t, ret_o = overlay(("ret_qk", 32 * TOK, F32), ("ret_v", 16 * TOK, F32), ("ret_o", 16 * TOK, F32))
        ret_hi, _, ret_lo = overlay(("ret_hi", 16 * TOK, F32R), ("ret_rest", 16 * TOK, F32), ("ret_lo", 16 * TOK, F32R))

        def ret_lo_tile(k):
            i = (k % 4 // 2) * 8 + (k // 4) * 2 + k % 2
            return ret_lo[:, i * TOK:(i + 1) * TOK]
        ret_raw, ret_rot = ret_qk[:, 0:16 * TOK], ret_qk[:, 16 * TOK:32 * TOK]
        ret_v = tiles(ret_v_t[:, :], TT)
        conv_t, diagonal_t = overlay(("conv_t", KT * (TOK + 30) + 2 * KT * TOK, F32), ("diagonals", 2 * PE_TAPS * P, F32))
        diagonals = tiles(diagonal_t[:, :], 2)
        glu = tiles(conv_t[:, 0:KT * (TOK + 30)], KT)
        dw_out = conv_t[:, KT * (TOK + 30):KT * (TOK + 30) + KT * TOK]
        dw = tiles(dw_out, KT)
        (gla_t,) = overlay(("gla_t", 64 * TOK, F32))
        gla_q, gla_k = gla_t[:, 0:4 * TOK], gla_t[:, 4 * TOK:8 * TOK]
        gla_v = tiles(gla_t[:, 8 * TOK:16 * TOK], TT)
        log_g, cum_g = gla_t[:, 16 * TOK:24 * TOK], gla_t[:, 24 * TOK:32 * TOK]
        decayed = tiles(gla_t[:, 32 * TOK:56 * TOK], 6)
        ke_tok = tiles(gla_t[:, 56 * TOK:64 * TOK], 16)
        hidden_hi = sb("hidden_hi", 32 * TOK, F32R)
        hidden_lo = sb("hidden_lo", 32 * TOK, F32R)


        def V(name, i=0, n=1):
            return vec[:, VEC[name] + i:VEC[name] + i + n]

        def C(name, i=0, n=None):
            n = n or P
            return con[:, CON[name] + i:CON[name] + i + n]

        consts_in = sem("consts_in")
        raw_in = [sem(f"raw_in{i}") for i in range(RAW)]
        hi_ready = sem("hi_ready")
        lo_ready = sem("lo_ready")
        unit_done = sem("unit_done")
        evicted = sem("evicted")
        cond_sig_ready = sem("cond_sig_ready")
        cond_full_ready = sem("cond_full_ready")
        cond_hi_ready = sem("cond_hi_ready")
        cond_ready = sem("cond_ready")
        mod_cols_ready = sem("mod_cols_ready")
        mod_cols_out = sem("mod_cols_out")
        mod_ready = sem("mod_ready")
        sq_ready = sem("sq_ready")
        sums_ready = sem("sums_ready")
        mean_ready = sem("mean_ready")
        rstd_ready = sem("rstd_ready")
        half_ready = sem("half_ready")
        bcast_ready = sem("bcast_ready")
        norm_ready = sem("norm_ready")
        full_ready = sem("full_ready")
        h_hi_ready = sem("h_hi_ready")
        h_lo_ready = sem("h_lo_ready")
        hid_hi_ready = sem("hid_hi_ready")
        hid_sq_ready = sem("hid_sq_ready")
        hid_ready = sem("hid_ready")
        dve_chain = sem("dve_chain")
        qk_norm_ready = sem("qk_norm_ready")
        rot_ready = sem("rot_ready")
        rope_part = sem("rope_part")
        qk_ready = sem("qk_ready")
        four_ready = sem("four_ready")
        four_mid_ready = sem("four_mid_ready")
        four_out = sem("four_out")
        four_hi = sem("four_hi")
        y_full_ready = sem("y_full_ready")
        conv_hi = sem("conv_hi")
        y_ready = sem("y_ready")
        s_ready = sem("s_ready")
        max_ready = sem("max_ready")
        exp_ready = sem("exp_ready")
        p_ready = sem("p_ready")
        pt_ready = sem("pt_ready")
        pt_act = sem("pt_act")
        pt_dve = sem("pt_dve")
        o_ready = sem("o_ready")
        o_hi = sem("o_hi")
        o_lo = sem("o_lo")
        merged = sem("merged")
        merge_step = sem("merge_step")
        stored = sem("stored")
        con2_in = sem("con2_in")
        angle_ready = sem("angle_ready")
        sin_ready = sem("sin_ready")
        updated = sem("updated")
        square_used = sem("square_used")
        product_normed = sem("product_normed")
        tanh_ready = sem("tanh_ready")
        rot_a = sem("rot_a")
        rot_done = sem("rot_done")
        decay_arg = sem("decay_arg")
        decay_ready = sem("decay_ready")
        scores_ready = sem("scores_ready")
        weighted = sem("weighted")
        head_out = sem("head_out")
        head_copied = sem("head_copied")
        gated = sem("gated")
        gated_full = sem("gated_full")
        ret_hi_ready = sem("ret_hi_ready")
        ret_ready = sem("ret_ready")
        glu_ready = sem("glu_ready")
        pad_ready = sem("pad_ready")
        tap = sem("tap")
        diagonals_ready = sem("diagonals_ready")
        conv_summed = sem("conv_summed")
        dw_ready = sem("dw_ready")
        centred = sem("centred")
        ln_scaled = sem("ln_scaled")
        silu_in = sem("silu_in")
        w2_in = sem("w2_in")
        logits_ready = sem("logits_ready")
        added_ready = sem("added_ready")
        gla_dve = sem("gla_dve")
        gla_act = sem("gla_act")
        sin_part = sem("sin_part")
        ke_ready = sem("ke_ready")
        ke_out = sem("ke_out")
        state_in = sem("state_in")
        state_ready = sem("state_ready")
        gla_o = sem("gla_o")
        head_normed = sem("head_normed")

        CHAINS, FILLS, NORMS, squared, summed, raised = {}, {}, {}, [0], [0], [0]

        def chain(name, width, sums=1, powers=None):
            CHAINS[name] = (summed[0], squared[0], raised[0])
            raised[0] += sums if powers is None else powers
            squared[0] += width
            summed[0] += sums

        def fill(name):
            FILLS[name] = len(FILLS)
            if "norm" in name:
                NORMS[name] = len(NORMS)

        BROADCASTS = {}
        for l in range(DEPTH):
            for who in ("ctx", "x"):
                chain(f"{who}{l}.norm1", KT)
            for who in ("ctx", "x"):
                kv = who == "ctx" and l == DEPTH - 1
                fill(f"{who}{l}.norm1")
                for name in (f"{who}{l}.norm1", f"{who}{l}.qk") + (() if kv else (f"{who}{l}.norm2",)):
                    BROADCASTS.setdefault(name, len(BROADCASTS))
                if (who, l) == ("ctx", 0):
                    BROADCASTS["x0.norm1"] = len(BROADCASTS)
                chain(f"{who}{l}.qk", 1 if kv else 5)
                if not kv:
                    fill(f"{who}{l}.m")
                    chain(f"{who}{l}.norm2", KT); fill(f"{who}{l}.norm2")
        for i in range(4):
            b = f"b{i}"
            chain(f"{b}.n0", KT); fill(f"{b}.n0"); NORMS[f"{b}.n0"] = len(NORMS)
            if i % 3 == 0:
                chain(f"{b}.heads", 16, sums=4)
            elif i % 3 == 1:
                chain(f"{b}.mean", 0, powers=0); chain(f"{b}.var", KT); fill(f"{b}.y"); NORMS[f"{b}.y"] = len(NORMS)
            else:
                chain(f"{b}.heads", KT); fill(f"{b}.y"); NORMS[f"{b}.y"] = len(NORMS)
            chain(f"{b}.n1", 0)
            chain(f"{b}.n2", KT); fill(f"{b}.n2"); NORMS[f"{b}.n2"] = len(NORMS)
            chain(f"{b}.n3", 0)
        RETS = {"b0": 0, "b3": 1}
        GATES = {"b0": 0, "b2": 16, "b3": 24}
        FIRST_PART = ("qk", "glu", "gate")
        CHAIN_READS = {f"b{i}.{part}": CHAINS[f"b{i}.{c}"][0] for i in range(4) for part, c in (("out", "n1"), ("down", "n3"))}
        half = 4 * TOK
        sq_flat = squares.rearrange("p k n -> p (k n)")
        GLA_ARG = [(cum_g[:, 0:half], sq_flat[:, 0:half]), (sq_flat[:, half:2 * half], log_g[:, half:2 * half])]

        TWO_PI = [6.28125, 0.001934051513671875, float(2 * np.pi - 6.28125 - 0.001934051513671875)]

        PRODUCTS = {f"b{i}.{part}": 2 * i + j for i in range(4) for j, part in enumerate(("out", "down"))}
        PASSES = {w: n for n, w in enumerate(("ctx0", "x0", "x1"))}
        FFNS = {w: n for n, w in enumerate(("ctx0", "x0", "x1", "b0", "b1", "b2", "b3"))}

        block = ctx.enter_context(nc.Block())

        @block.sync
        def _(sp):
            for dst, src in ((vec[:, :], vec_d), (con[:, :], con_d),
                             (resid["ctx"], ctxT.rearrange("(k p) t -> p k t", p=P)),
                             (resid["x"], xT.rearrange("(k p) t -> p k t", p=P))):
                sp.dma_start(dst, src).then_inc(consts_in, 16)
            rows = stream.rearrange("u p n -> (u p) n")

            def block2_inputs():
                sp.wait_ge(o_lo, 3 * HEADS)
                sp.wait_ge(y_ready, 3 * 4)
                at = CON["dim_dft"]
                sp.dma_start(con[:, at:at + N_CON2], con2_d).then_inc(con2_in, 16)
                sp.wait_ge(evicted, FIRST["x1.up"])
                sp.dma_start(scaled[:, 0, :].bitcast(I32), pos_d).then_inc(con2_in, 16)
            for stage, _, src in STAGES:

                def load(u, src=src):
                    at_least(sp, lo_ready, u.s - RAW + 1, u.e)
                    sp.dma_start(w_raw[:, u.raw(), :], rows[bass.ds((SOURCE[src] + u.j + u.e) * P, P), :]
                                 ).then_inc(raw_in[u.raw()], 16)

                over_units(sp, stage, load)
                if stage == "x1.down":
                    block2_inputs()
                if stage == "b1.down":
                    sp.wait_ge(hid_ready, 32 * FFNS["b1"] + 32)
                    sp.dma_start(gate_w2[0:48, :], w2_d).then_inc(w2_in, 16)
            sp.wait_ge(updated, KT * 8)
            sp.dma_start(out_d.rearrange("(k p) t -> p k t", p=P), resid["x"]).then_inc(stored, 16)
            sp.wait_ge(stored, 16)

        @block.tensor
        def _(pe):
            def mm(out, lhsT, rhs, start=True, stop=True):
                return pe.matmul(out, lhsT, rhs, start=start, stop=stop, skip_group_check=True)

            def product(u, out, hi, lo, ks=range(KT), first=True, last=True, ready=None):
                w = u.split()
                for k in ks:
                    cols = slice(k * P, (k + 1) * P)
                    a, b = first and k == ks[0], last and k == ks[-1]
                    if ready:
                        ready(k)
                    mm(out, w_hi[:, w, cols], hi(k), start=a, stop=False)
                    mm(out, w_hi[:, w, cols], lo(k), start=False, stop=False)
                    done = mm(out, w_lo[:, w, cols], hi(k), start=False, stop=b)
                return done

            def pair_by_token(u):
                if u.j % 2 == 0:
                    return
                at_least(pe, lo_ready, u.s + 1, u.e)
                at_least(pe, evicted, u.s - 3, u.e)
                for t in range(TT):
                    tok = slice(t * P, (t + 1) * P)
                    o = bank[(u.s - 1 + t) % 4][:, 0:2 * P]
                    for k in range(KT):
                        w = slice(u.split(-1), u.split(-1) + 2)
                        both = lambda part: part[:, w, k * P:(k + 1) * P]
                        mm(o, H(k)[:, tok], both(w_hi), start=k == 0, stop=False)
                        mm(o, L(k)[:, tok], both(w_hi), start=False, stop=False)
                        m = mm(o, H(k)[:, tok], both(w_lo), start=False, stop=k == KT - 1)
                    m.then_inc(unit_done, 1)

            def product_by_token(u, out, hi, lo):
                w = u.split()
                for t in range(TT):
                    tok = slice(t * P, (t + 1) * P)
                    for k in range(KT):
                        cols = slice(k * P, (k + 1) * P)
                        o = out[:, tok]
                        mm(o, hi(k)[:, tok], w_hi[:, w, cols], start=k == 0, stop=False)
                        mm(o, lo(k)[:, tok], w_hi[:, w, cols], start=False, stop=False)
                        done = mm(o, hi(k)[:, tok], w_lo[:, w, cols], start=False, stop=k == KT - 1)
                return done

            def begin(u):
                at_least(pe, lo_ready, u.s + 1, u.e)
                at_least(pe, evicted, u.s - 3, u.e)

            H = lambda k: h_hi[:, k, :]
            L = lambda k: h_lo[:, k, :]
            Y = lambda k: y_hi[:, k, :]
            YL = lambda k: y_lo[:, k, :]

            def plain(u):
                begin(u)
                product(u, bank[u.bank][:, 0:TOK], H, L).then_inc(unit_done, 1)

            def add_squares(tile, col, start, stop):
                for t in range(TT):
                    m = mm(bank[7][:, col + t:col + t + 1], tile[:, t * P:(t + 1) * P], C("mean", n=1),
                           start=start and t == 0, stop=stop)
                return m

            def row_sums(name, width, first=0):
                r, sq0, _ = CHAINS[name]
                at_least(pe, mean_ready, r)
                for k in range(first, width):
                    pe.wait_ge(sq_ready, sq0 + k + 1)
                    s = add_squares(squares[:, k, :], 0, k == 0, k == width - 1)
                s.then_inc(sums_ready, 1)

            def statistics(name, width, first=0):
                row_sums(name, width, first)
                broadcast(name, (bank[6][:, 0:TOK],))

            def broadcast(name, outs, i=0, heads=1, col=0):
                _, _, n = CHAINS[name]
                pe.wait_ge(rstd_ready, n + i + 1)
                for j, out in enumerate(outs):
                    for t in range(TT):
                        for h in range(heads):
                            c = col + (j * TT + t) * heads + h
                            rows = slice(h * P // heads, (h + 1) * P // heads)
                            b = mm(out[rows, t * P:(t + 1) * P],
                                   inv_rms[:, c:c + 1].broadcast_to([P, P // heads]), C("ident"))
                b.then_inc(bcast_ready, 1)

            HALVES = [bank[4 + j // 2][:, (j % 2) * TOK:(j % 2 + 1) * TOK] for j in range(6)]

            def first_unit(stage, name, j=0):
                u = Unit(stage, j)
                begin(u)

                def ready(k):
                    pe.wait_ge(h_lo_ready, KT * FILLS[name] + k + 1)
                product(u, bank[u.bank][:, 0:TOK], H, L, ready=ready).then_inc(unit_done, 1)

            def stage_of(stage, name):
                first_unit(stage, name)
                over_units(pe, stage, plain, skip=1)

            def modulation(l):
                pe.wait_ge(cond_ready, 1)

                def body(u):
                    if u.j % 2 == 0:
                        return
                    at_least(pe, lo_ready, u.s + 1, u.e)
                    at_least(pe, evicted, u.s - 3, u.e)
                    pair = l * NM // 2 + u.j // 2
                    w = slice(u.split(-1), u.split(-1) + 2)
                    for k in range(KT):
                        for part in (w_hi, w_lo):
                            m = mm(bank[u.bank][0:4, 0:2 * P], cond_parts[:, k, :], part[:, w, k * P:(k + 1) * P],
                                   start=k == 0 and part is w_hi, stop=k == KT - 1 and part is w_lo)
                    m.then_inc(unit_done, 2)
                    at_least(pe, evicted, u.s + 1, u.e)
                    at_least(pe, mod_cols_out, pair - 1, u.turn * 4)
                    for i in range(2):
                        m = mm(bank[4 + pair % 2][:, 2 * i:2 * i + 2], mod_rows[:, i * P:(i + 1) * P],
                               con[0:4, CON["part_sel"]:CON["part_sel"] + 2])
                    m.then_inc(mod_cols_ready, 1)
                over_units(pe, f"mod{l}", body)

            def head_statistics(name, n):
                r, sq0, _ = CHAINS[name]
                at_least(pe, mean_ready, r)
                for j in range(n):
                    pe.wait_ge(sq_ready, sq0 + j + 1)
                    for t in range(TT):
                        c = 4 * j + 2 * t
                        s = mm(bank[7][:, c:c + 2], squares[:, j, t * P:(t + 1) * P], C("head_mean", n=2))
                s.then_inc(sums_ready, 1)

            def small(w):
                n = PASSES[w]
                first_unit(f"{w}.small", f"{w}.norm1")
                for j in range(1, 14):
                    u = Unit(f"{w}.small", j)
                    begin(u)
                    if j == 1:
                        product_by_token(u, bank[u.bank][:, 0:TOK], H, L).then_inc(unit_done, 1)
                    else:
                        product(u, bank[u.bank][:, 0:TOK], H, L).then_inc(unit_done, 1)
                    if j == 7:
                        head_statistics(f"{w}.qk", 5)
                    if j == 8:
                        pe.wait_ge(evicted, FIRST[f"{w}.small"] + 8)
                        for f in range(2):
                            for t in range(TT):
                                m = mm(bank[4 + f][:, t * 2 * P:(t + 1) * 2 * P],
                                       z_four[:, f, t * P:(t + 1) * P], C("dim_dft", n=2 * P))
                        m.then_inc(four_ready, 1)
                    if j == 9:
                        pe.wait_ge(four_mid_ready, n + 1)
                        broadcast(f"{w}.qk", HALVES[:5], heads=2)
                    if j == 11:
                        pe.wait_ge(qk_norm_ready, 5 * n + 5)
                        if w != "ctx0":
                            for i in range(5):
                                m = mm(bank[4 + i // 2][:, (i % 2) * TOK:(i % 2 + 1) * TOK], C("rot"),
                                       qk_n[:, i, :])
                            m.then_inc(rot_ready, 1)
                        for f in range(2):
                            for t in range(TT):
                                for part, table in enumerate(("tok_cos", "tok_sin")):
                                    m = mm(bank[7][:, f * TOK:(f + 1) * TOK],
                                           four_mid[:, f * 2 + t, part * P:(part + 1) * P],
                                           C(table, t * TOK, TOK), start=t == 0 and part == 0,
                                           stop=t == TT - 1 and part == 1)
                        m.then_inc(four_out, 1)

            def attention(w):
                n = PASSES[w]
                keys = 2 if w == "ctx0" else 4
                K = [ctx_k[:, :]] if w == "ctx0" else [qk[:, 0, :], ctx_k[:, :]]
                VT = [ctx_v[:, t, :] for t in range(TT)]
                if w != "ctx0":
                    VT = [z_v[:, t, :] for t in range(TT)] + VT
                if w == "ctx0":
                    pe.wait_ge(qk_norm_ready, 5)
                else:
                    pe.wait_ge(qk_ready, n)
                pe.wait_ge(y_ready, 4 * n + 2)

                def head_scores(a):
                    rows = slice((a % 2) * HD, (a % 2) * HD + HD)
                    at_least(pe, exp_ready, 2 * (HEADS * n + a))
                    for t in range(TT):
                        for i, keys_t in enumerate(K):
                            m = mm(bank[4 + t][:, i * TOK:(i + 1) * TOK],
                                   qk[rows, 1 + a // 2, t * P:(t + 1) * P], keys_t[rows, :])
                        m.then_inc(s_ready, 1)

                head_scores(0)
                for a in range(HEADS):
                    g = HEADS * n + a
                    rows = slice((a % 2) * HD, (a % 2) * HD + HD)
                    plain(Unit(f"{w}.gates", 3 * a))
                    plain(Unit(f"{w}.gates", 3 * a + 1))
                    at_least(pe, o_lo, g)
                    if keys == 4:
                        at_least(pe, pt_dve, g - HEADS)
                    for t in range(TT):
                        pe.wait_ge(p_ready, 2 * g + t + 1)
                        for k in range(keys):
                            o = bank[6 + k // 2][:, (k % 2) * TOK + t * P:(k % 2) * TOK + (t + 1) * P]
                            m = pe.transpose(o, prob[:, t, k * P:(k + 1) * P], C("ident"))
                    m.then_inc(pt_ready, 1)
                    if a < HEADS - 1:
                        head_scores(a + 1)
                    plain(Unit(f"{w}.gates", 3 * a + 2))
                    pe.wait_ge(pt_act, g + 1)
                    if keys == 4:
                        pe.wait_ge(pt_dve, g - HEADS + 1)
                    for k in range(keys):
                        m = mm(bank[6][rows, 0:TOK], VT[k][:, rows], prob_t[:, k, :], start=k == 0,
                               stop=k == keys - 1)
                    m.then_inc(o_ready, 1)

            def merge(w):
                n = PASSES[w]
                pe.wait_ge(o_lo, HEADS * n + HEADS)
                pe.wait_ge(y_ready, 4 * n + 4)

                def body(u):
                    begin(u)
                    at_least(pe, evicted, u.s - 1, u.e)
                    b = bank[u.bank]
                    product(u, b[:, 0:TOK], Y, YL, ks=range(0, 2))
                    product(u, b[:, TOK:2 * TOK], Y, YL, ks=range(2, 4))
                    product(u, bank[4 + u.s % 2][:, 0:TOK], Y, YL, ks=range(4, 8)).then_inc(unit_done, 1)
                over_units(pe, f"{w}.outs", body)

            def down(w, step=None):
                f = FFNS[w]

                def body(u):
                    kg = u.j % 4
                    at_least(pe, lo_ready, u.s + 1, u.e)
                    if kg == 0:
                        at_least(pe, evicted, u.s - 4, u.e)
                    pe.wait_ge(hid_ready, 32 * f + KT * (kg + 1))
                    hid = lambda big: lambda k: big[:, (kg * KT + k) * TOK:(kg * KT + k + 1) * TOK]
                    product(u, bank[4 + (u.j // 4) % 2][:, 0:TOK], hid(hidden_hi), hid(hidden_lo),
                            first=kg == 0, last=kg == 3).then_inc(unit_done, 1)
                    if step and kg == 3 and (u.j > 3 or not isinstance(u.e, int)):
                        step(u.j // 4 - 1, u.e)
                over_units(pe, f"{w}.down", body, skip=RAW if step else 0)
                if step:
                    step(KT - 1)

            pe.wait_ge(consts_in, 16 * 4)
            for l in range(DEPTH):
                for who in ("ctx", "x"):
                    row_sums(f"{who}{l}.norm1", KT)
                modulation(l)
                for who in ("ctx", "x"):
                    w = f"{who}{l}"
                    if w != "x0":
                        broadcast(f"{w}.norm1", (bank[6][:, 0:TOK],), col=EARLY[who])
                    if w == "ctx1":
                        first_unit("ctx1.kv", "ctx1.norm1")
                        u = Unit("ctx1.kv", 1)
                        begin(u)
                        product_by_token(u, bank[u.bank][:, 0:TOK], H, L).then_inc(unit_done, 1)
                        head_statistics("ctx1.qk", 1)
                        broadcast("ctx1.qk", HALVES[:1], heads=2)
                        continue
                    small(w)
                    attention(w)
                    merge(w)
                    first_unit(f"{w}.wo", f"{w}.m")
                    _, sq0, _ = CHAINS[f"{w}.norm2"]
                    for j in range(1, KT):
                        plain(Unit(f"{w}.wo", j))
                        if j > 1:
                            pe.wait_ge(sq_ready, sq0 + j - 1)
                            add_squares(squares[:, j - 2, :], 0, j == 2, False)
                    statistics(f"{w}.norm2", KT, KT - 2)
                    stage_of(f"{w}.up", f"{w}.norm2")
                    if w == "ctx0":
                        broadcast("x0.norm1", (bank[6][:, 0:TOK],), col=EARLY["x"])
                    down(w)

            def product_squares(stage, group, name):
                r, _, _ = CHAINS[name]

                def step(m, e=0):
                    if m == 0:
                        at_least(pe, mean_ready, r)
                    at_least(pe, evicted, FIRST[stage] + (m + 1) * group, e)
                    done = add_squares(squares[:, m % 2, :], 0, m == 0, m == KT - 1)
                    if m < KT - 1:
                        done.then_inc(square_used, 1)
                    else:
                        done.then_inc(sums_ready, 1)
                        broadcast(name, (bank[6][:, 0:TOK],))
                return step

            def retention(b):
                n = RETS[b]
                qt = lambda i: ret_rot[:, i * TOK:(i + 1) * TOK]

                stage_of(f"{b}.qk", f"{b}.n0")
                over_units(pe, f"{b}.v", pair_by_token)
                pe.wait_ge(evicted, FIRST[f"{b}.g"])
                r, sq0, _ = CHAINS[f"{b}.heads"]
                def head_broadcast(h):
                    broadcast(f"{b}.heads", (bank[7][:, TOK:2 * TOK],), i=h, col=2 * (h % 2))

                for h in range(4):
                    pe.wait_ge(rot_done, 8 * n + 5 + h)
                    at_least(pe, weighted, 4 * n + h)
                    for t in range(TT):
                        for d in range(2):
                            m = mm(bank[4][:, t * TOK:(t + 1) * TOK], qt(8 + 2 * h + d)[:, t * P:(t + 1) * P],
                                   qt(2 * h + d), start=d == 0, stop=d == 1)
                    m.then_inc(scores_ready, 1)
                    plain(Unit(f"{b}.g", 4 * h))
                    plain(Unit(f"{b}.g", 4 * h + 1))
                    pe.wait_ge(weighted, 4 * n + h + 1)
                    at_least(pe, sq_ready, sq0 + 4 * h)
                    for v in range(4):
                        for t in range(TT):
                            m = mm(bank[5 + v // 2][:, (v % 2) * TOK:(v % 2 + 1) * TOK],
                                   ret_v[:, t, h * 512 + v * P:h * 512 + (v + 1) * P],
                                   scores[:, h % 2, t * TOK:(t + 1) * TOK], start=t == 0, stop=t == 1)
                    m.then_inc(head_out, 1)
                    plain(Unit(f"{b}.g", 4 * h + 2))
                    plain(Unit(f"{b}.g", 4 * h + 3))
                    pe.wait_ge(sq_ready, sq0 + 4 * h + 4)
                    at_least(pe, mean_ready, r + h)
                    for v in range(4):
                        m = add_squares(squares[:, 4 * (h % 2) + v, :], 2 * (h % 2), v == 0, v == 3)
                    m.then_inc(sums_ready, 1)
                    if h > 0:
                        pe.wait_ge(gated_full, 16 * n + 4 * (h - 1))
                        head_broadcast(h - 1)
                pe.wait_ge(gated_full, 16 * n + 12)
                head_broadcast(3)
                step = product_squares(f"{b}.out", 2, f"{b}.n1")

                def out(u):
                    kg = u.j % 2
                    at_least(pe, lo_ready, u.s + 1, u.e)
                    if kg == 0:
                        at_least(pe, evicted, u.s - 2, u.e)
                    pe.wait_ge(ret_ready, 16 * n + KT * (kg + 1))
                    product(u, bank[4 + (u.j // 2) % 2][:, 0:TOK],
                            lambda k: ret_hi[:, (kg * KT + k) * TOK:(kg * KT + k + 1) * TOK],
                            lambda k: ret_lo_tile(kg * KT + k),
                            first=kg == 0, last=kg == 1).then_inc(unit_done, 1)
                    if kg == 1 and u.j > 1:
                        step(u.j // 2 - 1, u.e)
                over_units(pe, f"{b}.out", out, skip=RAW)
                step(KT - 1)

            def conformer(b):
                r, _, _ = CHAINS[f"{b}.mean"]
                at_least(pe, mean_ready, r)

                def taps(m):
                    pe.wait_ge(glu_ready, m + 1)
                    pe.wait_ge(diagonals_ready, m + 1)
                    at_least(pe, dw_ready, m - 1)
                    for t in range(PE_TAPS):
                        at = DVE_TAPS + t
                        c = mm(bank[4 + m % 2][:, 0:TOK], diagonals[:, m % 2, t * P:(t + 1) * P],
                               glu[:, m, at:at + TOK], start=t == 0, stop=t == PE_TAPS - 1)
                    c.then_inc(conv_summed, 1)

                def mean(m):
                    pe.wait_ge(dw_ready, m + 1)
                    return mm(bank[7][:, 0:TOK], C("mean"), dw[:, m, :], start=m == 0, stop=m == KT - 1)

                first_unit(f"{b}.glu", f"{b}.n0")
                for j in range(1, 2 * KT):
                    plain(Unit(f"{b}.glu", j))
                    if j % 2 == 1 and j > 1:
                        taps(j // 2 - 1)
                    if j % 2 == 1 and j > 5:
                        mean(j // 2 - 3)
                taps(KT - 1)
                for m in range(KT - 3, KT):
                    s = mean(m)
                s.then_inc(sums_ready, 1)
                statistics(f"{b}.var", KT)
                out_by_tile(b)

            def out_by_tile(b):
                step = product_squares(f"{b}.out", 1, f"{b}.n1")
                first_unit(f"{b}.out", f"{b}.y")
                for j in range(1, KT):
                    plain(Unit(f"{b}.out", j))
                    step(j - 1)
                step(KT - 1)

            def gla(b):
                stage_of(f"{b}.gate", f"{b}.n0")
                plain(Unit(f"{b}.qk", 0))
                pe.wait_ge(w2_in, 16)
                pe.wait_ge(evicted, FIRST[f"{b}.gate"] + 2)
                for d in range(2):
                    rows = slice(32 * d, 32 * d + 16)
                    for h in range(4):
                        i = 4 * d + h
                        m = mm(bank[4 + i // 2][:, (i % 2) * TOK:(i % 2 + 1) * TOK],
                               gate_w2[rows, h * P:(h + 1) * P], gla_low[rows, :])
                m.then_inc(logits_ready, 1)
                over_units(pe, f"{b}.qk", plain, skip=1)

                over_units(pe, f"{b}.v", pair_by_token)
                for d in range(2):
                    pe.wait_ge(ke_ready, d + 1)
                    for h in range(4):
                        for t in range(TT):
                            i = (d * 4 + h) * 2 + t
                            m = pe.transpose(bank[4 + i // 4][:, (i % 4) * P:(i % 4 + 1) * P],
                                             decayed[:, 3 * d + 2, h * TOK + t * P:h * TOK + (t + 1) * P],
                                             C("ident"))
                m.then_inc(ke_out, 1)
                pe.wait_ge(evicted, FIRST[f"{b}.r"])
                chunk = lambda c: slice((c % 2) * CHUNK, (c % 2 + 1) * CHUNK)
                for h in range(4):
                    col = lambda c: slice(h * TOK + c * CHUNK, h * TOK + (c + 1) * CHUNK)
                    if h == 0:
                        pe.wait_ge(state_in, 1)
                    else:
                        pe.wait_ge(sq_ready, CHAINS[f"{b}.heads"][1] + 2 * h)
                    for d in range(2):
                        for c in range(4):
                            m = mm(bank[7][chunk(c), d * P + (c // 2) * CHUNK:d * P + (c // 2 + 1) * CHUNK],
                                   decayed[:, 3 * d + 1, col(c)], decayed[:, 3 * d, col(c)])
                    m.then_inc(scores_ready, 1)
                    for d in range(2):
                        for i in range(3):
                            c = i if d == 0 else 3 - i
                            j = 3 * d + i
                            m = mm(added(j),
                                   ke_tok[chunk(c), (d * 4 + h) * 2 + c // 2, :],
                                   gla_v[chunk(c), c // 2, h * TOK:(h + 1) * TOK])
                    m.then_inc(added_ready, 1)
                    plain(Unit(f"{b}.r", 2 * h))
                    pe.wait_ge(state_ready, h + 1)
                    for t in range(TT):
                        for v in range(2):
                            o = bank[4][:, v * TOK + t * P:v * TOK + (t + 1) * P]
                            cols = slice(v * P, (v + 1) * P)
                            mm(o, gla_v[:, t, h * TOK + v * P:h * TOK + (v + 1) * P], gla_s[:, t, :], stop=False)
                            for c in (2 * t, 2 * t + 1):
                                o = bank[4][:, v * TOK + c * CHUNK:v * TOK + (c + 1) * CHUNK]
                                if c > 0:
                                    m = mm(o, gla_state[:, c - 1, cols], decayed[:, 0, col(c)], start=False)
                                if c < 3:
                                    m = mm(o, gla_state[:, 3 + 2 - c, cols], decayed[:, 3, col(c)], start=False)
                    m.then_inc(head_out, 1)
                    plain(Unit(f"{b}.r", 2 * h + 1))
                _, sq0, _ = CHAINS[f"{b}.heads"]
                pe.wait_ge(sq_ready, sq0 + KT)
                for h in range(4):
                    for v in range(2):
                        m = add_squares(squares[:, 2 * h + v, :], 2 * h, v == 0, v == 1)
                m.then_inc(sums_ready, 1)
                broadcast(f"{b}.heads", HALVES[:4])
                out_by_tile(b)

            pe.wait_ge(con2_in, 32)
            for i in range(4):
                b = f"b{i}"
                statistics(f"{b}.n0", KT)
                (retention, conformer, gla)[i % 3](b)
                statistics(f"{b}.n2", KT)
                stage_of(f"{b}.up", f"{b}.n2")
                down(b, product_squares(f"{b}.down", 4, f"{b}.n3"))

        @block.scalar
        def _(act):
            def split_hi(u, lead=LEAD, pair=False):
                if isinstance(u.e, int) and u.s + lead >= TOTAL:
                    return
                s = u.s + lead
                at_least(act, raw_in[u.raw(lead)], 16 * (s // RAW + 1), 2 * u.e)
                both = 1 if pair and u.j % 2 == 1 else 0
                at_least(act, unit_done, s - SPLIT + 1 + both, u.e)
                act.activation(w_hi[:, u.split(lead), :], w_raw[:, u.raw(lead), :], ACT.Copy
                               ).then_inc(hi_ready, 1)

            def copy_out(u, out, func=ACT.Copy, scale=1.0):
                at_least(act, unit_done, u.s + 1, u.e)
                act.activation(out, bank[u.bank][:, 0:TOK], func, scale=scale).then_inc(evicted, 1)

            def square(name, k, ap):
                r, _, _ = CHAINS[name]
                if k == 0:
                    at_least(act, sums_ready, r)
                act.activation(squares[:, k, :], ap, ACT.Square).then_inc(sq_ready, 1)

            def norm(name, which, who, ready, before, first=0):
                for k in range(first, KT):
                    ready(act, k)
                    square(name, k, resid[who][:, k, :])
                h_free(name, before)
                for k in range(KT):
                    modulated(name, which, who, k)

            def h_free(name, before):
                act.wait_ge(unit_done, before)
                at_least(act, h_lo_ready, KT * FILLS[name])

            def modulated(name, which, who, k):
                c = 0 if who == "x" else 1
                act.wait_ge(norm_ready, KT * NORMS[name] + k + 1)
                shift = mod[:, which * 3 * KT + k, c:c + 1]
                gain = mod_gain[:, 2 * which + c, k:k + 1]
                act.activation(full[:, k, :], scaled[:, k, :], ACT.Identity, bias=shift, scale=gain
                               ).then_inc(full_ready, 1)
                act.activation(h_hi[:, k, :], scaled[:, k, :], ACT.Identity, bias=shift, scale=gain
                               ).then_inc(h_hi_ready, 1)

            def small(w):
                n = PASSES[w]
                outs = {0: z_k, 1: z_v.rearrange("p t n -> p (t n)"), 6: z_four[:, 0, :], 7: z_four[:, 1, :]}
                if w == "ctx0":
                    outs[1] = ctx_v.rearrange("p t n -> p (t n)")
                outs |= {2 + j: z_q[:, j, :] for j in range(4)} | {8 + j: z_conv[:, j, :] for j in range(6)}
                for j in range(14):
                    u = Unit(f"{w}.small", j)
                    split_hi(u)
                    copy_out(u, outs[j])
                    if j == 5:
                        act.wait_ge(evicted, u.s + 1)
                        for i in range(5):
                            square(f"{w}.qk", i, z_k if i == 0 else z_q[:, i - 1, :])
                    if j == 9:
                        act.wait_ge(four_ready, n + 1)
                        act.activation(four_mid[:, 0:2, :].rearrange("p a n -> p (a n)"), bank[4][:, :], ACT.Copy)
                        act.activation(four_mid[:, 2:4, :].rearrange("p a n -> p (a n)"), bank[5][:, :], ACT.Copy
                                       ).then_inc(four_mid_ready, 1)
                    if j == 12:
                        act.wait_ge(four_out, n + 1)
                        act.activation(y_hi[:, 2:4, :].rearrange("p a n -> p (a n)"), bank[7][:, :], ACT.Copy
                                       ).then_inc(four_hi, 1)
                for j in range(2):
                    act.wait_ge(y_full_ready, 2 * n + j + 1)
                    act.activation(y_hi[:, j, :], full[:, j, :], ACT.Copy).then_inc(conv_hi, 1)

            def attention(w):
                n = PASSES[w]
                keys = 2 if w == "ctx0" else 4
                for a in range(HEADS):
                    g = HEADS * n + a
                    units = [Unit(f"{w}.gates", 3 * a + i) for i in range(3)]

                    def gate(u):
                        copy_out(u, gates[:, u.j, :], ACT.Tanh, 0.5)
                    split_hi(units[0])
                    for t in range(TT):
                        act.wait_ge(max_ready, 2 * g + t + 1)
                        act.activation(prob[:, t, 0:keys * P], bank[4 + t][:, 0:keys * P], ACT.Exp,
                                       bias=neg_max[:, t:t + 1], scale=HD ** -0.5,
                                       accum_out=row_sum[:, t:t + 1]).then_inc(exp_ready, 1)
                    gate(units[0])
                    split_hi(units[1])
                    gate(units[1])
                    split_hi(units[2])
                    act.wait_ge(pt_ready, g + 1)
                    act.activation(prob_t[:, 0:2, :].rearrange("p a n -> p (a n)"), bank[6][:, :], ACT.Copy
                                   ).then_inc(pt_act, 1)
                    gate(units[2])
                    rows = slice((a % 2) * HD, (a % 2) * HD + HD)
                    act.wait_ge(o_ready, g + 1)
                    act.activation(y_hi[rows, 4 + a // 2, :], bank[6][rows, 0:TOK], ACT.Copy).then_inc(o_hi, 1)

            def merge(w):
                f = FILLS[f"{w}.m"]

                def body(u):
                    split_hi(u)
                    high(u.j - 1)

                def high(m):
                    if m >= 0:
                        act.wait_ge(merged, KT * PASSES[w] + m + 1)
                        act.activation(h_hi[:, m, :], sums[:, 2 + m % 2, :], ACT.Copy, scale=0.5
                                       ).then_inc(h_hi_ready, 1)
                over_units(act, f"{w}.outs", body)
                high(KT - 1)

            def up(w):
                f = FFNS[w]

                def body(u):
                    split_hi(u)
                    at_least(act, hid_ready, 32 * f + u.j - 3, u.e)
                    copy_out(u, relu[:, u.j % 4, :], ACT.Relu)
                    at_least(act, evicted, u.s + 1, u.e)
                    act.activation(hidden_hi[:, bass.ds(u.index * TOK, TOK)], relu[:, u.j % 4, :],
                                   ACT.Square).then_inc(hid_hi_ready, 1)
                over_units(act, f"{w}.up", body, peel=f == 0)

            act.wait_ge(consts_in, 16 * 4)
            act.activation(cond_sig[:, :], V("c", n=2 * KT), ACT.Sigmoid).then_inc(cond_sig_ready, 1)
            for j in range(LEAD):
                split_hi(Unit("mod0", j), 0)
            act.wait_ge(cond_full_ready, 1)
            act.activation(cond_parts[:, :, 0:2], cond_full.rearrange("p (k c) -> p k c", c=2), ACT.Copy
                           ).then_inc(cond_hi_ready, 1)
            for l in range(DEPTH):
                for who in ("ctx", "x"):
                    for k in range(KT):
                        if l > 0:
                            act.wait_ge(evicted, FIRST[f"{who}{l - 1}.down"] + 4 * (k + 1))
                        square(f"{who}{l}.norm1", k, resid[who][:, k, :])

                def mod_rows_out(u):
                    if u.j % 2 == 1:
                        at_least(act, unit_done, u.s + 1, u.e)
                        act.activation(mod_rows, bank[u.bank][0:4, 0:2 * P], ACT.Copy).then_inc(evicted, 2)
                    split_hi(u, pair=True)
                over_units(act, f"mod{l}", mod_rows_out)
                act.wait_ge(mod_ready, 6 * l + 6)
                for who in ("ctx", "x"):
                    w = f"{who}{l}"
                    if w != "x0":
                        norm(f"{w}.norm1", 0, who, None, FIRST[f"{w}.kv" if w == "ctx1" else f"{w}.small"], KT)
                    if w == "ctx1":
                        for j, out in ((0, z_k), (1, ctx_v.rearrange("p t n -> p (t n)"))):
                            u = Unit("ctx1.kv", j)
                            split_hi(u)
                            copy_out(u, out)
                        act.wait_ge(evicted, u.s + 1)
                        square("ctx1.qk", 0, z_k)
                        continue
                    small(w)
                    attention(w)
                    merge(w)
                    first = FIRST[f"{w}.wo"]
                    for j in range(KT):
                        split_hi(Unit(f"{w}.wo", j))
                        if j > 0:
                            act.wait_ge(evicted, first + j)
                            square(f"{w}.norm2", j - 1, resid[who][:, j - 1, :])
                    norm(f"{w}.norm2", 1, who, lambda e, k: e.wait_ge(evicted, first + k + 1), FIRST[f"{w}.up"], KT - 1)
                    up(w)

                    def down(u):
                        split_hi(u)
                        if w == "ctx0" and isinstance(u.e, int) and u.j < KT:
                            modulated("x0.norm1", 0, "x", u.j)
                    if w == "ctx0":
                        h_free("x0.norm1", FIRST["ctx0.down"])
                    over_units(act, f"{w}.down", down, peel=w == "ctx0")

            def norm2(name, ready, before):
                for k in range(KT):
                    ready(k)
                    square(name, k, resid["x"][:, k, :])
                high(name, before)

            def high(name, before):
                act.wait_ge(unit_done, before)
                for k in range(KT):
                    high_tile(name, k)

            def high_tile(name, k):
                act.wait_ge(full_ready, KT * NORMS[name] + k + 1)
                act.activation(h_hi[:, k, :], full[:, k, :], ACT.Copy).then_inc(h_hi_ready, 1)

            def product_out(stage, group, bias=None):
                flat = scratch.rearrange("p k n -> p (k n)")
                r, _, _ = CHAINS[stage.split(".")[0] + (".n1" if "out" in stage else ".n3")]
                before = CHAIN_READS[stage]
                act.wait_ge(sums_ready, before)

                def body(u):
                    split_hi(u)
                    if u.j % group != group - 1:
                        return
                    at_least(act, unit_done, u.s + 1, u.e)
                    src = bank[u.bank if group == 1 else 4 + (u.j // group) % 2][:, 0:TOK]
                    m = (u.j // group) * TOK + u.e * (TOK // group)
                    b = bias(u.j) if bias else 0.0
                    act.activation(flat[:, bass.ds(m + KT * TOK, TOK)], src, ACT.Identity, bias=b)
                    tile = u.j // group
                    if tile > 1 or not isinstance(u.e, int):
                        at_least(act, square_used, (KT - 1) * PRODUCTS[stage] + tile - 1, u.turn * (RAW // group))
                    act.activation(squares[:, tile % 2, :], src, ACT.Square, bias=b).then_inc(evicted, group)
                over_units(act, stage, body, peel=True)

            def tanh_gate(u, n):
                if u.j >= 4:
                    act.wait_ge(evicted, u.s - 3)
                act.wait_ge(unit_done, u.s + 1)
                act.activation(relu[:, n % 4, :], bank[u.bank][:, 0:TOK], ACT.Tanh, scale=0.5
                               ).then_inc(tanh_ready, 1)

            def retention(b):
                n = RETS[b]
                if b == "b0":
                    act.wait_ge(angle_ready, 2)
                    for i, name in enumerate(("pos_cos", "pos_sin")):
                        act.activation(C(name, n=TOK), scaled[:, 6 + i, :], ACT.Sin).then_inc(sin_ready, 1)

                def raw(u):
                    split_hi(u)
                    copy_out(u, ret_raw[:, bass.ds(u.index * TOK, TOK)])
                over_units(act, f"{b}.qk", raw)
                if b == "b0":
                    act.activation(log_tmp[:, 0:16], V("decay", n=16), ACT.Abs).then_inc(gla_act, 1)
                    act.wait_ge(gla_act, 1)
                    act.activation(log_tmp[:, 16:32], log_tmp[:, 0:16], ACT.Exp, scale=-1.0).then_inc(gla_act, 1)

                def high_heads(h):
                    for k in range(4 * h, 4 * h + 4):
                        act.wait_ge(gated_full, 16 * n + k + 1)
                        act.activation(ret_hi[:, k * TOK:(k + 1) * TOK], scratch[:, 8 + k, :], ACT.Copy
                                       ).then_inc(ret_hi_ready, 1)

                def value(u):
                    split_hi(u, pair=True)
                    at_least(act, unit_done, u.s + 1, u.e)
                    at = (u.j - u.j % 2) * P + u.e * P
                    act.activation(ret_v[:, u.j % 2, bass.ds(at, 2 * P)], bank[u.bank][:, 0:2 * P], ACT.Copy
                                   ).then_inc(evicted, 1)
                over_units(act, f"{b}.v", value)
                for h in range(4):
                    g = 4 * n + h
                    us = [Unit(f"{b}.g", 4 * h + i) for i in range(4)]
                    split_hi(us[0])
                    act.wait_ge(decay_arg, g + 1)
                    act.activation(decay_m[:, h % 2, :], decay_m[:, h % 2, :], ACT.Exp).then_inc(decay_ready, 1)
                    tanh_gate(us[0], GATES[b] + 4 * h)
                    split_hi(us[1])
                    tanh_gate(us[1], GATES[b] + 4 * h + 1)
                    split_hi(us[2])
                    act.wait_ge(head_out, g + 1 + (4 if n else 0))
                    at_least(act, sums_ready, CHAINS[f"{b}.heads"][0] + h - 1)
                    for i in range(2):
                        cols = slice((4 * h + 2 * i) * TOK, (4 * h + 2 * i + 2) * TOK)
                        act.activation(ret_o[:, cols], bank[5 + i][:, :], ACT.Copy).then_inc(head_copied, 1)
                        k = 4 * (h % 2) + 2 * i
                        act.activation(squares[:, k:k + 2, :].rearrange("p a n -> p (a n)"), bank[5 + i][:, :],
                                       ACT.Square).then_inc(sq_ready, 2)
                    tanh_gate(us[2], GATES[b] + 4 * h + 2)
                    split_hi(us[3])
                    tanh_gate(us[3], GATES[b] + 4 * h + 3)
                    if h > 0:
                        high_heads(h - 1)
                high_heads(3)
                product_out(f"{b}.out", 2)

            def conformer(b):
                def body(u):
                    split_hi(u)
                    at_least(act, unit_done, u.s + 1, u.e)
                    half, pair = u.j % 2, u.j // 2
                    bias = vec[:, bass.ds(u.turn * 4 + VEC["b_in"] + half * KT + pair, 1)]
                    if half == 0:
                        at_least(act, glu_ready, pair - 1, u.turn * 4)
                        act.activation(relu[:, pair % 2, :], bank[u.bank][:, 0:TOK], ACT.Identity, bias=bias
                                       ).then_inc(evicted, 1)
                    else:
                        act.activation(relu[:, 2 + pair % 2, :], bank[u.bank][:, 0:TOK], ACT.Sigmoid, bias=bias
                                       ).then_inc(evicted, 1)
                        if pair > 1 or not isinstance(u.e, int):
                            at_least(act, conv_summed, pair - 1, u.turn * 4)
                        for t in range(PE_TAPS):
                            w = vec[:, bass.ds(u.turn * (4 * TAPS) + VEC["w_dw"] + pair * TAPS + DVE_TAPS + t, 1)]
                            d = act.activation(diagonals[:, pair % 2, t * P:(t + 1) * P], C("ident"), ACT.Copy, scale=w)
                        d.then_inc(diagonals_ready, 1)
                over_units(act, f"{b}.glu", body, peel=True)
                r, _, _ = CHAINS[f"{b}.var"]
                for k in range(KT):
                    act.wait_ge(centred, k + 1)
                    square(f"{b}.var", k, dw[:, k, :])
                act.wait_ge(unit_done, FIRST[f"{b}.out"])
                for k in range(KT):
                    act.wait_ge(ln_scaled, k + 1)
                    gain, bias = V("ln_gain", k), V("ln_bias", k)
                    act.activation(squares[:, k, :], scaled[:, k, :], ACT.Identity, bias=bias, scale=gain)
                    act.activation(glu[:, k, 0:TOK], scaled[:, k, :], ACT.Sigmoid, bias=bias, scale=gain
                                   ).then_inc(silu_in, 1)
                    if k > 1:
                        high_tile(f"{b}.y", k - 2)
                high_tile(f"{b}.y", KT - 2)
                high_tile(f"{b}.y", KT - 1)
                product_out(f"{b}.out", 1, lambda j: V("b_out", j))

            def gla(b):
                for d in range(2):
                    u = Unit(f"{b}.gate", d)
                    split_hi(u)
                    act.wait_ge(unit_done, u.s + 1)
                    rows = slice(32 * d, 32 * d + 32)
                    act.activation(gla_low[rows, :], bank[u.bank][rows, 0:TOK], ACT.Copy).then_inc(evicted, 1)
                for j in range(8):
                    u = Unit(f"{b}.qk", j)
                    split_hi(u)
                    if j == 2:
                        act.wait_ge(gla_dve, 1)
                        act.activation(cum_g, log_g, ACT.Abs).then_inc(gla_act, 1)
                        act.wait_ge(gla_act, 3)
                        act.activation(cum_g, cum_g, ACT.Exp, scale=-1.0).then_inc(gla_act, 1)
                        act.wait_ge(gla_act, 4)
                        act.activation(cum_g, cum_g, ACT.Ln, bias=1.0).then_inc(gla_act, 1)
                    out = (gla_q if j < 4 else gla_k)[:, (j % 4) * TOK:(j % 4 + 1) * TOK]
                    copy_out(u, out, scale=P ** -0.5 if j < 4 else 1.0)
                for j in range(8):
                    u = Unit(f"{b}.v", j)
                    split_hi(u, pair=True)
                    if j in (1, 4):
                        d = 0 if j == 1 else 1
                        act.wait_ge(gla_dve, 3 + d)
                        a, e = GLA_ARG[d]
                        for i, (arg, sign) in enumerate(((a, 1.0), (a, -1.0), (e, 1.0))):
                            act.activation(decayed[:, 3 * d + i, :], arg, ACT.Exp, scale=sign / 16.0
                                           ).then_inc(gla_act, 1)
                    if j == 4:
                        ends = cum_g.rearrange("p (c n) -> p c n", n=CHUNK)[:, :, CHUNK - 1]
                        act.activation(decay_end[:, :], ends, ACT.Exp, scale=1.0 / 16.0).then_inc(gla_act, 1)
                    act.wait_ge(unit_done, u.s + 1)
                    act.activation(gla_v[:, j % 2, (j - j % 2) * P:(j - j % 2 + 2) * P], bank[u.bank][:, 0:2 * P],
                                   ACT.Copy).then_inc(evicted, 1)
                act.wait_ge(ke_out, 1)
                for i in range(4):
                    m = act.activation(ke_tok[:, 4 * i:4 * i + 4, :].rearrange("p a n -> p (a n)"),
                                       bank[4 + i][:, :], ACT.Copy)
                m.then_inc(state_in, 1)
                for h in range(4):
                    us = [Unit(f"{b}.r", 2 * h + i) for i in range(2)]
                    split_hi(us[0])
                    tanh_gate(us[0], GATES[b] + 2 * h)
                    split_hi(us[1])
                    act.wait_ge(head_out, 4 + h + 1)
                    act.activation(full[:, 2 * h:2 * h + 2, :].rearrange("p a n -> p (a n)"), bank[4][:, :], ACT.Copy
                                   ).then_inc(gla_o, 1)
                    act.activation(squares[:, 2 * h:2 * h + 2, :].rearrange("p a n -> p (a n)"), bank[4][:, :],
                                   ACT.Square).then_inc(sq_ready, 2)
                    tanh_gate(us[1], GATES[b] + 2 * h + 1)
                high(f"{b}.y", FIRST[f"{b}.out"])
                product_out(f"{b}.out", 1)

            act.wait_ge(con2_in, 32)
            for i in range(4):
                b = f"b{i}"
                if i == 0:
                    norm2(f"{b}.n0", lambda k: act.wait_ge(evicted, FIRST["x1.down"] + 4 * (k + 1)), FIRST["b0.qk"])
                else:
                    norm2(f"{b}.n0", lambda k: act.wait_ge(updated, KT * (2 * i - 1) + k + 1), FIRST[f"{b}.{FIRST_PART[i % 3]}"])
                (retention, conformer, gla)[i % 3](b)
                norm2(f"{b}.n2", lambda k: act.wait_ge(updated, KT * 2 * i + k + 1), FIRST[f"{b}.up"])
                up(b)
                product_out(f"{b}.down", 4)

        @block.vector
        def _(dve):
            chained = [0]

            def link(ins):
                chained[0] += 1
                ins.then_inc(dve_chain, 1)
                dve.wait_ge(dve_chain, chained[0])

            def split_lo(u, lead=LEAD):
                if isinstance(u.e, int) and u.s + lead >= TOTAL:
                    return
                at_least(dve, hi_ready, u.s + lead + 1, u.e)
                w = u.split(lead)
                dve.tensor_tensor(w_lo[:, w, :], w_raw[:, u.raw(lead), :], w_hi[:, w, :].bitcast(F32),
                                  ALU.subtract).then_inc(lo_ready, 1)

            def inverse_rms(name, cols, parts=1, i=0):
                mean(name, cols, cols, EPS / parts, i)
                broadcast_done(name, i)

            def mean(name, out, cols, eps=EPS, i=0):
                dve.wait_ge(sums_ready, CHAINS[name][0] + i + 1)
                dve.tensor_scalar(mean_sq[:, out], bank[7][:, cols], eps, None, ALU.add).then_inc(mean_ready, 1)

            def broadcast_done(name, i=0):
                dve.wait_ge(bcast_ready, BROADCASTS.get(name, CHAINS[name][2]) + i + 1)

            def row_rms(name):
                inverse_rms(name, slice(0, TT))

            ROW = bank[6][:, 0:TOK]
            halves = lambda j: bank[4 + j // 2][:, (j % 2) * TOK:(j % 2 + 1) * TOK]

            def h_low(f, k):
                dve.wait_ge(h_hi_ready, KT * f + k + 1)
                dve.tensor_tensor(h_lo[:, k, :], full[:, k, :], h_hi[:, k, :].bitcast(F32), ALU.subtract
                                  ).then_inc(h_lo_ready, 1)

            def scale_tile(who, k):
                dve.tensor_tensor(scaled[:, k, :], ROW, resid[who][:, k, :], ALU.mult).then_inc(norm_ready, 1)

            def norm(name, who):
                f = FILLS[name]
                at_least(dve, h_hi_ready, KT * f)
                if "norm1" in name:
                    broadcast_done(name)
                else:
                    row_rms(name)
                for k in range(KT):
                    scale_tile(who, k)
                    if k > 1:
                        h_low(f, k - 2)
                h_low(f, KT - 2)
                h_low(f, KT - 1)

            def qk_normed(w, n_tiles, out):
                l = w[-1]
                broadcast_done(f"{w}.qk")
                for i in range(n_tiles):
                    src = z_k if i == 0 else z_q[:, i - 1, :]
                    q = dve.scalar_tensor_tensor(out=out(i), in0=src, scalar=V(f"g_k{l}" if i == 0 else f"g_q{l}"),
                                                 in1=halves(i), op0=ALU.mult, op1=ALU.mult)
                    q.then_inc(qk_norm_ready, 1)

            def small(w):
                n = PASSES[w]
                l = w[-1]
                for j in range(14):
                    split_lo(Unit(f"{w}.small", j))
                    if j == 7:
                        mean(f"{w}.qk", slice(0, 20), slice(0, 20))
                    if j == 9:
                        if w == "ctx0":
                            qk_normed(w, 5, lambda i: ctx_k[:, :] if i == 0 else qk[:, i, :])
                        else:
                            qk_normed(w, 5, lambda i: qk_n[:, i, :])
                    if j == 11 and w != "ctx0":
                        dve.wait_ge(rot_ready, n)
                        for i in range(5):
                            b = bank[4 + i // 2][:, (i % 2) * TOK:(i % 2 + 1) * TOK]
                            m = dve.tensor_tensor(scaled[:, i, :], b, C("rope_sin", n=TOK), ALU.mult)
                        link(m)
                        dve.wait_ge(rope_part, 5 * n)
                        for i in range(5):
                            q = dve.tensor_tensor(qk[:, i, :], scaled[:, i, :], full[:, i, :], ALU.add)
                        q.then_inc(qk_ready, 1)
                dve.wait_ge(four_hi, n + 1)
                for f in range(2):
                    dve.tensor_tensor(y_lo[:, 2 + f, :], bank[7][:, f * TOK:(f + 1) * TOK],
                                      y_hi[:, 2 + f, :].bitcast(F32), ALU.subtract).then_inc(y_ready, 1)
                dve.wait_ge(evicted, FIRST[f"{w}.small"] + 14)
                if w != "ctx0":
                    dve.wait_ge(rope_part, 5 * n)
                    dve.wait_ge(qk_ready, n)
                link(dve.memset(conv_in[:, :, 0:1], 0.0))
                link(dve.memset(conv_in[:, :, TOK + 1:TOK + 2], 0.0))
                link(dve.tensor_tensor(conv_in[:, :, 1:TOK + 1], z_conv[:, 2:4, :], z_conv[:, 4:6, :], ALU.mult))
                for j in range(3):
                    for f in range(2):
                        tap = conv_in[:, f, j:j + TOK]
                        wt = V(f"w_conv{l}", 2 * j + f)
                        if j == 0:
                            m = dve.tensor_scalar(scaled[:, f, :], tap, wt, None, ALU.mult)
                        else:
                            m = dve.scalar_tensor_tensor(out=scaled[:, f, :], in0=tap, scalar=wt,
                                                         in1=scaled[:, f, :], op0=ALU.mult, op1=ALU.add)
                    link(m)
                for f in range(2):
                    dve.tensor_tensor(full[:, f, :], scaled[:, f, :], z_conv[:, f, :], ALU.mult
                                      ).then_inc(y_full_ready, 1)
                for f in range(2):
                    dve.wait_ge(conv_hi, 2 * n + f + 1)
                    dve.tensor_tensor(y_lo[:, f, :], full[:, f, :], y_hi[:, f, :].bitcast(F32), ALU.subtract
                                      ).then_inc(y_ready, 1)

            def attention(w):
                n = PASSES[w]
                keys = 2 if w == "ctx0" else 4
                for a in range(HEADS):
                    g = HEADS * n + a
                    units = [Unit(f"{w}.gates", 3 * a + i) for i in range(3)]
                    for t in range(TT):
                        dve.wait_ge(s_ready, 2 * g + t + 1)
                        link(dve.tensor_reduce(row_max[:, t:t + 1], bank[4 + t][:, 0:keys * P], AX_X, ALU.max))
                        dve.tensor_scalar(neg_max[:, t:t + 1], row_max[:, t:t + 1], -(HD ** -0.5), None, ALU.mult
                                          ).then_inc(max_ready, 1)
                    split_lo(units[0])
                    for t in range(TT):
                        dve.wait_ge(exp_ready, 2 * g + t + 1)
                        link(dve.reciprocal(inv_sum[:, t:t + 1], row_sum[:, t:t + 1]))
                        dve.tensor_scalar(prob[:, t, 0:keys * P], prob[:, t, 0:keys * P], inv_sum[:, t:t + 1],
                                          None, ALU.mult).then_inc(p_ready, 1)
                    split_lo(units[1])
                    dve.wait_ge(pt_ready, g + 1)
                    if keys == 4:
                        dve.tensor_copy(prob_t[:, 2:4, :].rearrange("p a n -> p (a n)"), bank[7][:, :]
                                        ).then_inc(pt_dve, 1)
                    split_lo(units[2])
                    rows = slice((a % 2) * HD, (a % 2) * HD + HD)
                    dve.wait_ge(o_hi, g + 1)
                    dve.tensor_tensor(y_lo[rows, 4 + a // 2, :], bank[6][rows, 0:TOK],
                                      y_hi[rows, 4 + a // 2, :].bitcast(F32), ALU.subtract).then_inc(o_lo, 1)

            def merge(w):
                n = PASSES[w]

                def body(u):
                    split_lo(u)
                    at_least(dve, unit_done, u.s + 1, u.e)
                    m = u.j
                    b = bank[u.bank]
                    at_least(dve, merged, KT * n + m - 1)
                    for i, p in enumerate((b[:, 0:TOK], b[:, TOK:2 * TOK], bank[4 + u.s % 2][:, 0:TOK])):
                        t = dve.scalar_tensor_tensor(out=terms[:, m % 2, i, :], in0=gates[:, i * KT + m, :],
                                                     scalar=1.0, in1=p, op0=ALU.add, op1=ALU.mult)
                    t.then_inc(evicted, 1)
                    low(m - 1)

                def low(m):
                    if m >= 0:
                        dve.wait_ge(h_hi_ready, KT * FILLS[f"{w}.m"] + m + 1)
                        dve.scalar_tensor_tensor(out=h_lo[:, m, :], in0=sums[:, 2 + m % 2, :], scalar=0.5,
                                                 in1=h_hi[:, m, :].bitcast(F32), op0=ALU.mult, op1=ALU.subtract
                                                 ).then_inc(h_lo_ready, 1)
                over_units(dve, f"{w}.outs", body)
                low(KT - 1)

            def add_gated(w, who, l):
                c = 0 if who == "x" else 1

                def body(u):
                    split_lo(u)
                    at_least(dve, unit_done, u.s + 1, u.e)
                    r = resid[who][:, u.j, :]
                    dve.scalar_tensor_tensor(out=r, in0=bank[u.bank][:, 0:TOK], scalar=mod[:, 2 * KT + u.j, c:c + 1],
                                             in1=r, op0=ALU.mult, op1=ALU.add).then_inc(evicted, 1)
                over_units(dve, f"{w}.wo", body)

            def up(w):
                f = FFNS[w]

                def body(u):
                    split_lo(u)
                    at_least(dve, evicted, u.s + 1, u.e)
                    dve.tensor_tensor(relu_sq[:, u.j % 2, :], relu[:, u.j % 4, :], relu[:, u.j % 4, :], ALU.mult
                                      ).then_inc(hid_sq_ready, 1)
                    at_least(dve, hid_sq_ready, 32 * f + u.j + 1, u.e)
                    at_least(dve, hid_hi_ready, 32 * f + u.j + 1, u.e)
                    cols = bass.ds(u.index * TOK, TOK)
                    dve.tensor_tensor(hidden_lo[:, cols], relu_sq[:, u.j % 2, :], hidden_hi[:, cols].bitcast(F32),
                                      ALU.subtract).then_inc(hid_ready, 1)
                over_units(dve, f"{w}.up", body)

            def down(w, who):
                c = 0 if who == "x" else 1
                flat = resid[who].rearrange("p k n -> p (k n)")
                mflat = mod.rearrange("p m c -> p (m c)")

                def body(u):
                    split_lo(u)
                    if w == "ctx0" and isinstance(u.e, int) and u.j < KT:
                        scale_tile("x", u.j)
                        f = FILLS["x0.norm1"]
                        if u.j > 0:
                            h_low(f, u.j - 1)
                        if u.j == KT - 1:
                            h_low(f, u.j)
                    if u.j % 4 != 3:
                        return
                    at_least(dve, unit_done, u.s + 1, u.e)
                    m4 = u.e + (u.j // 4) * 4
                    r = flat[:, bass.ds(m4 * (TOK // 4), TOK)]
                    if isinstance(u.e, int):
                        m = m4 // 4
                        g = mflat[:, (5 * KT + m) * 2 + c:(5 * KT + m) * 2 + c + 1]
                    else:
                        g = mflat[:, bass.ds(u.turn * 4 + (5 * KT + u.j // 4) * 2 + c, 1)]
                    dve.scalar_tensor_tensor(out=r, in0=bank[4 + (u.j // 4) % 2][:, 0:TOK], scalar=g,
                                             in1=r, op0=ALU.mult, op1=ALU.add).then_inc(evicted, 4)
                if w == "ctx0":
                    at_least(dve, h_hi_ready, KT * FILLS["x0.norm1"])
                    broadcast_done("x0.norm1")
                over_units(dve, f"{w}.down", body, peel=w == "ctx0")

            dve.wait_ge(consts_in, 16 * 4)
            dve.wait_ge(cond_sig_ready, 1)
            dve.tensor_tensor(cond_full[:, :], cond_sig[:, :], V("c", n=2 * KT), ALU.mult).then_inc(cond_full_ready, 1)
            dve.wait_ge(cond_hi_ready, 1)
            dve.tensor_tensor(cond_parts[:, :, 2:4], cond_full.rearrange("p (k c) -> p k c", c=2),
                              cond_parts[:, :, 0:2].bitcast(F32), ALU.subtract).then_inc(cond_ready, 1)
            for j in range(LEAD):
                split_lo(Unit("mod0", j), 0)
            for l in range(DEPTH):
                for who in ("ctx", "x"):
                    mean(f"{who}{l}.norm1", slice(EARLY[who], EARLY[who] + TT), slice(0, TT))

                def mod_out(u):
                    split_lo(u)
                    if u.j % 2 == 0:
                        return
                    pair = l * NM // 2 + u.j // 2
                    at_least(dve, mod_cols_ready, pair + 1, u.turn * 4)
                    dve.tensor_copy(mod_raw[:, bass.ds((u.index - 1) * 2, 4)], bank[4 + pair % 2][:, 0:4]
                                    ).then_inc(mod_cols_out, 1)
                over_units(dve, f"mod{l}", mod_out)
                dve.wait_ge(mod_cols_out, (l + 1) * NM // 2)
                raw = tiles(mod_raw[:, :], NM)
                for c in range(2):
                    dve.tensor_tensor(mod[:, :, c], raw[:, :, c], V(f"b_mod{l}", n=NM), ALU.add
                                      ).then_inc(mod_ready, 1)
                dve.wait_ge(mod_ready, 6 * l + 2)
                for which in range(2):
                    for c in range(2):
                        dve.scalar_tensor_tensor(out=mod_gain[:, 2 * which + c, :],
                                                 in0=mod[:, (which * 3 + 1) * KT:(which * 3 + 2) * KT, c],
                                                 scalar=1.0, in1=V(f"g{which + 1}_{l}", n=KT), op0=ALU.add,
                                                 op1=ALU.mult).then_inc(mod_ready, 1)
                for who in ("ctx", "x"):
                    w = f"{who}{l}"
                    if w != "x0":
                        norm(f"{w}.norm1", who)
                    if w == "ctx1":
                        for j in range(2):
                            split_lo(Unit("ctx1.kv", j))
                        inverse_rms("ctx1.qk", slice(0, 4))
                        link(dve.scalar_tensor_tensor(out=ctx_k[:, :], in0=z_k, scalar=V("g_k1"),
                                                      in1=halves(0), op0=ALU.mult, op1=ALU.mult))
                        continue
                    small(w)
                    attention(w)
                    merge(w)
                    add_gated(w, who, l)
                    norm(f"{w}.norm2", who)
                    up(w)
                    down(w, who)

            def norm2(name, gain):
                f = FILLS[name]
                dve.wait_ge(h_hi_ready, KT * f)
                row_rms(name)
                for k in range(KT):
                    dve.scalar_tensor_tensor(out=full[:, k, :], in0=resid["x"][:, k, :], scalar=V("gains", gain * KT + k),
                                             in1=ROW, op0=ALU.mult, op1=ALU.mult
                                             ).then_inc(full_ready, 1)
                    if k > 0:
                        h_low(f, k - 1)
                h_low(f, KT - 1)

            normed = [0]

            def post(name, gain):
                row_rms(name)

                def add(k):
                    dve.wait_ge(product_normed, normed[0] + k + 1)
                    x = resid["x"][:, k, :]
                    dve.tensor_tensor(x, x, scaled[:, k, :], ALU.add).then_inc(updated, 1)
                for k in range(KT):
                    dve.scalar_tensor_tensor(out=scaled[:, k, :], in0=scaled[:, k, :],
                                             scalar=V("gains", gain * KT + k), in1=ROW,
                                             op0=ALU.mult, op1=ALU.mult).then_inc(product_normed, 1)
                    if k > 0:
                        add(k - 1)
                add(KT - 1)
                normed[0] += KT

            def angles():
                s = lambda i: scaled[:, i, :]
                magic = 1.5 * 2 ** 23
                link(dve.tensor_copy(s(1), s(0).bitcast(I32)))
                link(dve.tensor_scalar(s(2), s(1), V("inv_freq"), None, ALU.mult))
                for i, quarter in ((6, 0.25), (7, 0.0)):
                    link(dve.tensor_scalar(s(3), s(2), 1.0 / (2 * np.pi), quarter, ALU.mult, ALU.add))
                    link(dve.tensor_scalar(s(3), s(3), magic, None, ALU.add))
                    link(dve.tensor_scalar(s(3), s(3), magic, None, ALU.subtract))
                    src = s(2)
                    for part in TWO_PI:
                        link(dve.scalar_tensor_tensor(out=s(i), in0=s(3), scalar=-part, in1=src,
                                                      op0=ALU.mult, op1=ALU.add))
                        src = s(i)
                    link(dve.tensor_scalar(s(i), s(i), quarter * 2 * np.pi, 3.1415925, ALU.add, ALU.min))
                    dve.tensor_scalar(s(i), s(i), -3.1415925, None, ALU.max).then_inc(angle_ready, 1)

            def log_decays():
                dve.wait_ge(gla_act, 2)
                e, s, q, a = (log_tmp[:, 16:32], log_tmp[:, 0:16], log_tmp[:, 32:48], log_decay[:, :])
                link(dve.tensor_scalar(s, e, 2.0, None, ALU.add))
                link(dve.reciprocal(s, s))
                link(dve.tensor_tensor(s, s, e, ALU.mult))
                link(dve.tensor_tensor(q, s, s, ALU.mult))
                link(dve.memset(a, 1.0 / 17))
                for n in range(15, 0, -2):
                    link(dve.tensor_tensor(a, a, q, ALU.mult))
                    link(dve.tensor_scalar(a, a, 1.0 / n, None, ALU.add))
                link(dve.scalar_tensor_tensor(out=a, in0=a, scalar=-2.0, in1=s, op0=ALU.mult, op1=ALU.mult))
                link(dve.tensor_scalar(e, V("decay", n=16), 0.0, None, ALU.min))
                link(dve.tensor_tensor(a, a, e, ALU.add))

            def silu_gate(u, n, out):
                dve.wait_ge(tanh_ready, n + 1)
                dve.scalar_tensor_tensor(out=out, in0=relu[:, n % 4, :], scalar=1.0, in1=bank[u.bank][:, 0:TOK],
                                         op0=ALU.add, op1=ALU.mult).then_inc(evicted, 1)

            def retention(b):
                n, j = RETS[b], int(b[1]) // 3
                if b == "b0":
                    angles()
                over_units(dve, f"{b}.qk", split_lo)
                if b == "b0":
                    log_decays()
                if b == "b0":
                    dve.wait_ge(sin_ready, 2)
                dve.wait_ge(evicted, FIRST[f"{b}.v"])

                def value(u):
                    split_lo(u)
                    if u.j % 2 == 0:
                        return
                    pair, at = u.j // 2, (u.j // 2) * 2 * TOK + u.e * TOK
                    t1, t2 = ret_raw[:, bass.ds(at, TOK)], ret_raw[:, bass.ds(at + TOK, TOK)]
                    ring_at = 4 * (pair % 2)
                    at_least(dve, rot_a, 8 * n + pair + 1, u.turn * 4)
                    dve.tensor_tensor(squares[:, ring_at + 2, :], t2, C("pos_sin", n=TOK), ALU.mult)
                    dve.tensor_tensor(squares[:, ring_at + 3, :], t1, C("pos_sin", n=TOK), ALU.mult
                                      ).then_inc(sin_part, 1)
                    at_least(dve, sin_part, 8 * n + pair + 1, u.turn * 4)
                    dve.tensor_tensor(ret_rot[:, bass.ds(at, TOK)], squares[:, ring_at, :], squares[:, ring_at + 2, :],
                                      ALU.subtract)
                    dve.tensor_tensor(ret_rot[:, bass.ds(at + TOK, TOK)], squares[:, ring_at + 1, :],
                                      squares[:, ring_at + 3, :], ALU.add).then_inc(rot_done, 1)
                over_units(dve, f"{b}.v", value)
                def gated_head(h):
                    inverse_rms(f"{b}.heads", slice(2 * (h % 2), 2 * (h % 2) + 2), parts=2, i=h)
                    for k in range(4 * h, 4 * h + 4):
                        x = scratch[:, 8 + k, :]
                        dve.wait_ge(gated, 16 * n + k + 1)
                        dve.scalar_tensor_tensor(out=x, in0=x, scalar=0.5 * 2 ** -0.5, in1=bank[7][:, TOK:2 * TOK],
                                                 op0=ALU.mult, op1=ALU.mult).then_inc(gated_full, 1)
                        if k % 4 > 0:
                            ret_low(k - 1)
                    ret_low(4 * h + 3)

                def ret_low(k):
                    dve.wait_ge(ret_hi_ready, 16 * n + k + 1)
                    dve.tensor_tensor(ret_lo_tile(k), scratch[:, 8 + k, :],
                                      ret_hi[:, k * TOK:(k + 1) * TOK].bitcast(F32), ALU.subtract
                                      ).then_inc(ret_ready, 1)

                for h in range(4):
                    g = 4 * n + h
                    us = [Unit(f"{b}.g", 4 * h + i) for i in range(4)]
                    fwd, bwd = (log_decay[:, (2 * j + d) * 4 + h:(2 * j + d) * 4 + h + 1] for d in range(2))
                    link(dve.tensor_scalar(decay_m[:, h % 2, :], C("after", n=TT * TOK), fwd, None, ALU.mult))
                    dve.scalar_tensor_tensor(out=decay_m[:, h % 2, :], in0=C("before", n=TT * TOK), scalar=bwd,
                                             in1=decay_m[:, h % 2, :], op0=ALU.mult, op1=ALU.add
                                             ).then_inc(decay_arg, 1)
                    split_lo(us[0])
                    dve.wait_ge(decay_ready, g + 1)
                    dve.wait_ge(scores_ready, g + 1 + (4 if n else 0))
                    dve.scalar_tensor_tensor(out=scores[:, h % 2, :], in0=bank[4][:, :], scalar=1.0 / 16,
                                             in1=decay_m[:, h % 2, :], op0=ALU.mult, op1=ALU.mult
                                             ).then_inc(weighted, 1)
                    g0 = GATES[b] + 4 * h
                    silu_gate(us[0], g0, scratch[:, 8 + 4 * h, :])
                    for i in range(1, 4):
                        split_lo(us[i])
                        silu_gate(us[i], g0 + i, scratch[:, 8 + 4 * h + i, :])
                    if h > 0:
                        gated_head(h - 1)
                gated_head(3)
                over_units(dve, f"{b}.out", split_lo)

            def conformer(b):
                dve.memset(glu[:, :, 0:15], 0.0).then_inc(pad_ready, 1)
                dve.memset(glu[:, :, TOK + 15:TOK + 30], 0.0).then_inc(pad_ready, 1)
                dve.wait_ge(pad_ready, 2)
                wide = TOK + 30

                def body(u):
                    split_lo(u)
                    if u.j % 2 == 0:
                        return
                    pair = u.j // 2
                    at_least(dve, evicted, u.s + 1, u.e)
                    tile = u.turn * 4 + pair
                    at = u.turn * (4 * wide) + pair * wide
                    dve.tensor_tensor(conv_t[:, bass.ds(at + 15, TOK)], relu[:, pair % 2, :], relu[:, 2 + pair % 2, :],
                                      ALU.mult).then_inc(glu_ready, 1)
                    at_least(dve, glu_ready, pair + 1, u.turn * 4)
                    acc = dw_out[:, bass.ds(u.turn * (4 * TOK) + pair * TOK, TOK)]
                    sums_of = (acc, sum_ring[:, 0:2, :].rearrange("p a n -> p (a n)"))
                    done = lambda i: at_least(dve, tap, pair * (DVE_TAPS + 1) + i, u.turn * (4 * (DVE_TAPS + 1)))
                    for t in range(DVE_TAPS):
                        w = vec[:, bass.ds(u.turn * (4 * TAPS) + VEC["w_dw"] + pair * TAPS + t, 1)]
                        src, out = conv_t[:, bass.ds(at + t, TOK)], sums_of[t % 2]
                        if t == 0:
                            m = dve.tensor_scalar(out, src, w, vec[:, bass.ds(u.turn * 4 + VEC["b_dw"] + pair, 1)],
                                                  ALU.mult, ALU.add)
                        elif t == 1:
                            m = dve.tensor_scalar(out, src, w, None, ALU.mult)
                        else:
                            done(t - 1)
                            m = dve.scalar_tensor_tensor(out=out, in0=src, scalar=w, in1=out, op0=ALU.mult, op1=ALU.add)
                        m.then_inc(tap, 1)
                    done(DVE_TAPS)
                    dve.tensor_tensor(acc, acc, sums_of[1], ALU.add).then_inc(tap, 1)
                    done(DVE_TAPS + 1)
                    at_least(dve, conv_summed, pair + 1, u.turn * 4)
                    dve.tensor_tensor(acc, acc, bank[4 + pair % 2][:, 0:TOK], ALU.add).then_inc(dw_ready, 1)
                over_units(dve, f"{b}.glu", body)
                r, _, _ = CHAINS[f"{b}.mean"]
                dve.wait_ge(sums_ready, r + 1)
                for k in range(KT):
                    dve.tensor_tensor(dw[:, k, :], dw[:, k, :], bank[7][:, 0:TOK], ALU.subtract).then_inc(centred, 1)
                dve.wait_ge(centred, KT)
                dve.tensor_copy(row_max[:, 0:1], row_max[:, 1:2]).then_inc(mean_ready, 1)
                row_rms(f"{b}.var")
                def silu(k):
                    dve.wait_ge(silu_in, k + 1)
                    dve.tensor_tensor(full[:, k, :], squares[:, k, :], glu[:, k, 0:TOK], ALU.mult).then_inc(full_ready, 1)

                f = FILLS[f"{b}.y"]
                for k in range(KT + 4):
                    if k < KT:
                        dve.tensor_tensor(scaled[:, k, :], ROW, dw[:, k, :], ALU.mult).then_inc(ln_scaled, 1)
                    if 2 <= k < KT + 2:
                        silu(k - 2)
                    if k >= 4:
                        h_low(f, k - 4)
                over_units(dve, f"{b}.out", split_lo)

            def gla(b):
                for d in range(2):
                    split_lo(Unit(f"{b}.gate", d))
                dve.wait_ge(logits_ready, 1)
                for i in range(8):
                    m = dve.tensor_scalar(log_g[:, i * TOK:(i + 1) * TOK], bank[4 + i // 2][:, (i % 2) * TOK:(i % 2 + 1) * TOK],
                                          V("gate_b", i), None, ALU.add)
                m.then_inc(gla_dve, 1)
                reset = squares.rearrange("p k n -> p (k n)")
                link(dve.memset(reset, 1.0))
                link(dve.memset(reset.rearrange("p (c n) -> p c n", n=CHUNK)[:, :, 0:1], 0.0))
                c3, l3 = (x.rearrange("p (c n) -> p c n", n=CHUNK) for x in (cum_g, log_g))
                s3 = reset.rearrange("p (c n) -> p c n", n=CHUNK)
                rest = lambda d: c3[:, 16 * d:16 * d + 16, CHUNK - 1:CHUNK].broadcast_to([P, 16, CHUNK])
                for j in range(8):
                    split_lo(Unit(f"{b}.qk", j))
                    if j == 3:
                        dve.wait_ge(gla_act, 5)
                        link(dve.scalar_tensor_tensor(out=log_g, in0=log_g, scalar=0.0, in1=cum_g, op0=ALU.min,
                                                      op1=ALU.subtract))
                    if j == 4:
                        dve.tensor_tensor_scan(cum_g, reset, log_g, 0.0, ALU.mult, ALU.add).then_inc(gla_dve, 1)
                    if j == 5:
                        dve.wait_ge(gla_dve, 2)
                        dve.tensor_tensor(s3[:, 0:16, :], rest(0), c3[:, 0:16, :], ALU.subtract).then_inc(gla_dve, 1)
                    if j == 6:
                        link(dve.tensor_tensor(s3[:, 16:32, :], rest(1), c3[:, 16:32, :], ALU.subtract))
                        link(dve.tensor_tensor(s3[:, 16:32, :], s3[:, 16:32, :], l3[:, 16:32, :], ALU.add))
                        dve.tensor_tensor(l3[:, 16:32, :], c3[:, 16:32, :], l3[:, 16:32, :], ALU.subtract
                                          ).then_inc(gla_dve, 1)
                dve.wait_ge(evicted, FIRST[f"{b}.v"])
                for j in range(8):
                    split_lo(Unit(f"{b}.v", j))
                    if j in (2, 5):
                        d = 0 if j == 2 else 1
                        dve.wait_ge(gla_act, 5 + 3 * (d + 1))
                        for i, x in ((2, gla_k), (0, gla_q), (1, gla_k)):
                            m = dve.tensor_tensor(decayed[:, 3 * d + i, :], decayed[:, 3 * d + i, :], x, ALU.mult)
                        m.then_inc(ke_ready, 1)
                dve.wait_ge(gla_act, 12)
                link(dve.memset(gla_s, 0.0))
                for h in range(4):
                    us = [Unit(f"{b}.r", 2 * h + i) for i in range(2)]
                    split_lo(us[0])
                    dve.wait_ge(scores_ready, 4 + h + 1)
                    dve.wait_ge(added_ready, h + 1)
                    dve.wait_ge(head_out, 4 + h)
                    for d, name in enumerate(("mask_fwd", "mask_bwd")):
                        m = C(name, n=CHUNK).unsqueeze(1).broadcast_to([P, 2, CHUNK])
                        out = sum_ring[:, d, :].rearrange("p (a n) -> p a n", a=2)
                        x = dve.tensor_tensor(out, bank[7][:, d * P:(d + 1) * P].rearrange("p (a n) -> p a n", a=2), m,
                                              ALU.mult)
                    link(x)
                    for i in range(2):
                        rows = slice(i * CHUNK, (i + 1) * CHUNK)
                        f3, b3 = (sum_ring[rows, d, :].rearrange("p (a n) -> p a n", a=2) for d in range(2))
                        x = dve.tensor_tensor(gla_s[rows, :, i * CHUNK:(i + 1) * CHUNK], f3, b3, ALU.add)
                    link(x)
                    for i in range(3):
                        for d in range(2):
                            j3 = 3 * d + i
                            u_ps = added(j3)
                            if i == 0:
                                m = dve.tensor_copy(gla_state[:, j3, :], u_ps)
                            else:
                                c = i if d == 0 else 3 - i
                                at = (4 * d + h) * 4 + c
                                m = dve.scalar_tensor_tensor(out=gla_state[:, j3, :], in0=gla_state[:, j3 - 1, :],
                                                             scalar=decay_end[:, at:at + 1], in1=u_ps, op0=ALU.mult,
                                                             op1=ALU.add)
                        if i < 2:
                            link(m)
                    m.then_inc(state_ready, 1)
                    silu_gate(us[0], GATES[b] + 2 * h, scaled[:, 2 * h, :])
                    split_lo(us[1])
                    silu_gate(us[1], GATES[b] + 2 * h + 1, scaled[:, 2 * h + 1, :])
                inverse_rms(f"{b}.heads", slice(0, 8), parts=4)
                f = FILLS[f"{b}.y"]
                for k in range(KT + 3):
                    if k < KT:
                        dve.scalar_tensor_tensor(out=full[:, k, :], in0=full[:, k, :], scalar=V("gla_gain", k % 2),
                                                 in1=halves(k // 2), op0=ALU.mult, op1=ALU.mult
                                                 ).then_inc(head_normed, 1)
                    if 1 <= k < KT + 1:
                        dve.wait_ge(head_normed, k)
                        dve.scalar_tensor_tensor(out=full[:, k - 1, :], in0=full[:, k - 1, :], scalar=0.25,
                                                 in1=scaled[:, k - 1, :], op0=ALU.mult, op1=ALU.mult
                                                 ).then_inc(full_ready, 1)
                    if k >= 3:
                        h_low(f, k - 3)
                over_units(dve, f"{b}.out", split_lo)

            dve.wait_ge(con2_in, 32)
            for i in range(4):
                b = f"b{i}"
                norm2(f"{b}.n0", 4 * i)
                (retention, conformer, gla)[i % 3](b)
                post(f"{b}.n1", 4 * i + 1)
                norm2(f"{b}.n2", 4 * i + 2)
                up(b)
                over_units(dve, f"{b}.down", split_lo)
                post(f"{b}.n3", 4 * i + 3)

        @block.gpsimd
        def _(pool):
            def power(name, n=TT, col=0, i=0):
                r, _, _ = CHAINS[name]
                pool.wait_ge(mean_ready, r + i + 1)
                pool.tensor_tensor(inv_rms[:, col:col + n], mean_sq[:, col:col + n],
                                   neg_half[:, 0:1].broadcast_to([P, n]), ALU.pow).then_inc(rstd_ready, 1)

            pool.memset(neg_half[:, :], -0.5).then_inc(half_ready, 1)
            pool.wait_ge(half_ready, 1)
            pool.wait_ge(consts_in, 16 * 4)
            for l in range(DEPTH):
                for who in ("ctx", "x"):
                    power(f"{who}{l}.norm1", col=EARLY[who])
                for who in ("ctx", "x"):
                    w = f"{who}{l}"
                    if w == "ctx1":
                        power(f"{w}.qk", 4)
                        continue
                    power(f"{w}.qk", 20)
                    n = PASSES[w]
                    if w != "ctx0":
                        for i in range(5):
                            pool.wait_ge(qk_norm_ready, 5 * n + i + 1)
                            pool.tensor_tensor(full[:, i, :], qk_n[:, i, :], C("rope_cos", n=TOK), ALU.mult
                                               ).then_inc(rope_part, 1)
                    for m in range(KT):
                        pool.wait_ge(evicted, FIRST[f"{w}.outs"] + m + 1)
                        at_least(pool, h_lo_ready, KT * FILLS[f"{w}.m"] + m - 1)
                        pool.tensor_tensor(sums[:, m % 2, :], terms[:, m % 2, 0, :], terms[:, m % 2, 1, :], ALU.add
                                           ).then_inc(merge_step, 1)
                        pool.wait_ge(merge_step, KT * n + m + 1)
                        pool.tensor_tensor(sums[:, 2 + m % 2, :], sums[:, m % 2, :], terms[:, m % 2, 2, :], ALU.add
                                           ).then_inc(merged, 1)
                    power(f"{w}.norm2")
            for i in range(4):
                b = f"b{i}"
                power(f"{b}.n0")
                if i % 3 == 0:
                    n = RETS[b]
                    pool.wait_ge(sin_ready, 2)
                    pool.wait_ge(sums_ready, CHAINS[f"{b}.n0"][0] + 1)
                    pool.wait_ge(evicted, FIRST[f"{b}.v"])
                    for pair in range(8):
                        at_least(pool, rot_done, 8 * n + pair - 1)
                        for t in range(2):
                            m = pool.tensor_tensor(squares[:, 4 * (pair % 2) + t, :],
                                                   ret_raw[:, (2 * pair + t) * TOK:(2 * pair + t + 1) * TOK],
                                                   C("pos_cos", n=TOK), ALU.mult)
                        m.then_inc(rot_a, 1)
                    for k in range(16):
                        pool.wait_ge(evicted, FIRST[f"{b}.g"] + k + 1)
                        pool.wait_ge(head_copied, 8 * n + 2 * (k // 4) + 2)
                        x = scratch[:, 8 + k, :]
                        pool.tensor_tensor(x, x, ret_o[:, k * TOK:(k + 1) * TOK], ALU.mult).then_inc(gated, 1)
                        if k % 4 == 3:
                            power(f"{b}.heads", col=2 * (k // 4 % 2), i=k // 4)
                elif i % 3 == 1:
                    power(f"{b}.var")
                else:
                    power(f"{b}.heads", 8)
                for part in ("n1", "n2", "n3"):
                    power(f"{b}.{part}")


def _by_feature(v):
    return np.ascontiguousarray(np.asarray(v).reshape(-1, P).T)


def _units(w):
    g, m = w.shape[0] // D, w.shape[1] // P
    return w.reshape(g, KT, P, m, P).transpose(3, 0, 2, 1, 4).reshape(m * g, P, D)


def _head_order(w, axis):
    shape = w.shape[:axis] + (2, 4, HD) + w.shape[axis + 1:]
    return np.swapaxes(w.reshape(shape), axis, axis + 1).reshape(w.shape)


def pack_stream(a):
    parts = []
    for l in range(DEPTH):
        w = a["w_in"][l]
        conv, four, q, kv, gates = w[:, 0:768], w[:, 768:1024], w[:, 1024:1536], w[:, 1536:1792], w[:, 1792:]
        outs = np.concatenate([a["w_conv_out"][l], a["w_four_out"][l], _head_order(a["w_attn_out"][l], 0)])
        parts += [_units(a["w_mod"][l]), _units(kv), _units(_head_order(q, 1)), _units(four), _units(conv),
                  _units(gates), _units(outs), _units(a["w_o"][l]), _units(a["w_ff1"][l]), _units(a["w_ff2"][l])]
    for i in range(4):
        j = i // 3
        if i % 3 == 0:
            parts += [_units(a["ret_w_in_2"][j]), _units(a["ret_w_out_2"][j])]
        elif i % 3 == 1:
            w = a["conv_w_in_2"][j]
            both = w.reshape(D, 2, KT, P).transpose(0, 2, 1, 3).reshape(D, 2 * D)
            parts += [_units(both), _units(a["conv_w_out_2"][j])]
        else:
            gate = np.zeros((D, 2 * P), np.float32)
            for d in range(2):
                gate[:, P * d + 32 * d:P * d + 32 * d + 16] = a["gla_gate_w1_2"][j, d]
            parts += [_units(gate), _units(a["gla_w_in_2"][j]), _units(a["gla_w_out_2"][j])]
        parts += [_units(a["mlp_w_up_2"][i]), _units(a["mlp_w_down_2"][i])]
    return np.concatenate(parts)


def pack_vectors(a):
    out = np.zeros((P, N_VEC), np.float32)

    def put(name, cols):
        out[:, VEC[name]:VEC[name] + cols.shape[1]] = cols
    for l in range(DEPTH):
        put(f"b_mod{l}", _by_feature(a["b_mod"][l]))
        put(f"g1_{l}", _by_feature(a["g_norm1"][l]))
        put(f"g2_{l}", _by_feature(a["g_norm2"][l]))
        put(f"w_conv{l}", _by_feature(a["w_conv"][l].reshape(-1)))
        put(f"g_q{l}", np.tile(a["g_q"][l], 2)[:, None])
        put(f"g_k{l}", np.tile(a["g_k"][l], 2)[:, None])
    both = np.stack([_by_feature(a["c"][0]), _by_feature(a["c_ctx"])], 2)
    put("c", both.reshape(P, 2 * KT))
    put("gains", _by_feature(a["norm_gains_2"].reshape(-1)))
    put("b_in", _by_feature(a["conv_b_in_2"].reshape(-1)))
    put("w_dw", a["conv_w_dw_2"][0].reshape(TAPS, KT, P).transpose(2, 1, 0).reshape(P, TAPS * KT))
    put("b_dw", _by_feature(a["conv_b_dw_2"]))
    put("ln_gain", _by_feature(a["conv_ln_gain_2"]))
    put("ln_bias", _by_feature(a["conv_ln_bias_2"]))
    put("b_out", _by_feature(a["conv_b_out_2"]))
    put("gate_b", _by_feature(a["gla_gate_b_2"].reshape(-1)))
    put("gla_gain", _by_feature(a["gla_norm_gain_2"]))
    put("decay", np.tile(a["ret_decay_logit_2"].reshape(1, 16), (P, 1)))
    put("inv_freq", (np.float32(10000.0) ** (-np.arange(P, dtype=np.float32) / np.float32(P)))[:, None])
    return out


def constants():
    out, out2 = np.zeros((P, N_CON), np.float32), np.zeros((P, N_CON2), np.float32)

    def put(name, cols):
        o, at = (out2, CON2[name]) if name in CON2 else (out, CON[name])
        o[:, at:at + cols.shape[1]] = cols
    p = np.arange(P)
    put("mean", np.full((P, P), 1.0 / D))
    put("ident", np.eye(P))
    rot = np.zeros((P, P))
    first = p[p % HD < HD // 2]
    rot[first + HD // 2, first] = -1.0
    rot[first, first + HD // 2] = 1.0
    put("rot", rot)
    put("head_mean", np.stack([p < HD, p >= HD], 1) / HD)
    put("part_sel", (p[:, None] % 2 == np.arange(2)[None]) & (p[:, None] < 4))
    dim = 2 * np.pi * np.outer(p, p) / 64
    same = p[:, None] // 64 == p[None, :] // 64
    put("dim_dft", np.concatenate([np.cos(dim) * same, np.sin(dim) * same], 1) / 8)
    t = np.arange(TOK)
    tok = 2 * np.pi * np.outer(t, t) / TOK
    by_tile = lambda m: m.reshape(TT, P, TOK).transpose(1, 0, 2).reshape(P, TT * TOK)
    put("tok_cos", by_tile(np.cos(tok) / 16))
    put("tok_sin", by_tile(-np.sin(tok) / 16))
    n_freq = HD // 4
    inv = np.float32(10000.0) ** (-np.arange(n_freq, dtype=np.float32) / np.float32(n_freq))
    row, col = (t // 64).astype(np.float32), (t % 64).astype(np.float32)
    ang = np.concatenate([row[None] * inv[:, None], col[None] * inv[:, None]]).astype(np.float32)
    ang = np.tile(ang, (4, 1)).astype(np.float64)
    put("rope_cos", np.cos(ang))
    put("rope_sin", np.sin(ang))
    s = np.arange(TOK)
    put("after", by_tile(np.maximum(t[None, :] - s[:, None], 0.0)))
    put("before", by_tile(np.maximum(s[:, None] - t[None, :], 0.0)))
    c = np.arange(CHUNK)
    put("mask_fwd", np.tile(c[None, :] >= c[:, None], (2, 1)))
    put("mask_bwd", np.tile(c[None, :] < c[:, None], (2, 1)))
    return {"constants": out, "constants2": out2}


def kernel(**inputs):
    import concourse.bacc as _bacc
    from concourse.bass_utils import run_bass_kernel_spmd as _run

    a = {k: np.asarray(v) for k, v in inputs.items()}
    w2 = np.zeros((48, 512), np.float32)
    for d in range(2):
        w2[32 * d:32 * d + 16] = a["gla_gate_w2_2"][0, d]
    arrays = {
        "stream": pack_stream(a), "xT": np.ascontiguousarray(a["x"][0].T), "ctxT": np.ascontiguousarray(a["ctx"][0].T),
        "vectors": pack_vectors(a), **constants(),
        "positions": np.ascontiguousarray(np.tile(a["positions_2"], (P, 1))), "gate_w2": w2,
    }
    nc = _bacc.Bacc("TRN2", target_bir_lowering=False, num_devices=1)
    args = [nc.dram_tensor(n, v.shape, mybir.dt.from_np(v.dtype), kind="ExternalInput").ap() for n, v in arrays.items()]
    out = nc.dram_tensor("out", (D, TOK), F32, kind="ExternalOutput").ap()
    build(nc, *args, out)
    r = _run(nc, [arrays], core_ids=[0])
    return np.ascontiguousarray(r.results[0]["out"].T)[None]
```
